# Optimizing a Trainium2 kernel written in Bass

```python
import jax, jax.numpy as jnp
from jax import lax
import numpy as np

D_MODEL = 1024
BATCH = 1
SEQ = 256
DEPTH = 2

N_A_LAYERS = DEPTH // 2
N_B_LAYERS = DEPTH - N_A_LAYERS

DN_ALPHA = (2 * DEPTH) ** 0.25
DN_BETA = (8 * DEPTH) ** -0.25
LN_EPS = 1e-5
RMS_EPS = 1e-6
NEG_INF = -1e30
Q_BLOCK = 128

NSA_HEADS = 16
NSA_KV_GROUPS = 4
NSA_GROUP_SIZE = NSA_HEADS // NSA_KV_GROUPS
NSA_HEAD_DIM = D_MODEL // NSA_HEADS
CMP_LEN = 32
CMP_STRIDE = 16
CMP_HIDDEN = 2 * NSA_HEAD_DIM
SEL_BLOCK = 64
SEL_TOPN = 16
FORCE_BONUS = 1e4
WINDOW = 512
NSA_Q_COLS = NSA_HEADS * NSA_HEAD_DIM
NSA_KV_COLS = NSA_KV_GROUPS * NSA_HEAD_DIM
NSA_IN_COLS = NSA_Q_COLS + 6 * NSA_KV_COLS + 3 * NSA_HEADS

MLA_HEADS = 16
MLA_NOPE = 64
MLA_ROPE = 32
MLA_V = 64
MLA_Q_LORA = 768
MLA_KV_LORA = 256
ROPE_THETA = 10000.0

PEER_HEADS = 8
PEER_NKEYS = 128
PEER_EXPERTS = PEER_NKEYS * PEER_NKEYS
PEER_QDIM = 256
PEER_HALF = PEER_QDIM // 2
PEER_TOPK = 16
PEER_CHUNK = 128

kernel_name = "yoco_nsa_mla_peer_deepnorm"

def layer_norm(x, g, b):
    xf = x.astype(jnp.float32)
    mu = xf.mean(-1, keepdims=True)
    var = jnp.square(xf - mu).mean(-1, keepdims=True)
    y = (xf - mu) * lax.rsqrt(var + LN_EPS)
    return (y * g.astype(jnp.float32) + b.astype(jnp.float32)).astype(x.dtype)

def rms_norm(x, g):
    xf = x.astype(jnp.float32)
    y = xf * lax.rsqrt(jnp.square(xf).mean(-1, keepdims=True) + RMS_EPS)
    return (y * g.astype(jnp.float32)).astype(x.dtype)

def masked_softmax(s, mask, axis=-1):
    s = jnp.where(mask, s.astype(jnp.float32), NEG_INF)
    p = jax.nn.softmax(s, axis=axis)
    return jnp.where(mask, p, 0.0)

def alibi_slopes(n):
    return jnp.asarray([2.0 ** (-8.0 * (h + 1) / n) for h in range(n)], jnp.float32)

def rope_cos_sin(seq, dim):
    inv = 1.0 / (ROPE_THETA ** (jnp.arange(0, dim, 2, dtype=jnp.float32) / dim))
    ang = jnp.arange(seq, dtype=jnp.float32)[:, None] * inv[None, :]
    return jnp.cos(ang), jnp.sin(ang)

def apply_rope(x, cos, sin):
    shp = (cos.shape[0],) + (1,) * (x.ndim - 3) + (cos.shape[1],)
    c, s = cos.reshape(shp), sin.reshape(shp)
    xf = x.astype(jnp.float32)
    x1, x2 = jnp.split(xf, 2, axis=-1)
    return jnp.concatenate([x1 * c - x2 * s, x2 * c + x1 * s], axis=-1).astype(x.dtype)

def cmp_to_sel_matrix(n_cmp, n_sel):
    start = np.arange(n_cmp)[:, None] * CMP_STRIDE
    bstart = np.arange(n_sel)[None, :] * SEL_BLOCK
    ov = np.clip(np.minimum(start + CMP_LEN, bstart + SEL_BLOCK) - np.maximum(start, bstart), 0, None)
    return (ov / CMP_LEN).astype(np.float32)

def nsa_compress(k, w1, w2, pe):
    B, S, G, dh = k.shape
    chunks = k.reshape(B, S // CMP_STRIDE, CMP_STRIDE, G, dh)
    w1r = w1.reshape(2, CMP_STRIDE, dh, CMP_HIDDEN)
    p_first = jnp.einsum('bnlgd,ldh->bngh', chunks, w1r[0])
    p_second = jnp.einsum('bnlgd,ldh->bngh', chunks, w1r[1])
    pe_term = jnp.einsum('ld,ldh->h', pe, w1.reshape(CMP_LEN, dh, CMP_HIDDEN))
    h = jax.nn.gelu(p_first[:, :-1] + p_second[:, 1:] + pe_term)
    return jnp.einsum('bngh,hd->bngd', h, w2)

def nsa_mixer(x, w_in, ck_w1, ck_w2, ck_pe, cv_w1, cv_w2, cv_pe, w_out):
    B, S, _ = x.shape
    G, R, dh = NSA_KV_GROUPS, NSA_GROUP_SIZE, NSA_HEAD_DIM
    proj = x @ w_in
    splits = np.cumsum([NSA_Q_COLS] + [NSA_KV_COLS] * 6).tolist()
    q, kc, vc, ks, vs, kw, vw, gates = jnp.split(proj, splits, axis=-1)
    q = q.reshape(B, S, G, R, dh)
    kc, vc, ks, vs, kw, vw = [a.reshape(B, S, G, dh) for a in (kc, vc, ks, vs, kw, vw)]
    gates = jax.nn.sigmoid(gates.astype(jnp.float32)).reshape(B, S, G, R, 3)

    kc_cmp = nsa_compress(kc, ck_w1, ck_w2, ck_pe)
    vc_cmp = nsa_compress(vc, cv_w1, cv_w2, cv_pe)
    n_cmp = S // CMP_STRIDE - 1
    cmp_end = jnp.arange(n_cmp) * CMP_STRIDE + (CMP_LEN - 1)
    n_sel = S // SEL_BLOCK
    top_n = min(SEL_TOPN, n_sel)
    sel_map = jnp.asarray(cmp_to_sel_matrix(n_cmp, n_sel))
    ks_blocks = ks.reshape(B, n_sel, SEL_BLOCK, G, dh).transpose(0, 3, 1, 2, 4)
    vs_blocks = vs.reshape(B, n_sel, SEL_BLOCK, G, dh).transpose(0, 3, 1, 2, 4)
    kw_pad = jnp.pad(kw, ((0, 0), (WINDOW, 0), (0, 0), (0, 0)))
    vw_pad = jnp.pad(vw, ((0, 0), (WINDOW, 0), (0, 0), (0, 0)))
    slopes = alibi_slopes(NSA_HEADS).reshape(G, R)
    scale = dh ** -0.5
    n_qb = S // Q_BLOCK

    def block_fn(i):
        b = i // n_qb
        q0 = (i % n_qb) * Q_BLOCK
        t = q0 + jnp.arange(Q_BLOCK)
        qb = lax.dynamic_slice(q, (b, q0, 0, 0, 0), (1, Q_BLOCK, G, R, dh))[0]
        gb = lax.dynamic_slice(gates, (b, q0, 0, 0, 0), (1, Q_BLOCK, G, R, 3))[0]
        kcb, vcb = kc_cmp[b], vc_cmp[b]
        dist_c = t[:, None] - cmp_end[None, :]
        s_c = jnp.einsum('tgrd,ngd->grtn', qb, kcb).astype(jnp.float32) * scale \
            - slopes[:, :, None, None] * dist_c.astype(jnp.float32)
        p_c = masked_softmax(s_c, dist_c >= 0)
        o_c = jnp.einsum('grtn,ngd->tgrd', p_c.astype(vcb.dtype), vcb)
        imp = jnp.einsum('grtn,nj->gtj', p_c, sel_map)
        blk_t = t // SEL_BLOCK
        j = jnp.arange(n_sel)
        eligible = j[None, :] <= blk_t[:, None]
        forced = (j[None, :] == 0) | (j[None, :] == blk_t[:, None]) | (j[None, :] == blk_t[:, None] - 1)
        imp = jnp.where(eligible, imp + jnp.where(forced, FORCE_BONUS, 0.0), NEG_INF)
        _, sel_idx = lax.top_k(imp, top_n)
        k_g = jax.vmap(lambda kk, ii: kk[ii])(ks_blocks[b], sel_idx)
        v_g = jax.vmap(lambda vv, ii: vv[ii])(vs_blocks[b], sel_idx)
        pos_s = sel_idx[..., None] * SEL_BLOCK + jnp.arange(SEL_BLOCK)
        dist_s = (t[None, :, None, None] - pos_s)[:, None]
        s_s = jnp.einsum('tgrd,gtnld->grtnl', qb, k_g).astype(jnp.float32) * scale \
            - slopes[:, :, None, None, None] * dist_s.astype(jnp.float32)
        p_s = masked_softmax(s_s, dist_s >= 0, axis=(-2, -1))
        o_s = jnp.einsum('grtnl,gtnld->tgrd', p_s.astype(v_g.dtype), v_g)
        kwb = lax.dynamic_slice(kw_pad, (b, q0, 0, 0), (1, WINDOW + Q_BLOCK, G, dh))[0]
        vwb = lax.dynamic_slice(vw_pad, (b, q0, 0, 0), (1, WINDOW + Q_BLOCK, G, dh))[0]
        s_pos = q0 - WINDOW + jnp.arange(WINDOW + Q_BLOCK)
        dist_w = t[:, None] - s_pos[None, :]
        mask_w = (dist_w >= 0) & (dist_w < WINDOW) & (s_pos[None, :] >= 0)
        s_w = jnp.einsum('tgrd,sgd->grts', qb, kwb).astype(jnp.float32) * scale \
            - slopes[:, :, None, None] * dist_w.astype(jnp.float32)
        p_w = masked_softmax(s_w, mask_w)
        o_w = jnp.einsum('grts,sgd->tgrd', p_w.astype(vwb.dtype), vwb)
        o = gb[..., 0:1] * o_c + gb[..., 1:2] * o_s + gb[..., 2:3] * o_w
        return o.reshape(Q_BLOCK, NSA_Q_COLS).astype(q.dtype)

    out = lax.map(block_fn, jnp.arange(B * n_qb)).reshape(B, S, NSA_Q_COLS)
    return out @ w_out

def mla_shared_kv(x, w_dkv, kv_norm_g, w_kr, w_uk, w_uv, cos, sin):
    c_kv = rms_norm(x @ w_dkv, kv_norm_g)
    k_rope = apply_rope(x @ w_kr, cos, sin)
    k_nope = jnp.einsum('bsc,chd->bshd', c_kv, w_uk)
    v = jnp.einsum('bsc,chd->bshd', c_kv, w_uv)
    return k_nope, k_rope, v

def mla_mixer(x, w_dq, q_norm_g, w_uq, w_out, k_nope, k_rope, v, cos, sin):
    B, S, _ = x.shape
    H = MLA_HEADS
    q = jnp.einsum('bsc,chd->bshd', rms_norm(x @ w_dq, q_norm_g), w_uq)
    q_nope = q[..., :MLA_NOPE]
    q_rope = apply_rope(q[..., MLA_NOPE:], cos, sin)
    scale = (MLA_NOPE + MLA_ROPE) ** -0.5
    n_qb = S // Q_BLOCK
    kpos = jnp.arange(S)

    def block_fn(i):
        b = i // n_qb
        q0 = (i % n_qb) * Q_BLOCK
        t = q0 + jnp.arange(Q_BLOCK)
        qn = lax.dynamic_slice(q_nope, (b, q0, 0, 0), (1, Q_BLOCK, H, MLA_NOPE))[0]
        qr = lax.dynamic_slice(q_rope, (b, q0, 0, 0), (1, Q_BLOCK, H, MLA_ROPE))[0]
        s = (jnp.einsum('thd,shd->hts', qn, k_nope[b]) + jnp.einsum('thd,sd->hts', qr, k_rope[b])).astype(jnp.float32) * scale
        p = masked_softmax(s, kpos[None, :] <= t[:, None])
        vb = v[b]
        o = jnp.einsum('hts,shd->thd', p.astype(vb.dtype), vb)
        return o.reshape(Q_BLOCK, H * MLA_V)

    out = lax.map(block_fn, jnp.arange(B * n_qb)).reshape(B, S, H * MLA_V)
    return out @ w_out

def peer_ffn(x, w_q, subkeys, u, v):
    B, S, D = x.shape
    T, K = PEER_CHUNK, PEER_TOPK
    xt = x.reshape(-1, T, D)

    def chunk_fn(xc):
        q = (xc @ w_q).reshape(T, PEER_HEADS, 2, PEER_HALF)
        s = jnp.einsum('thcd,hckd->thck', q, subkeys).astype(jnp.float32)
        sv, si = lax.top_k(s, K)
        cand = sv[:, :, 0, :, None] + sv[:, :, 1, None, :]
        cidx = si[:, :, 0, :, None] * PEER_NKEYS + si[:, :, 1, None, :]
        cs, cp = lax.top_k(cand.reshape(T, PEER_HEADS, K * K), K)
        eidx = jnp.take_along_axis(cidx.reshape(T, PEER_HEADS, K * K), cp, axis=-1)
        g = jax.nn.softmax(cs, axis=-1)
        ue, ve = u[eidx], v[eidx]
        a = jax.nn.gelu(jnp.einsum('td,thkd->thk', xc, ue).astype(jnp.float32))
        return jnp.einsum('thk,thkd->td', (g * a).astype(xc.dtype), ve)

    return lax.map(chunk_fn, xt).reshape(B, S, D)

def setup_inputs(seed: int = 0) -> dict:
    key = jax.random.key(seed)
    ks = iter(jax.random.split(key, 40))
    D = D_MODEL

    def nrm(shape, scale):
        return jax.random.normal(next(ks), shape, jnp.float32) * scale

    def gain(shape):
        return 1.0 + nrm(shape, 0.02)

    na, nb = N_A_LAYERS, N_B_LAYERS
    flat = CMP_LEN * NSA_HEAD_DIM
    return {
        "x": nrm((BATCH, SEQ, D), 1.0),
        "nsa_w_in": nrm((na, D, NSA_IN_COLS), D ** -0.5),
        "nsa_cmp_k_w1": nrm((na, flat, CMP_HIDDEN), flat ** -0.5),
        "nsa_cmp_k_w2": nrm((na, CMP_HIDDEN, NSA_HEAD_DIM), CMP_HIDDEN ** -0.5),
        "nsa_cmp_k_pe": nrm((na, CMP_LEN, NSA_HEAD_DIM), 0.1),
        "nsa_cmp_v_w1": nrm((na, flat, CMP_HIDDEN), flat ** -0.5),
        "nsa_cmp_v_w2": nrm((na, CMP_HIDDEN, NSA_HEAD_DIM), CMP_HIDDEN ** -0.5),
        "nsa_cmp_v_pe": nrm((na, CMP_LEN, NSA_HEAD_DIM), 0.1),
        "nsa_w_out": nrm((na, NSA_Q_COLS, D), DN_BETA * NSA_Q_COLS ** -0.5),
        "nsa_ln_g": gain((na, D)),
        "nsa_ln_b": nrm((na, D), 0.02),
        "mla_w_dkv": nrm((D, MLA_KV_LORA), D ** -0.5),
        "mla_kv_norm_g": gain((MLA_KV_LORA,)),
        "mla_w_kr": nrm((D, MLA_ROPE), D ** -0.5),
        "mla_w_uk": nrm((MLA_KV_LORA, MLA_HEADS, MLA_NOPE), MLA_KV_LORA ** -0.5),
        "mla_w_uv": nrm((MLA_KV_LORA, MLA_HEADS, MLA_V), MLA_KV_LORA ** -0.5),
        "mla_w_dq": nrm((nb, D, MLA_Q_LORA), D ** -0.5),
        "mla_q_norm_g": gain((nb, MLA_Q_LORA)),
        "mla_w_uq": nrm((nb, MLA_Q_LORA, MLA_HEADS, MLA_NOPE + MLA_ROPE), MLA_Q_LORA ** -0.5),
        "mla_w_out": nrm((nb, MLA_HEADS * MLA_V, D), DN_BETA * (MLA_HEADS * MLA_V) ** -0.5),
        "mla_ln_g": gain((nb, D)),
        "mla_ln_b": nrm((nb, D), 0.02),
        "peer_w_q": nrm((DEPTH, D, PEER_HEADS * PEER_QDIM), D ** -0.5),
        "peer_subkeys": nrm((DEPTH, PEER_HEADS, 2, PEER_NKEYS, PEER_HALF), PEER_HALF ** -0.5),
        "peer_u": nrm((DEPTH, PEER_EXPERTS, D), D ** -0.5),
        "peer_v": nrm((DEPTH, PEER_EXPERTS, D), DN_BETA),
        "peer_ln_g": gain((DEPTH, D)),
        "peer_ln_b": nrm((DEPTH, D), 0.02),
    }

def reference(x, nsa_w_in, nsa_cmp_k_w1, nsa_cmp_k_w2, nsa_cmp_k_pe, nsa_cmp_v_w1, nsa_cmp_v_w2,
              nsa_cmp_v_pe, nsa_w_out, nsa_ln_g, nsa_ln_b, mla_w_dkv, mla_kv_norm_g, mla_w_kr,
              mla_w_uk, mla_w_uv, mla_w_dq, mla_q_norm_g, mla_w_uq, mla_w_out, mla_ln_g, mla_ln_b,
              peer_w_q, peer_subkeys, peer_u, peer_v, peer_ln_g, peer_ln_b):
    S = x.shape[1]
    cos, sin = rope_cos_sin(S, MLA_ROPE)
    h = x
    k_nope = k_rope = v_shared = None
    for layer in range(DEPTH):
        if layer < N_A_LAYERS:
            a = layer
            mix = nsa_mixer(h, nsa_w_in[a], nsa_cmp_k_w1[a], nsa_cmp_k_w2[a], nsa_cmp_k_pe[a],
                            nsa_cmp_v_w1[a], nsa_cmp_v_w2[a], nsa_cmp_v_pe[a], nsa_w_out[a])
            h = layer_norm(DN_ALPHA * h + mix, nsa_ln_g[a], nsa_ln_b[a])
        else:
            if layer == N_A_LAYERS:
                k_nope, k_rope, v_shared = mla_shared_kv(h, mla_w_dkv, mla_kv_norm_g, mla_w_kr,
                                                         mla_w_uk, mla_w_uv, cos, sin)
            bi = layer - N_A_LAYERS
            mix = mla_mixer(h, mla_w_dq[bi], mla_q_norm_g[bi], mla_w_uq[bi], mla_w_out[bi],
                            k_nope, k_rope, v_shared, cos, sin)
            h = layer_norm(DN_ALPHA * h + mix, mla_ln_g[bi], mla_ln_b[bi])
        ffn = peer_ffn(h, peer_w_q[layer], peer_subkeys[layer], peer_u[layer], peer_v[layer])
        h = layer_norm(DN_ALPHA * h + ffn, peer_ln_g[layer], peer_ln_b[layer])
    return h


_drawn_inputs = setup_inputs


def setup_inputs(seed=0):
    import zlib

    import numpy as np

    out = dict(_drawn_inputs(seed))
    spreads = {}
    factors = {'nsa_cmp_k_pe': 4.221, 'mla_kv_norm_g': 7.425, 'mla_q_norm_g': 8.0}
    for name, (base, spread) in spreads.items():
        noise = np.random.default_rng([zlib.crc32(name.encode()), seed]).standard_normal(out[name].shape)
        drawn = base * np.exp(spread * noise) if base else spread * noise
        out[name] = __import__('jax').numpy.asarray(drawn.astype(out[name].dtype))
    for name, factor in factors.items():
        out[name] = (out[name] * factor).astype(out[name].dtype)
    return out
```

```python
import concourse.bass as bass
import numpy as np
from concourse import mybir
from concourse.alu_op_type import AluOpType as ALU
from contextlib import ExitStack

F32 = mybir.dt.float32
U32 = mybir.dt.uint32
ACT = mybir.ActivationFunctionType
AX = mybir.AxisListType

P = 128
D = 1024
KD = D // P
SEQ = 256
TILES = SEQ // P
HEADS = 16
HD = 64
GROUPS = 4
CMP_STRIDE = 16
CMP_LEN = 32
NCMP = SEQ // CMP_STRIDE
NSA_SCALE = HD ** -0.5
ROPE = 32
HALF = ROPE // 2
QK = HD + ROPE
KV_LORA = 256
Q_LORA = 768
MLA_SCALE = QK ** -0.5
PH = 8
TOPK = 16
NKEYS = 128
EXPERTS = NKEYS * NKEYS
ALPHA = 4.0 ** 0.25
LN_EPS = 1e-5
RMS_EPS = 1e-6
MASKED = -1.0e30
LOWEST = -3.0e38

RUN = [TOPK // (i + 1) for i in range(TOPK)]
RUN_AT = [sum(RUN[:i]) for i in range(TOPK)]
NCAND = sum(RUN)

SLOTS = 8
WSLOTS = 3
WCOLS = 4096

NSA_CHUNKS = [("kvc", 4096), ("ck1", 2048), ("cv1", 2048), ("ksw", 4096), ("q0", 4096), ("q1", 4096),
              ("vsw", 4096), ("gate", KD * 48), ("wo0", 4096), ("wo1", 4096)]
PEER_W = KD * 256 + 2 * NKEYS
PEER_CHUNKS = [(f"pq{c}", PEER_W) for c in range(PH)]
MLA_CHUNKS = [("dkv", KD * (KV_LORA + ROPE)), ("uk", 2048), ("uv", 2048), ("dq0", KD * 384), ("dq1", KD * 384),
              ("uq0", 3072), ("uq1", 3072), ("uq2", 3072), ("mo0", 4096), ("mo1", 4096)]
LAYERS = [NSA_CHUNKS + PEER_CHUNKS, MLA_CHUNKS + PEER_CHUNKS]


def chunk_plan():
    at, off = {}, 0
    for l, chunks in enumerate(LAYERS):
        for name, width in chunks:
            at[l, name] = (off, width)
            off += width * P
    order = [at[0, n] for n, _ in LAYERS[0]]
    for _ in range(TILES):
        order += [at[1, n] for n, _ in LAYERS[1]]
    return order, off


CONST = {}
_at = 0
for _name, _w in [("ident", P), ("cmp_bias", TILES * HEADS * NCMP), ("cmp_mask", TILES * NCMP), ("causal", 2 * P),
                  ("rope", TILES * 2 * HALF), ("number", NCAND), ("pe", 2 * 16), ("w2k", HD), ("w2v", HD),
                  ("q_gain", 6), ("kv_gain", 2)]:
    CONST[_name] = (_at, _w)
    _at += _w
NCONST = _at


class Banks:

    def __init__(self):
        self.n = 0

    def take(self):
        n = self.n
        self.n += 1
        return n % 3, n // 3

    def skip(self, k):
        self.n += k


def spread(ap, axis, n):
    ap = ap.unsqueeze(axis)
    shape = list(ap.shape)
    shape[axis] = n
    return ap.broadcast_to(shape)


def trunk_kernel(nc, x, xT, weights, consts, alibi, ln_params, experts0, experts1, out):
    ctx = ExitStack()
    with ctx:
        def sb(name, shape, dt=F32):
            return ctx.enter_context(nc.sbuf_tensor("t_" + name, shape, dt))

        def pb(name, shape):
            return ctx.enter_context(nc.psum_tensor("p_" + name, shape, F32))

        def sem(name):
            return ctx.enter_context(nc.semaphore(name))

        ring = sb("ring", [P, SLOTS, 2 * D])
        wring = sb("wring", [P, WSLOTS, WCOLS])
        h = sb("h", [P, TILES, D])
        hT = sb("hT", [P, KD, SEQ])
        keyscore = sb("keyscore", [P, TILES, 2 * PH, NKEYS])
        lnp = sb("lnp", [P, 2, D])
        cst = sb("cst", [P, NCONST])
        zeros = sb("zeros", [P, P])
        kT = sb("kT", [QK, HEADS, SEQ])
        vM = sb("vM", [P, TILES, D])
        S = sb("S", [P, 2, 2, 2 * P])
        shared = sb("shared", [P, 3072])
        ropeT = sb("ropeT", [P, QK])
        small = sb("small", [P, 256])
        gates = sb("gates", [P, TILES, 3, HEADS])
        coef = sb("coef", [P, 3, HEADS])
        diag = sb("diag", [P, 2, P])
        work = sb("work", [P, 2, NKEYS])
        onehot = sb("onehot", [P, TOPK, NCAND])
        top_val = sb("top_val", [P, 2, TOPK])
        top_pos = sb("top_pos", [P, 2, TOPK], U32)
        top_idx = sb("top_idx", [P, 2, TOPK])
        cand = sb("cand", [P, 2, NCAND])
        cand_idx = sb("cand_idx", [P, NCAND])
        best = sb("best", [P, TOPK])
        best_pos = sb("best_pos", [P, TOPK], U32)
        best_posf = sb("best_posf", [P, TOPK])
        best_idx = sb("best_idx", [P, TOPK])
        expert_id = sb("expert_id", [P, 2, TOPK], U32)
        gate_in = sb("gate_in", [P, 2, TOPK])
        gate_e = sb("gate_e", [P, 2, TOPK])
        gate_sum = sb("gate_sum", [P, 2])
        gate_w = sb("gate_w", [P, 2, TOPK])
        dots = sb("dots", [P, SLOTS])
        gelu = sb("gelu", [P, SLOTS])

        acc = pb("acc", [P, D])
        xdup = pb("xdup", [P, D])
        bank = [pb(f"bank{i}", [P, 512]) for i in range(3)]
        heads_out = pb("heads_out", [P, 512])

        flat = ring[:].rearrange("p s c -> p (s c)")
        cut = [0]

        def early(n):
            cut[0] += n
            return flat[:, cut[0] - n:cut[0]]

        bias = early(HEADS * 2 * P).rearrange("p (h s) -> p h s", h=HEADS)
        qT = early(8 * SEQ).rearrange("p (j t) -> p j t", j=8)
        kswT = early(4 * SEQ).rearrange("p (b a t) -> p b a t", b=2, a=2)
        kc2 = early(8 * P).rearrange("p (v g u) -> p v g u", v=2, g=GROUPS)
        vsw = early(TILES * 512).rearrange("p (t c) -> p t c", t=TILES)
        kcT = early(2 * NCMP).rearrange("p (a n) -> p a n", a=2)
        vblk = early(GROUPS * 4 * HD).rearrange("p (g j d) -> p g j d", g=GROUPS, j=4)
        hk = early(GROUPS * NCMP).rearrange("p (g n) -> p g n", g=GROUPS)
        hv = early(GROUPS * 4 * 32).rearrange("p (g j n) -> p g j n", g=GROUPS, j=4)
        pc = early(HEADS * 32).rearrange("p (h n) -> p h n", h=HEADS)
        pcT = early(GROUPS * P).rearrange("p (g t) -> p g t", g=GROUPS)
        sc_raw = early(HEADS * NCMP).rearrange("p (h n) -> p h n", h=HEADS)
        sc_exp = early(HEADS * NCMP).rearrange("p (h n) -> p h n", h=HEADS)
        pe_bias = early(2)
        assert cut[0] <= SLOTS * 2 * D

        def view(name, ap=cst):
            a, w = CONST[name]
            return cst[:, a:a + w]

        ident = view("ident")
        cmp_bias = view("cmp_bias").rearrange("p (t h n) -> p t h n", t=TILES, h=HEADS)
        cmp_mask = view("cmp_mask").rearrange("p (t n) -> p t n", t=TILES)
        causal = view("causal")
        rope = view("rope").rearrange("p (t c k) -> p t c k", t=TILES, c=2)
        number = view("number")
        pe_cols = view("pe").rearrange("p (v l) -> p v l", v=2)
        w2k, w2v, q_gain, kv_gain = view("w2k"), view("w2v"), view("q_gain"), view("kv_gain")

        cq = shared[:, 0:Q_LORA]
        cqT = shared[:, Q_LORA:2 * Q_LORA].rearrange("p (k t) -> p k t", k=6)
        q_nat = shared[:, 2 * Q_LORA:2 * Q_LORA + HEADS * QK]
        mixed = shared[:, 0:D]
        probs = shared[:, D:2 * D].rearrange("p (s r k) -> p s r k", s=2, r=2)
        probsT = shared[:, 2 * D:3 * D].rearrange("p (s b t) -> p s b t", s=2, b=4)
        mixedT = S[:].rearrange("p a b c -> p (a b c)").rearrange("p (k t) -> p k t", k=KD)
        pqT = shared[:, 0:D].rearrange("p (s i t) -> p s i t", s=2, i=2)
        ckv = cq[:, 0:KV_LORA + ROPE]
        ckvT = cqT[:, 0:2, :]
        rope_tmp = S[:].rearrange("p a b c -> p (a b c)")

        def mlaqT(t):
            return keyscore[0:QK, t, :, :]

        stat = small[:, 0:12].rearrange("p (a b) -> p a b", a=2)
        moments = small[:, 12:14]
        std = small[:, 14:15]
        rstd = small[:, 15:16]
        row_max = small[:, 16:20]
        neg_max = small[:, 20:24]
        rms_in = small[:, 24:25]
        rms_std = small[:, 25:26]
        rms_r = small[:, 26:27]
        cmp_max = small[:, 32:48]
        row_sum = small[:, 48:96].rearrange("p (b h) -> p b h", b=3)
        inv_sum = small[:, 96:112]
        kr_tmp = small[:, 112:176].rearrange("p (a k) -> p a k", a=4)
        denom = small[:, 176:224].rearrange("p (b h) -> p b h", b=3)

        x_loaded = sem("x_loaded")
        xT_loaded = sem("xT_loaded")
        const_loaded = sem("const_loaded")
        alibi_loaded = sem("alibi_loaded")
        ln_loaded = sem("ln_loaded")
        w_loaded = [sem(f"w_loaded{i}") for i in range(WSLOTS)]
        zeroed = sem("zeroed")
        bank_filled = [sem(f"bank_filled{i}") for i in range(3)]
        bank_drained = [sem(f"bank_drained{i}") for i in range(3)]
        heads_filled = sem("heads_filled")
        heads_drained = sem("heads_drained")
        scores_ready = sem("scores_ready")
        probs_ready = sem("probs_ready")
        cmp_ready = sem("cmp_ready")
        cmp_exp = sem("cmp_exp")
        cmp_probs = sem("cmp_probs")
        gate_exp = sem("gate_exp")
        pe_done = sem("pe_done")
        mixed_ready = sem("mixed_ready")
        var_ready = sem("var_ready")
        std_ready = sem("std_ready")
        ln_done = sem("ln_done")
        rms_ready = sem("rms_ready")
        rms_std_ready = sem("rms_std_ready")
        latent_ready = sem("latent_ready")
        q_rotated = sem("q_rotated")
        dve_chain = sem("dve_chain")
        act_chain = sem("act_chain")
        gate_in_ready = sem("gate_in_ready")
        gate_e_ready = sem("gate_e_ready")
        ids_ready = sem("ids_ready")
        gathers_issued = sem("gathers_issued")
        gathered = [sem(f"gathered{i}") for i in range(SLOTS)]
        slot_free = sem("slot_free")
        dot_ready = sem("dot_ready")
        gelu_ready = sem("gelu_ready")
        diag_ready = sem("diag_ready")
        acc_read = sem("acc_read")
        out_stored = sem("out_stored")

        plan, _ = chunk_plan()
        chunk_end = []
        ITEMS = 2 * TILES * PH
        LN_LOAD = [0, 0, 1, 2, 3, 4, 5, 5]
        LN_ROW = [0, 2, 1, 2, 1, 3]
        NSA_UNITS = 2 * HEADS // 2
        MLA_UNITS = HEADS // 2

        def unit0(stage, t):
            return t * NSA_UNITS if stage == "nsa" else TILES * NSA_UNITS + t * MLA_UNITS

        def peer_ln(phase):
            return [3, 5, 7, 8][phase]

        def mla_ln(t):
            return [4, 6][t]

        block = ctx.enter_context(nc.Block())

        @block.gpsimd
        def _(pool):
            for ap in (zeros[:], ropeT[:], kcT, vblk, hk, hv):
                nc.gpsimd.memset(ap, 0.0)
            nc.gpsimd.memset(pc, 0.0).then_inc(zeroed, 1)
            for layer, table in enumerate((experts0, experts1)):
                with pool.Fori(0, TILES * PH // 2, 1) as i:
                    for half in range(2):
                        item = 2 * i + (layer * TILES * PH + half)
                        for s in range(TOPK):
                            if s == 0:
                                pool.wait_ge(ids_ready, item + 1)
                            pool.wait_ge(slot_free, item * TOPK + (s + 1))
                            pool.sem_inc(gathers_issued, 1)
                            nc.gpsimd.indirect_dma_start(
                                out=ring[:, s % SLOTS, :], out_offset=None, in_=table,
                                in_offset=bass.IndirectOffsetOnAxis(ap=expert_id[:, half, s:s + 1], axis=0),
                            ).then_inc(gathered[s % SLOTS], 16)

        @block.tensor
        def _(pe):
            banks = Banks()
            chunks = [0]

            def chunk():
                n = chunks[0]
                chunks[0] += 1
                pe.wait_ge(w_loaded[n % WSLOTS], 16 * (n // WSLOTS + 1))
                return wring[:, n % WSLOTS, :]

            def release(n=1):
                chunk_end.extend([((banks.n - 1) % 3, (banks.n - 1) // 3)] * n)

            def fill():
                b, use = banks.take()
                if use:
                    pe.wait_ge(bank_drained[b], use)
                return b, use

            def drained(b, use):
                pe.wait_ge(bank_drained[b], use + 1)

            def transposed_projection(w, cols, src, b, at, k_tiles, tokens):
                for k in range(k_tiles):
                    last = nc.tensor.matmul(bank[b][:, at:at + tokens.stop - tokens.start], w[:, k, cols],
                                            src[:, k, tokens], start=k == 0, stop=k == k_tiles - 1)
                return last

            def tile_transposes(src, n, width=P):
                uses = []
                for k in range(n):
                    if k % 4 == 0:
                        b, use = fill()
                        uses.append((b, use))
                    last = nc.tensor.transpose(bank[b][:, (k % 4) * P:(k % 4 + 1) * P], src[:, k * P:(k + 1) * P], ident)
                    if k % 4 == 3 or k == n - 1:
                        last.then_inc(bank_filled[b], 1)
                return uses

            def natural(src, tokens, w, cols, k_tiles, n):
                b, use = fill()
                for k in range(k_tiles):
                    last = nc.tensor.matmul(bank[b][:, 0:n], src[:, k, tokens], w[:, k, cols], start=k == 0, stop=k == k_tiles - 1)
                last.then_inc(bank_filled[b], 1)
                return b, use

            def attention(first, units, key_blocks, q_of, k_of, v_of):
                lo = 2 * P - key_blocks * P
                T_use = {}

                def scores(u):
                    b, _ = fill()
                    for r in range(2):
                        last = nc.tensor.matmul(bank[b][:, r * 2 * P + lo:(r + 1) * 2 * P], q_of(u, r), k_of(u, r),
                                                start=True, stop=True)
                    last.then_inc(bank_filled[b], 1)

                def transposes(u):
                    b, use = fill()
                    T_use[u] = (b, use)
                    pe.wait_ge(probs_ready, first + u + 1)
                    for r in range(2):
                        for kb in range(key_blocks):
                            c = r * key_blocks + kb
                            last = nc.tensor.transpose(bank[b][:, c * P:(c + 1) * P],
                                                       probs[:, (first + u) % 2, r, lo + kb * P:lo + (kb + 1) * P], ident)
                    last.then_inc(bank_filled[b], 1)

                def values(u):
                    if u % 4 == 0 and (first + u) // 4:
                        pe.wait_ge(heads_drained, (first + u) // 4)
                    drained(*T_use[u])
                    for r in range(2):
                        at = (2 * u + r) % 8 * HD
                        for kb in range(key_blocks):
                            last = nc.tensor.matmul(heads_out[:, at:at + HD], probsT[:, (first + u) % 2, r * key_blocks + kb, :],
                                                    v_of(u, r, kb), start=kb == 0, stop=kb == key_blocks - 1)
                    if u % 4 == 3:
                        last.then_inc(heads_filled, 1)

                scores(units[0])
                for u in units:
                    if u != units[-1]:
                        scores(u + 1)
                    transposes(u)
                    if u != units[0]:
                        values(u - 1)
                values(units[-1])

            def out_projection(n, t):
                pe.wait_ge(mixed_ready, n)
                for use in tile_transposes(mixed, KD):
                    pass
                return use

            def transpose_h(t, count):
                pe.wait_ge(ln_done, count)
                return tile_transposes(h[:, t, :], KD)

            def peer_scores(tiles, uses):
                lo, hi = tiles[0] * P, (tiles[-1] + 1) * P
                n = hi - lo
                for use in uses:
                    drained(*use)
                Q_use, W = {}, {}

                def query(c):
                    w = chunk()
                    W[c] = w
                    wq = w[:, 0:KD * 256].rearrange("p (k n) -> p k n", k=KD)
                    b, use = fill()
                    Q_use[c] = (b, use)
                    for i in range(2):
                        last = transposed_projection(wq, slice(i * P, (i + 1) * P), hT, b, i * n, KD, slice(lo, hi))
                    last.then_inc(bank_filled[b], 1)

                def score(c):
                    b, _ = fill()
                    drained(*Q_use[c])
                    for i in range(2):
                        for j in range(len(tiles)):
                            at = (i * len(tiles) + j) * NKEYS
                            last = nc.tensor.matmul(bank[b][:, at:at + NKEYS], pqT[:, c % 2, i, j * P:(j + 1) * P],
                                                    W[c][:, KD * 256 + i * NKEYS:KD * 256 + (i + 1) * NKEYS], start=True, stop=True)
                    last.then_inc(bank_filled[b], 1)
                    release()

                return query, score

            def peer_slices(tiles, uses, part):
                query, score = peer_scores(tiles, uses)
                query(part[0])
                for c in part:
                    if c != part[-1]:
                        query(c + 1)
                    score(c)

            both = slice(0, SEQ)
            pe.wait_ge(xT_loaded, 16)
            pe.wait_ge(const_loaded, 16)
            w = chunk().rearrange("p (k n) -> p k n", k=KD)
            kvc_use = []
            for v in range(2):
                b, use = fill()
                kvc_use.append((b, use))
                for i in range(2):
                    last = transposed_projection(w, slice((2 * v + i) * P, (2 * v + i + 1) * P), hT, b, i * SEQ, KD, both)
                last.then_inc(bank_filled[b], 1)
            release()
            hidden = []
            for v in range(2):
                w = chunk()[:, 0:2048].rearrange("p (l n) -> p l n", l=16)
                b, use = fill()
                hidden.append((b, use))
                for l in range(16):
                    nc.tensor.matmul(bank[b][:, 64:65], w[:, l, :], pe_cols[:, v, l:l + 1], start=l == 0, stop=l == 15)
                drained(*kvc_use[v])
                rows = kc2[:, v, :, :].rearrange("p g (n l) -> p g n l", l=8)
                for l in range(16):
                    last = nc.tensor.matmul(bank[b][:, 0:GROUPS * (NCMP - 1)], w[:, l, :],
                                            rows[:, :, l // 8:l // 8 + NCMP - 1, l % 8], start=l == 0, stop=l == 15)
                last.then_inc(bank_filled[b], 1)
                release()
            w = chunk().rearrange("p (k n) -> p k n", k=KD)
            for n in range(2):
                b, _ = fill()
                for i in range(2):
                    last = transposed_projection(w, slice((2 * n + i) * P, (2 * n + i + 1) * P), hT, b, i * SEQ, KD, both)
                last.then_inc(bank_filled[b], 1)
            release()
            b, use = fill()
            drained(*hidden[0])
            for par in range(2):
                last = nc.tensor.matmul(bank[b][par * HD:(par + 1) * HD, 0:2 * NCMP], w2k,
                                        hk.rearrange("p (a e) n -> p e a n", e=2)[:, par, :, :], start=True, stop=True)
            last.then_inc(bank_filled[b], 1)
            b, use = fill()
            drained(*hidden[1])
            for g in range(GROUPS):
                last = nc.tensor.matmul(bank[b][:, g * HD:(g + 1) * HD], hv[:, g, :, :].rearrange("p j n -> p (j n)"), w2v,
                                        start=True, stop=True)
            last.then_inc(bank_filled[b], 1)
            for _ in range(2):
                w = chunk().rearrange("p (k n) -> p k n", k=KD)
                for n in range(2):
                    b, use = fill()
                    for i in range(2):
                        last = transposed_projection(w, slice((2 * n + i) * P, (2 * n + i + 1) * P), hT, b, i * SEQ, KD, both)
                    last.then_inc(bank_filled[b], 1)
                release()
            w = chunk().rearrange("p (k n) -> p k n", k=KD)
            for t in range(TILES):
                natural(hT, slice(t * P, (t + 1) * P), w, slice(0, 512), KD, 512)
            release()
            w = chunk()[:, 0:KD * 48].rearrange("p (k n) -> p k n", k=KD)
            for t in range(TILES):
                last_use = natural(hT, slice(t * P, (t + 1) * P), w, slice(0, 48), KD, 48)
            release()
            for back in range(3):
                n = banks.n - 1 - back
                pe.wait_ge(bank_drained[n % 3], n // 3 + 1)

            wo = []
            uses = []
            for t in range(TILES):
                tok = slice(t * P, (t + 1) * P)

                def head(hh):
                    g, r = hh // 4, hh % 4
                    return (g % 2) * HD, g // 2, r

                for e in range(2):
                    b, use = fill()
                    for j in range(8):
                        p0 = e * HD
                        last = nc.tensor.matmul(bank[b][:, j * NCMP:(j + 1) * NCMP], qT[p0:p0 + HD, j, tok],
                                                kcT[p0:p0 + HD, j // 4, :], start=True, stop=True)
                    last.then_inc(bank_filled[b], 1)
                b, use = fill()
                pe.wait_ge(cmp_probs, t + 1)
                for g in range(GROUPS):
                    last = nc.tensor.transpose(bank[b][:, g * P:(g + 1) * P],
                                               pc[:, 4 * g:4 * g + 4, :].rearrange("p h n -> p (h n)"), ident)
                last.then_inc(bank_filled[b], 1)
                T_use = (b, use)
                for half in range(2):
                    b, use = fill()
                    if half == 0:
                        drained(*T_use)
                    for i in range(2):
                        g = 2 * half + i
                        last = nc.tensor.matmul(bank[b][:, i * 256:(i + 1) * 256], pcT[:, g, :],
                                                vblk[:, g, :, :].rearrange("p j d -> p (j d)"), start=True, stop=True)
                    last.then_inc(bank_filled[b], 1)

                def q_of(u, r):
                    p0, a, rr = head(2 * (u % 8) + r)
                    return qT[p0:p0 + HD, a * 4 + rr, tok]

                def k_of(u, r):
                    p0, a, _ = head(2 * (u % 8) + r)
                    return kswT[p0:p0 + HD, u // 8, a, 0:(t + 1) * P]

                def v_of(u, r, kb):
                    c = (u // 8) * 256 + (2 * (u % 8) + r) // 4 * HD
                    return vsw[:, kb, c:c + HD]

                attention(unit0("nsa", t), list(range(NSA_UNITS)), t + 1, q_of, k_of, v_of)
                pe.wait_ge(mixed_ready, t + 1)
                uses = tile_transposes(mixed, KD)
                if t == 0:
                    wo = [chunk().rearrange("p (k n) -> p k n", k=KD) for _ in range(2)]
                for use in uses:
                    drained(*use)
                for half in range(2):
                    natural(mixedT, slice(0, P), wo[half], slice(0, 512), KD, 512)
                if t == TILES - 1:
                    release(2)
            uses = []
            for t in range(TILES):
                uses += transpose_h(t, t + 1)
            peer_slices(range(TILES), uses, list(range(PH)))

            def mla_slices(t):
                tok = slice(t * P, (t + 1) * P)
                s0 = slice(0, P)

                def latent_keys():
                    for use in transpose_h(t, peer_ln(t)):
                        drained(*use)
                    w = chunk()[:, 0:KD * (KV_LORA + ROPE)].rearrange("p (k n) -> p k n", k=KD)
                    natural(hT, tok, w, slice(0, KV_LORA + ROPE), KD, KV_LORA + ROPE)
                    release()
                    b, use = fill()
                    pe.wait_ge(latent_ready, 2 * t + 1)
                    for k in range(2):
                        nc.tensor.transpose(bank[b][:, k * P:(k + 1) * P], ckv[:, k * P:(k + 1) * P], ident)
                    nc.tensor.transpose(bank[b][0:QK, 2 * P:3 * P], ropeT[:], ident).then_inc(bank_filled[b], 1)
                    drained(b, use)

                def keys_values():
                    w = chunk()[:, 0:2048].rearrange("p (k n) -> p k n", k=2)
                    for n in range(2):
                        b, _ = fill()
                        for i in range(4):
                            last = transposed_projection(w, slice((4 * n + i) * P, (4 * n + i + 1) * P), ckvT, b, i * P, 2, s0)
                        last.then_inc(bank_filled[b], 1)
                    release()
                    w = chunk()[:, 0:2048].rearrange("p (k n) -> p k n", k=2)
                    for n in range(2):
                        natural(ckvT, s0, w, slice(n * 512, (n + 1) * 512), 2, 512)
                    release()
                    for n in range(2):
                        w = chunk()[:, 0:KD * 384].rearrange("p (k n) -> p k n", k=KD)
                        natural(hT, tok, w, slice(0, 384), KD, 384)
                        release()
                    pe.wait_ge(latent_ready, 2 * t + 2)
                    for use in tile_transposes(cq, 6):
                        drained(*use)

                def queries():
                    for n in range(3):
                        w = chunk()[:, 0:3072].rearrange("p (k n) -> p k n", k=6)
                        natural(cqT, s0, w, slice(0, 512), 6, 512)
                        release()

                def q_of(u, r):
                    return mlaqT(t)[:, 2 * u + r, :]

                def k_of(u, r):
                    return kT[:, 2 * u + r, 0:(t + 1) * P]

                def v_of(u, r, kb):
                    return vM[:, kb, (2 * u + r) * HD:(2 * u + r + 1) * HD]

                def attention_a():
                    pe.wait_ge(q_rotated, t + 1)
                    for n in range(4):
                        b, use = fill()
                        for i in range(4):
                            hh = 4 * n + i
                            last = nc.tensor.transpose(bank[b][0:QK, i * P:(i + 1) * P], q_nat[:, hh * QK:(hh + 1) * QK], ident)
                        last.then_inc(bank_filled[b], 1)
                    drained(b, use)
                    attention(unit0("mla", t), list(range(4)), t + 1, q_of, k_of, v_of)

                def attention_b():
                    attention(unit0("mla", t), list(range(4, 8)), t + 1, q_of, k_of, v_of)
                    pe.wait_ge(mixed_ready, TILES + t + 1)
                    for use in tile_transposes(mixed, KD):
                        drained(*use)

                def output():
                    for half in range(2):
                        w = chunk().rearrange("p (k n) -> p k n", k=KD)
                        natural(mixedT, s0, w, slice(0, 512), KD, 512)
                        release()
                    for use in transpose_h(t, mla_ln(t)):
                        drained(*use)

                def peer_a():
                    peer_slices([t], [], list(range(4)))

                def peer_b():
                    peer_slices([t], [], list(range(4, 8)))

                return [latent_keys, keys_values, queries, attention_a, attention_b, output, peer_a, peer_b]

            pe.sem_inc(slot_free, SLOTS)
            for phase in range(2 * TILES):
                if phase:
                    pe.wait_ge(acc_read, phase)
                for half in range(2):
                    nc.tensor.matmul(acc[:, half * 512:(half + 1) * 512], zeros[:], spread(ident, 1, 4),
                                     start=True, stop=False, skip_group_check=True)
                slices = mla_slices(phase - 1) if phase in (1, 2) else None
                for head in range(PH):
                    if slices:
                        slices[head]()
                    step0 = (phase * PH + head) * TOPK
                    with pe.Fori(0, TOPK // SLOTS, 1) as i:
                        for k in range(SLOTS):
                            pe.wait_ge(diag_ready, i * SLOTS + (step0 + k + 1))
                            for half in range(2):
                                last = nc.tensor.matmul(acc[:, half * 512:(half + 1) * 512], diag[:, k % 2, :],
                                                        ring[:, k, D + half * 512:D + (half + 1) * 512],
                                                        start=False, stop=False, skip_group_check=True)
                            last.then_inc(slot_free, 1)

        @block.sync
        def _(sp):
            sp.dma_start(hT[:], xT).then_inc(xT_loaded, 16)
            for n, (off, width) in enumerate(plan):
                if n >= WSLOTS:
                    b, use = chunk_end[n - WSLOTS]
                    sp.wait_ge(bank_filled[b], use + 1)
                src = weights[off:off + P * width].rearrange("(p w) -> p w", p=P)
                sp.dma_start(wring[:, n % WSLOTS, 0:width], src).then_inc(w_loaded[n % WSLOTS], 16)
            for t in range(TILES):
                sp.wait_ge(ln_done, peer_ln(2 + t))
                sp.dma_start(out[t * P:(t + 1) * P, :], h[:, t, :]).then_inc(out_stored, 16)
            sp.wait_ge(out_stored, 16 * TILES)

        @block.scalar
        def _(act):
            banks = Banks()

            def full():
                b, use = banks.take()
                act.wait_ge(bank_filled[b], use + 1)
                return b

            def drain(dst, n=512):
                b = full()
                nc.scalar.activation(dst, bank[b][:, 0:n], ACT.Copy).then_inc(bank_drained[b], 1)

            def load_ln(n):
                row = LN_ROW[n]
                act.dma_start(lnp[:].rearrange("p a d -> p (a d)"),
                              ln_params[row, :].partition_broadcast(P)).then_inc(ln_loaded, 16)

            def layer_norm_root(e):
                act.wait_ge(var_ready, e + 1)
                nc.scalar.activation(std, rstd, ACT.Sqrt).then_inc(std_ready, 1)
                if e + 1 < len(LN_LOAD) and LN_LOAD[e + 1] != LN_LOAD[e]:
                    act.wait_ge(ln_done, e + 1)
                    load_ln(LN_LOAD[e + 1])

            def rms_root(n):
                act.wait_ge(rms_ready, n)
                nc.scalar.activation(rms_std, rms_in, ACT.Sqrt).then_inc(rms_std_ready, 1)

            def drain_hT(t):
                for n in range(2):
                    b = full()
                    nc.scalar.activation(hT[:, 4 * n:4 * n + 4, t * P:(t + 1) * P],
                                         bank[b][:].rearrange("p (k t) -> p k t", k=4), ACT.Copy).then_inc(bank_drained[b], 1)

            def drain_mixedT():
                for n in range(2):
                    drain(mixedT[:, 4 * n:4 * n + 4, :].rearrange("p k t -> p (k t)"))

            def attention(first, units, key_blocks, scale, branch_of):
                lo = 2 * P - key_blocks * P
                banks.skip(2 * len(units))
                for u in units:
                    n = first + u
                    act.wait_ge(scores_ready, n + 1)
                    for r in range(2):
                        br, hh = branch_of(u, r)
                        last = nc.scalar.activation(probs[:, n % 2, r, lo:2 * P], S[:, n % 2, r, lo:2 * P], ACT.Exp,
                                                    bias=neg_max[:, n % 2 * 2 + r:n % 2 * 2 + r + 1], scale=scale,
                                                    accum_out=row_sum[:, br, hh:hh + 1])
                    last.then_inc(probs_ready, 1)

            def peer_drains(tiles, part):
                n = len(tiles) * P

                def query(c):
                    b = full()
                    nc.scalar.activation(pqT[:, c % 2, :, 0:n], bank[b][:, 0:2 * n].rearrange("p (i t) -> p i t", i=2),
                                         ACT.Copy).then_inc(bank_drained[b], 1)

                def score(c):
                    b = full()
                    src = bank[b][:, 0:2 * n].rearrange("p (i j k) -> p j i k", i=2, j=len(tiles))
                    for j, t in enumerate(tiles):
                        last = nc.scalar.activation(keyscore[:, t, 2 * c:2 * c + 2, :], src[:, j, :, :], ACT.Copy)
                    last.then_inc(bank_drained[b], 1)

                query(part[0])
                for c in part:
                    if c != part[-1]:
                        query(c + 1)
                    score(c)

            act.dma_start(cst[:], consts).then_inc(const_loaded, 16)
            act.dma_start(h[:], x.rearrange("(t p) d -> p t d", p=P)).then_inc(x_loaded, 16)
            act.dma_start(bias, alibi).then_inc(alibi_loaded, 16)
            load_ln(0)

            for v in range(2):
                b = full()
                src = bank[b][:].rearrange("p (a u par) -> p a u par", a=2, par=2)
                dst = kc2[:, v, :, :].rearrange("p (a e) u -> p e a u", e=2)
                for e in range(2):
                    for par in range(2):
                        last = nc.scalar.activation(dst[par * HD:(par + 1) * HD, e, :, :],
                                                    src[e * HD:(e + 1) * HD, :, :, par], ACT.Copy)
                        if e + par == 2:
                            last.then_inc(bank_drained[b], 1)
            act.wait_ge(zeroed, 1)
            for v in range(2):
                b = full()
                nc.scalar.activation(pe_bias[:, v:v + 1], bank[b][:, 64:65], ACT.Copy).then_inc(pe_done, 1)
                act.wait_ge(pe_done, v + 1)
                src = bank[b][:, 0:GROUPS * (NCMP - 1)].rearrange("p (g n) -> p g n", g=GROUPS)
                for j in range(1 if v == 0 else 4):
                    dst = hk[:, :, 0:NCMP - 1] if v == 0 else hv[:, :, j, 0:NCMP - 1]
                    last = nc.scalar.activation(dst, src, ACT.Gelu_apprx_tanh, bias=pe_bias[:, v:v + 1])
                last.then_inc(bank_drained[b], 1)
            for br in range(2):
                drain(kswT[:, br, :, :].rearrange("p a t -> p (a t)"))
            drain(kcT.rearrange("p a n -> p (a n)"), 2 * NCMP)
            b = full()
            for j in range(4):
                q = slice(32 * j, 32 * j + 32)
                last = nc.scalar.activation(vblk[q, :, j, :], bank[b][q, 0:GROUPS * HD].rearrange("p (g d) -> p g d", g=GROUPS),
                                            ACT.Copy)
            last.then_inc(bank_drained[b], 1)
            for n in range(4):
                drain(qT[:, 2 * n:2 * n + 2, :].rearrange("p j t -> p (j t)"))
            for t in range(TILES):
                drain(vsw[:, t, :])
            for t in range(TILES):
                b = full()
                nc.scalar.activation(gates[:, t, :, :].rearrange("p b h -> p (b h)"), bank[b][:, 0:3 * HEADS], ACT.Exp,
                                     scale=-1.0).then_inc(bank_drained[b], 1)
            for t in range(TILES):
                banks.skip(5)
                act.wait_ge(cmp_ready, t + 1)
                nc.scalar.activation(sc_exp, sc_raw, ACT.Exp, scale=NSA_SCALE).then_inc(cmp_exp, 1)
                attention(unit0("nsa", t), range(NSA_UNITS), t + 1, NSA_SCALE, lambda u, r: (1 + u // 8, 2 * (u % 8) + r))
                drain_mixedT()
                banks.skip(2)
                layer_norm_root(t)
            for t in range(TILES):
                drain_hT(t)
            peer_drains(range(TILES), list(range(PH)))

            def gate_exps(item):
                act.wait_ge(gate_in_ready, item + 1)
                nc.scalar.activation(gate_e[:, item % 2, :], gate_in[:, item % 2, :], ACT.Exp,
                                     accum_out=gate_sum[:, item % 2:item % 2 + 1]).then_inc(gate_e_ready, 1)

            def mla_slices(t):
                def latent_keys():
                    drain_hT(t)
                    drain(ckv, KV_LORA + ROPE)
                    rms_root(2 * t + 1)
                    b = full()
                    for k in range(2):
                        nc.scalar.activation(ckvT[:, k, :], bank[b][:, k * P:(k + 1) * P], ACT.Copy, scale=kv_gain[:, k:k + 1])
                    nc.scalar.activation(kT[HD:QK, :, t * P:(t + 1) * P], spread(bank[b][HD:QK, 2 * P:3 * P], 1, HEADS),
                                         ACT.Copy).then_inc(bank_drained[b], 1)

                def keys_values():
                    for n in range(2):
                        b = full()
                        src = bank[b][:].rearrange("p (i s) -> p i s", i=4)
                        dst = kT[0:HD, 8 * n:8 * n + 8, t * P:(t + 1) * P].rearrange("p (i e) s -> p e i s", e=2)
                        for e in range(2):
                            last = nc.scalar.activation(dst[:, e, :, :], src[e * HD:(e + 1) * HD, :, :], ACT.Copy)
                        last.then_inc(bank_drained[b], 1)
                    for n in range(2):
                        drain(vM[:, t, n * 512:(n + 1) * 512])
                    for n in range(2):
                        drain(cq[:, n * 384:(n + 1) * 384], 384)
                    rms_root(2 * t + 2)
                    for n, w in ((0, 4), (1, 2)):
                        b = full()
                        for k in range(w):
                            last = nc.scalar.activation(cqT[:, 4 * n + k, :], bank[b][:, k * P:(k + 1) * P], ACT.Copy,
                                                        scale=q_gain[:, 4 * n + k:4 * n + k + 1])
                        last.then_inc(bank_drained[b], 1)

                def queries():
                    for n in range(3):
                        drain(q_nat[:, n * 512:(n + 1) * 512])

                def attention_a():
                    for n in range(4):
                        b = full()
                        nc.scalar.activation(mlaqT(t)[:, 4 * n:4 * n + 4, :].rearrange("p h t -> p (h t)"), bank[b][0:QK, :],
                                             ACT.Copy).then_inc(bank_drained[b], 1)
                    attention(unit0("mla", t), range(4), t + 1, MLA_SCALE, lambda u, r: (0, 2 * u + r))

                def attention_b():
                    attention(unit0("mla", t), range(4, 8), t + 1, MLA_SCALE, lambda u, r: (0, 2 * u + r))
                    drain_mixedT()

                def output():
                    banks.skip(2)
                    layer_norm_root(mla_ln(t) - 1)
                    drain_hT(t)

                def peer_a():
                    peer_drains([t], list(range(4)))

                def peer_b():
                    peer_drains([t], list(range(4, 8)))

                return [latent_keys, keys_values, queries, attention_a, attention_b, output, peer_a, peer_b]

            gate_exps(0)
            for phase in range(2 * TILES):
                slices = mla_slices(phase - 1) if phase in (1, 2) else None
                for head in range(PH):
                    item = phase * PH + head
                    if slices:
                        slices[head]()
                    if item + 1 < ITEMS:
                        gate_exps(item + 1)
                    step0 = item * TOPK
                    with act.Fori(0, TOPK // SLOTS, 1) as i:
                        for k in range(SLOTS):
                            act.wait_ge(dot_ready, i * SLOTS + (step0 + k + 1))
                            nc.scalar.activation(gelu[:, k:k + 1], dots[:, k:k + 1], ACT.Gelu_apprx_tanh).then_inc(gelu_ready, 1)
                layer_norm_root(peer_ln(phase) - 1)

        @block.vector
        def _(dve):
            banks = Banks()
            chain = [0]

            def link(ins):
                chain[0] += 1
                ins.then_inc(dve_chain, 1)
                dve.wait_ge(dve_chain, chain[0])

            def full():
                b, use = banks.take()
                dve.wait_ge(bank_filled[b], use + 1)
                return b, use

            def attention(first, units, key_blocks, scale, table_of, finish):
                lo = 2 * P - key_blocks * P

                def scores(u, place):
                    n = first + u
                    b, use = place
                    dve.wait_ge(bank_filled[b], use + 1)
                    for r in range(2):
                        last = nc.vector.tensor_tensor_reduce(
                            out=S[:, n % 2, r, lo:2 * P], in0=bank[b][:, r * 2 * P + lo:(r + 1) * 2 * P], in1=table_of(u, r)[:, lo:2 * P],
                            scale=1.0, scalar=LOWEST, op0=ALU.add, op1=ALU.max, accum_out=row_max[:, n % 2 * 2 + r:n % 2 * 2 + r + 1])
                    last.then_inc(bank_drained[b], 1)
                    dve.wait_ge(bank_drained[b], use + 1)
                    nc.vector.tensor_scalar(neg_max[:, n % 2 * 2:n % 2 * 2 + 2], row_max[:, n % 2 * 2:n % 2 * 2 + 2], -scale, None,
                                            ALU.mult).then_inc(scores_ready, 1)

                def drain_T(u):
                    b, use = full()
                    w = 2 * key_blocks * P
                    nc.vector.tensor_copy(probsT[:, (first + u) % 2, 0:2 * key_blocks, :].rearrange("p b t -> p (b t)"),
                                          bank[b][:, 0:w]).then_inc(bank_drained[b], 1)

                scores(units[0], banks.take())
                for u in units:
                    if u != units[-1]:
                        scores(u + 1, banks.take())
                    drain_T(u)
                    if u != units[0] and (u - 1) % 4 == 3:
                        finish(u - 1)
                finish(units[-1])

            def layer_norm(e, t, halves):
                y = h[:, t, :]
                if e == 0:
                    dve.wait_ge(x_loaded, 16)
                for half in range(2):
                    src, before, after = halves(half)
                    before()
                    sl = slice(half * 512, (half + 1) * 512)
                    ins = nc.vector.scalar_tensor_tensor(out=y[:, sl], in0=y[:, sl], scalar=ALPHA, in1=src, op0=ALU.mult, op1=ALU.add)
                    after(ins)
                for half in range(2):
                    ins = nc.vector.bn_stats(stat[:, half, :], y[:, half * 512:(half + 1) * 512])
                link(ins)
                link(nc.vector.bn_aggr(moments, stat))
                nc.vector.tensor_scalar(rstd, moments[:, 1:2], LN_EPS, None, ALU.add).then_inc(var_ready, 1)
                dve.wait_ge(std_ready, e + 1)
                link(nc.vector.reciprocal(rstd, std))
                link(nc.vector.tensor_scalar(y, y, moments[:, 0:1], rstd, ALU.subtract, ALU.mult))
                dve.wait_ge(ln_loaded, 16 * (LN_LOAD[e] + 1))
                link(nc.vector.tensor_tensor(y, y, lnp[:, 0, :], ALU.mult))
                nc.vector.tensor_tensor(y, y, lnp[:, 1, :], ALU.add).then_inc(ln_done, 1)

            def bank_halves():
                def halves(half):
                    b, use = banks.take()

                    def before():
                        dve.wait_ge(bank_filled[b], use + 1)

                    def after(ins):
                        ins.then_inc(bank_drained[b], 1)
                        dve.wait_ge(bank_drained[b], use + 1)

                    return bank[b][:], before, after
                return halves

            def acc_halves(phase):
                def halves(half):
                    def before():
                        dve.wait_ge(slot_free, SLOTS + (phase + 1) * PH * TOPK)

                    def after(ins):
                        if half:
                            ins.then_inc(acc_read, 1)
                            dve.wait_ge(acc_read, phase + 1)

                    return acc[:, half * 512:(half + 1) * 512], before, after
                return halves

            dve.wait_ge(const_loaded, 16)
            banks.skip(14)
            for t in range(TILES):
                b, use = banks.take()
                dve.wait_ge(bank_drained[b], use + 1)
                g = gates[:, t, :, :]
                link(nc.vector.tensor_scalar(g, g, 1.0, None, ALU.add))
            dve.wait_ge(alibi_loaded, 16)
            for t in range(TILES):
                for e in range(2):
                    b, use = full()
                    src = bank[b][:, 0:8 * NCMP].rearrange("p (a x) -> p a x", a=2)
                    dst = sc_raw.rearrange("p (a e r) n -> p e a (r n)", e=2, r=4)[:, e, :, :]
                    add = cmp_bias[:, t, :, :].rearrange("p (a e r) n -> p e a (r n)", e=2, r=4)[:, e, :, :]
                    nc.vector.tensor_tensor(dst, src, add, ALU.add).then_inc(bank_drained[b], 1)
                dve.wait_ge(bank_drained[b], use + 1)
                link(nc.vector.reduce_max(cmp_max, sc_raw, AX.X))
                nc.vector.tensor_tensor(sc_raw, sc_raw, spread(cmp_max, 2, NCMP), ALU.subtract).then_inc(cmp_ready, 1)
                dve.wait_ge(cmp_exp, t + 1)
                nc.vector.reduce_sum(row_sum[:, 0, :], sc_exp, AX.X)
                if t == 0:
                    dve.wait_ge(zeroed, 1)
                nc.vector.tensor_tensor(pc[:, :, 0:NCMP], sc_exp, spread(cmp_mask[:, t, :], 1, HEADS), ALU.mult).then_inc(cmp_probs, 1)
                b, use = full()
                nc.vector.tensor_copy(pcT.rearrange("p g t -> p (g t)"), bank[b][:]).then_inc(bank_drained[b], 1)

                def coefficients(br, hs):
                    link(nc.vector.tensor_tensor(denom[:, br, hs], gates[:, t, br, hs], row_sum[:, br, hs], ALU.mult))
                    link(nc.vector.reciprocal(coef[:, br, hs], denom[:, br, hs]))

                coefficients(0, slice(0, HEADS))
                mix = mixed.rearrange("p (h d) -> p h d", h=HEADS)
                for half in range(2):
                    b, use = full()
                    hs = slice(8 * half, 8 * half + 8)
                    nc.vector.tensor_tensor(mix[:, hs, :], bank[b][:].rearrange("p (h d) -> p h d", h=8),
                                            spread(coef[:, 0, hs], 2, HD), ALU.mult).then_inc(bank_drained[b], 1)

                def finish(u):
                    n = (unit0("nsa", t) + u) // 4 + 1
                    br, hs = 1 + u // 8, slice(8 * (u // 4 % 2), 8 * (u // 4 % 2) + 8)
                    dve.wait_ge(heads_filled, n)
                    coefficients(br, hs)
                    out8 = heads_out[:].rearrange("p (h d) -> p h d", h=8)
                    tmp = onehot[:].rearrange("p a b -> p (a b)")[:, 0:512].rearrange("p (h d) -> p h d", h=8)
                    nc.vector.tensor_tensor(tmp, out8, spread(coef[:, br, hs], 2, HD), ALU.mult).then_inc(heads_drained, 1)
                    dve.wait_ge(heads_drained, n)
                    ins = nc.vector.tensor_tensor(mix[:, hs, :], mix[:, hs, :], tmp, ALU.add)
                    if u == NSA_UNITS - 1:
                        ins.then_inc(mixed_ready, 1)
                    else:
                        link(ins)

                attention(unit0("nsa", t), list(range(NSA_UNITS)), t + 1, NSA_SCALE,
                          lambda u, r: bias[:, 2 * (u % 8) + r, :], finish)
                banks.skip(2)
                layer_norm(t, t, bank_halves())
            banks.skip(2 * TILES)
            scored = {}

            def peer_banks(tiles, part):
                banks.skip(1)
                for c in part:
                    if c != part[-1]:
                        banks.skip(1)
                    for t in tiles:
                        scored[t, c] = (banks.n % 3, banks.n // 3)
                    banks.skip(1)

            peer_banks(range(TILES), list(range(PH)))

            def top_k(item):
                phase, head = divmod(item, PH)
                t = phase % TILES
                b, use = scored[t, head]
                dve.wait_ge(bank_drained[b], use + 1)
                for c in range(2):
                    s = keyscore[:, t, 2 * head + c, :]
                    link(nc.vector.max(top_val[:, c, 0:8], s))
                    link(nc.vector.match_replace(work[:, c, :], top_val[:, c, 0:8], s, LOWEST))
                    nc.vector.max_index(top_pos[:, c, 0:8], top_val[:, c, 0:8], s)
                    link(nc.vector.max(top_val[:, c, 8:16], work[:, c, :]))
                    link(nc.vector.max_index(top_pos[:, c, 8:16], top_val[:, c, 8:16], work[:, c, :]))
                link(nc.vector.tensor_copy(top_idx[:], top_pos[:]))
                link(nc.vector.tensor_scalar(top_idx[:, 0, :], top_idx[:, 0, :], float(NKEYS), None, ALU.mult))
                for dst, src in ((cand[:, 0, :], top_val), (cand_idx[:], top_idx)):
                    for i in range(5):
                        nc.vector.tensor_scalar(dst[:, RUN_AT[i]:RUN_AT[i] + RUN[i]], src[:, 1, 0:RUN[i]], src[:, 0, i:i + 1], None, ALU.add)
                    nc.vector.tensor_tensor(dst[:, RUN_AT[5]:RUN_AT[8]].rearrange("p (i j) -> p i j", j=2),
                                            spread(src[:, 1, 0:2], 1, 3), spread(src[:, 0, 5:8], 2, 2), ALU.add)
                    link(nc.vector.tensor_scalar(dst[:, RUN_AT[8]:NCAND], src[:, 0, 8:16], src[:, 1, 0:1], None, ALU.add))
                link(nc.vector.max(best[:, 0:8], cand[:, 0, :]))
                link(nc.vector.match_replace(cand[:, 1, :], best[:, 0:8], cand[:, 0, :], LOWEST))
                nc.vector.max_index(best_pos[:, 0:8], best[:, 0:8], cand[:, 0, :])
                link(nc.vector.max(best[:, 8:16], cand[:, 1, :]))
                nc.vector.tensor_scalar(gate_in[:, item % 2, :], best[:], best[:, 0:1], None, ALU.subtract).then_inc(gate_in_ready, 1)
                link(nc.vector.max_index(best_pos[:, 8:16], best[:, 8:16], cand[:, 1, :]))
                link(nc.vector.tensor_copy(best_posf[:], best_pos[:]))
                link(nc.vector.tensor_tensor(onehot[:], spread(best_posf[:], 2, NCAND), spread(number, 1, TOPK), ALU.is_equal))
                link(nc.vector.tensor_tensor(onehot[:], onehot[:], spread(cand_idx[:], 1, TOPK), ALU.mult))
                link(nc.vector.reduce_sum(best_idx[:], onehot[:], AX.X))
                nc.vector.tensor_copy(expert_id[:, item % 2, :], best_idx[:]).then_inc(ids_ready, 1)

            def stream(item):
                s = item % 2
                dve.wait_ge(gate_e_ready, item + 1)
                link(nc.vector.reciprocal(inv_sum[:, s:s + 1], gate_sum[:, s:s + 1]))
                link(nc.vector.tensor_scalar(gate_w[:, s, :], gate_e[:, s, :], inv_sum[:, s:s + 1], None, ALU.mult))
                step0 = item * TOPK
                with dve.Fori(0, TOPK // SLOTS, 1) as i:
                    for k in range(SLOTS + 1):
                        if k < SLOTS:
                            dve.wait_ge(gathered[k], i * 16 + 16 * (item * TOPK // SLOTS + 1))
                            u_row = ring[:, k, 0:D]
                            nc.vector.tensor_tensor_reduce(out=u_row, in0=u_row, in1=xdup[:], scale=1.0, scalar=0.0, op0=ALU.mult,
                                                           op1=ALU.add, accum_out=dots[:, k:k + 1]).then_inc(dot_ready, 1)
                        if k:
                            j = k - 1
                            dve.wait_ge(gelu_ready, i * SLOTS + (step0 + j + 1))
                            dve.wait_ge(slot_free, i * SLOTS + (step0 + j + 1 + SLOTS - 2))
                            nc.vector.tensor_scalar(diag[:, j % 2, :], ident, gelu[:, j:j + 1], gate_w[:, s, bass.ds(i * SLOTS + j, 1)],
                                                    ALU.mult, ALU.mult).then_inc(diag_ready, 1)

            def rms(n, data, width):
                link(nc.vector.tensor_tensor_reduce(out=rope_tmp[:, 0:width], in0=data, in1=data, scale=1.0, scalar=0.0,
                                                    op0=ALU.mult, op1=ALU.add, accum_out=rms_r))
                nc.vector.tensor_scalar(rms_in, rms_r, 1.0 / width, RMS_EPS, ALU.mult, ALU.add).then_inc(rms_ready, 1)
                dve.wait_ge(rms_std_ready, n)
                link(nc.vector.reciprocal(rms_r, rms_std))
                link(nc.vector.tensor_scalar(data, data, rms_r, None, ALU.mult))

            def mla_slices(t):
                cos, sin = rope[:, t, 0, :], rope[:, t, 1, :]

                def rotate(x1, x2, y1, y2, tmp, cosb, sinb):
                    nc.vector.tensor_tensor(tmp[0], x1, cosb, ALU.mult)
                    nc.vector.tensor_tensor(tmp[1], x2, sinb, ALU.mult)
                    nc.vector.tensor_tensor(tmp[2], x2, cosb, ALU.mult)
                    link(nc.vector.tensor_tensor(tmp[3], x1, sinb, ALU.mult))
                    nc.vector.tensor_tensor(y1, tmp[0], tmp[1], ALU.subtract)
                    return nc.vector.tensor_tensor(y2, tmp[2], tmp[3], ALU.add)

                def latent_keys():
                    banks.skip(2)
                    b, use = banks.take()
                    dve.wait_ge(bank_drained[b], use + 1)
                    rms(2 * t + 1, ckv[:, 0:KV_LORA], KV_LORA)
                    rotate(ckv[:, KV_LORA:KV_LORA + HALF], ckv[:, KV_LORA + HALF:KV_LORA + ROPE], ropeT[:, HD:HD + HALF],
                           ropeT[:, HD + HALF:QK], [kr_tmp[:, i, :] for i in range(4)], cos, sin).then_inc(latent_ready, 1)
                    banks.skip(1)

                def keys_values():
                    banks.skip(4)
                    for _ in range(2):
                        b, use = banks.take()
                        dve.wait_ge(bank_drained[b], use + 1)
                    rms(2 * t + 2, cq, Q_LORA)
                    dve.sem_inc(latent_ready, 1)
                    banks.skip(2)

                def queries():
                    for _ in range(3):
                        b, use = banks.take()
                        dve.wait_ge(bank_drained[b], use + 1)
                    q3 = q_nat.rearrange("p (h e) -> p h e", h=HEADS)
                    x1, x2 = q3[:, :, HD:HD + HALF], q3[:, :, HD + HALF:QK]
                    tmp = [rope_tmp[:, i * 256:(i + 1) * 256].rearrange("p (h k) -> p h k", h=HEADS) for i in range(4)]
                    rotate(x1, x2, x1, x2, tmp, spread(cos, 1, HEADS), spread(sin, 1, HEADS)).then_inc(q_rotated, 1)

                def finish(u):
                    n = (unit0("mla", t) + u) // 4 + 1
                    hs = slice(8 * (u // 4), 8 * (u // 4) + 8)
                    dve.wait_ge(heads_filled, n)
                    link(nc.vector.reciprocal(coef[:, 0, hs], row_sum[:, 0, hs]))
                    nc.vector.tensor_tensor(mixed.rearrange("p (h d) -> p h d", h=HEADS)[:, hs, :],
                                            heads_out[:].rearrange("p (h d) -> p h d", h=8), spread(coef[:, 0, hs], 2, HD),
                                            ALU.mult).then_inc(heads_drained, 1)
                    if u == MLA_UNITS - 1:
                        dve.wait_ge(heads_drained, n)
                        dve.sem_inc(mixed_ready, 1)

                def attention_a():
                    banks.skip(4)
                    attention(unit0("mla", t), list(range(4)), t + 1, MLA_SCALE, lambda u, r: causal, finish)

                def attention_b():
                    attention(unit0("mla", t), list(range(4, 8)), t + 1, MLA_SCALE, lambda u, r: causal, finish)
                    banks.skip(2)

                def output():
                    layer_norm(mla_ln(t) - 1, t, bank_halves())
                    banks.skip(2)

                def peer_a():
                    peer_banks([t], list(range(4)))

                def peer_b():
                    peer_banks([t], list(range(4, 8)))

                return [latent_keys, keys_values, queries, attention_a, attention_b, output, peer_a, peer_b]

            top_k(0)
            for phase in range(2 * TILES):
                t = phase % TILES
                dve.wait_ge(ln_done, 2 if phase < 2 else mla_ln(t))
                link(nc.vector.tensor_copy(xdup[:], h[:, t, :]))
                slices = mla_slices(phase - 1) if phase in (1, 2) else None
                for head in range(PH):
                    item = phase * PH + head
                    if slices:
                        slices[head]()
                    if item + 1 < ITEMS:
                        top_k(item + 1)
                    stream(item)
                layer_norm(peer_ln(phase) - 1, t, acc_halves(phase))


def _kxn(w):
    k, n = w.shape
    return w.reshape(k // P, P, n).transpose(1, 0, 2).reshape(P, -1)


def _constants():
    p = np.arange(P)
    slope = np.array([2.0 ** (-8.0 * (i + 1) / HEADS) for i in range(HEADS)], np.float32)
    out = {"ident": np.eye(P, dtype=np.float32)}
    dist = P + p[:, None] - np.arange(2 * P)[None, :]
    table = -(slope[None, :, None] / np.float32(NSA_SCALE)) * dist[:, None, :].astype(np.float32)
    out["alibi"] = np.where(dist[:, None, :] >= 0, table, np.float32(MASKED)).astype(np.float32)
    out["causal"] = np.where(dist >= 0, 0.0, MASKED).astype(np.float32)
    t = np.arange(TILES)[None, :] * P + p[:, None]
    end = np.arange(NCMP) * CMP_STRIDE + CMP_LEN - 1
    dist_c = t[:, :, None] - end
    seen = (dist_c >= 0) & (np.arange(NCMP) < NCMP - 1)
    table = -(slope[None, None, :, None] / np.float32(NSA_SCALE)) * dist_c[:, :, None, :].astype(np.float32)
    out["cmp_bias"] = np.where(seen[:, :, None, :], table, np.float32(MASKED)).astype(np.float32)
    out["cmp_mask"] = seen.astype(np.float32)
    inv = (1.0 / (np.float32(10000.0) ** (np.arange(0, ROPE, 2, dtype=np.float32) / np.float32(ROPE)))).astype(np.float32)
    ang = t.astype(np.float32)[:, :, None] * inv
    out["rope"] = np.stack([np.cos(ang), np.sin(ang)], 2).astype(np.float32)
    out["number"] = np.broadcast_to(np.arange(NCAND, dtype=np.float32), (P, NCAND))
    return {k: np.ascontiguousarray(v.reshape(P, -1)) for k, v in out.items()}


def _layout(a):
    w = a["nsa_w_in"][0]
    q = w[:, 0:1024].reshape(D, 2, 2, 4, HD)
    q = q.transpose(0, 1, 3, 2, 4).reshape(D, 1024)
    kc, vc, ks, vs, kw, vw = [w[:, 1024 + 256 * i:1280 + 256 * i] for i in range(6)]
    gate = w[:, 2560:2608].reshape(D, HEADS, 3).transpose(0, 2, 1).reshape(D, 48)
    cat = np.concatenate
    wo = a["nsa_w_out"][0]
    ch = {
        (0, "kvc"): _kxn(cat([kc, vc], 1)), (0, "ksw"): _kxn(cat([ks, kw], 1)),
        (0, "ck1"): _kxn(a["nsa_cmp_k_w1"][0]), (0, "cv1"): _kxn(a["nsa_cmp_v_w1"][0]),
        (0, "q0"): _kxn(q[:, 0:512]), (0, "q1"): _kxn(q[:, 512:1024]), (0, "vsw"): _kxn(cat([vs, vw], 1)),
        (0, "gate"): _kxn(gate), (0, "wo0"): _kxn(wo[:, 0:512]), (0, "wo1"): _kxn(wo[:, 512:1024]),
        (1, "dkv"): _kxn(cat([a["mla_w_dkv"], a["mla_w_kr"]], 1)),
        (1, "uk"): _kxn(a["mla_w_uk"].reshape(KV_LORA, 1024)), (1, "uv"): _kxn(a["mla_w_uv"].reshape(KV_LORA, 1024)),
    }
    dq, uq, mo = a["mla_w_dq"][0], a["mla_w_uq"][0].reshape(Q_LORA, HEADS * QK), a["mla_w_out"][0]
    for i in range(2):
        ch[1, f"dq{i}"] = _kxn(dq[:, i * 384:(i + 1) * 384])
        ch[1, f"mo{i}"] = _kxn(mo[:, i * 512:(i + 1) * 512])
    for i in range(3):
        ch[1, f"uq{i}"] = _kxn(uq[:, i * 512:(i + 1) * 512])
    for l in range(2):
        for c in range(PH):
            wq = _kxn(a["peer_w_q"][l][:, c * 256:(c + 1) * 256])
            keys = a["peer_subkeys"][l][c].transpose(2, 0, 1).reshape(P, 2 * NKEYS)
            ch[l, f"pq{c}"] = cat([wq, keys], 1)
    weights = cat([ch[l, n].reshape(-1) for l in range(2) for n, _ in LAYERS[l]])
    c = _constants()
    c["pe"] = cat([a[f"nsa_cmp_{n}_pe"][0].reshape(16, P).T for n in "kv"], 1)
    c["w2k"], c["w2v"] = a["nsa_cmp_k_w2"][0], a["nsa_cmp_v_w2"][0]
    c["q_gain"] = a["mla_q_norm_g"][0].reshape(6, P).T
    c["kv_gain"] = a["mla_kv_norm_g"].reshape(2, P).T
    xs = a["x"][0]
    ln = np.stack([cat([a["nsa_ln_g"][0], a["nsa_ln_b"][0]]), cat([a["mla_ln_g"][0], a["mla_ln_b"][0]]),
                   cat([a["peer_ln_g"][0], a["peer_ln_b"][0]]), cat([a["peer_ln_g"][1], a["peer_ln_b"][1]])])
    return {
        "x": xs, "xT": xs.T.reshape(KD, P, SEQ).transpose(1, 0, 2), "weights": weights,
        "consts": cat([c[n] for n in CONST], 1), "alibi": c["alibi"].reshape(P, HEADS, 2 * P), "ln_params": ln,
        "experts0": cat([a["peer_u"][0], a["peer_v"][0]], 1), "experts1": cat([a["peer_u"][1], a["peer_v"][1]], 1),
    }


def kernel(**inputs):
    import concourse.bacc as bacc
    from concourse.bass_utils import run_bass_kernel_spmd

    arrays = {k: np.ascontiguousarray(v) for k, v in _layout({k: np.asarray(v) for k, v in inputs.items()}).items()}
    nc = bacc.Bacc("TRN2", target_bir_lowering=False, num_devices=1)
    args = [nc.dram_tensor(k, v.shape, mybir.dt.from_np(v.dtype), kind="ExternalInput").ap() for k, v in arrays.items()]
    out = nc.dram_tensor("out", (SEQ, D), F32, kind="ExternalOutput").ap()
    trunk_kernel(nc, *args, out)
    r = run_bass_kernel_spmd(nc, [arrays], core_ids=[0])
    return np.asarray(r.results[0]["out"]).reshape(1, SEQ, D)
```

```python
import concourse.bass as bass
import numpy as np
from concourse import mybir
from concourse.alu_op_type import AluOpType as ALU
from contextlib import ExitStack

F32 = mybir.dt.float32
U32 = mybir.dt.uint32
ACT = mybir.ActivationFunctionType
AX = mybir.AxisListType

P = 128
D = 1024
KD = D // P
SEQ = 256
TILES = SEQ // P
HEADS = 16
HD = 64
GROUPS = 4
CMP_STRIDE = 16
CMP_LEN = 32
NCMP = SEQ // CMP_STRIDE
NSA_SCALE = HD ** -0.5
ROPE = 32
HALF = ROPE // 2
QK = HD + ROPE
KV_LORA = 256
Q_LORA = 768
MLA_SCALE = QK ** -0.5
PH = 8
TOPK = 16
NKEYS = 128
EXPERTS = NKEYS * NKEYS
ALPHA = 4.0 ** 0.25
LN_EPS = 1e-5
RMS_EPS = 1e-6
MASKED = -1.0e30
LOWEST = -3.0e38

RUN = [TOPK // (i + 1) for i in range(TOPK)]
RUN_AT = [sum(RUN[:i]) for i in range(TOPK)]
NCAND = sum(RUN)

SLOTS = 8
WSLOTS = 3
WCOLS = 4096

NSA_CHUNKS = [("kvc", 4096), ("ck1", 2048), ("cv1", 2048), ("ksw", 4096), ("q0", 4096), ("q1", 4096),
              ("vsw", 4096), ("gate", KD * 48), ("wo0", 4096), ("wo1", 4096)]
PEER_W = KD * 256 + 2 * NKEYS
PEER_CHUNKS = [(f"pq{c}", PEER_W) for c in range(PH)]
MLA_CHUNKS = [("dkv", KD * (KV_LORA + ROPE)), ("uk", 2048), ("uv", 2048), ("dq0", KD * 384), ("dq1", KD * 384),
              ("uq0", 3072), ("uq1", 3072), ("uq2", 3072), ("mo0", 4096), ("mo1", 4096)]
LAYERS = [NSA_CHUNKS + PEER_CHUNKS, MLA_CHUNKS + PEER_CHUNKS]




def chunk_places():
    at, off = {}, 0
    for l, chunks in enumerate(LAYERS):
        for name, width in chunks:
            at[l, name] = (off, width)
            off += width * P
    return at


BURST = 4
BURSTS = TOPK // BURST
SLOTS_OF_PHASE = PH * BURSTS
ATT = {("n", 0): 8, ("n", 1): 16, ("m", 0): 4, ("m", 1): 8}


def att_steps(kind, t):
    return [(kind, t, "att", u) for u in range(-1, ATT[kind, t] + 1)]


def pq_steps(layer, t, lo=0, hi=PH):
    return [(layer, t, "pq", c) for c in range(lo, hi + 1)]


def phase_slots(phase):
    slots = [[] for _ in range(SLOTS_OF_PHASE)]
    if phase == 0:
        for n, step in enumerate(pq_steps(0, 0, 3)):
            slots[2 + 4 * n].append(step)
        line = [("n", 1, "cs"), ("n", 1, "ct"), ("n", 1, "cv")] + att_steps("n", 1) + [("n", 1, "o"), ("n", 1, "w", 0), ("n", 1, "w", 1),
                                                                                       ("n", 1, "h")]
        for n, step in enumerate(line):
            slots[n].append(step)
        at = len(line)
        pq = pq_steps(0, 1)
    elif phase < 2 * TILES - 1:
        t = phase - 1
        line = [[("p", t, "ln", t)], [("m", t, "h0")], [("m", t, "dkv")], [("m", t, "dq", 0)], [("m", t, "dq", 1), ("m", t, "lt")],
                [("m", t, "uk")], [("m", t, "uv")], [("m", t, "ct")]]
        line += [[("m", t, "uq", n)] for n in range(3)]
        line += [[("m", t, "qt", n)] for n in range(2)]
        line += [[x] for x in att_steps("m", t)]
        line += [[("m", t, "o")], [("m", t, "w", 0)], [("m", t, "w", 1)], [("m", t, "h")]]
        for n, steps in enumerate(line):
            slots[n] += steps
        at = len(line)
        pq = pq_steps(1, t)
    else:
        if phase == 2 * TILES - 1:
            slots[0].append(("p", 0, "ln", phase - 1))
        return slots
    for n in range(at, SLOTS_OF_PHASE):
        for _ in range(2 if len(pq) > SLOTS_OF_PHASE - n else 1):
            if pq:
                slots[n].append(pq.pop(0))
    assert not pq
    return slots


PROLOGUE = ([("n", 0, "cs"), ("n", 0, "ct"), ("n", 0, "cv")] + att_steps("n", 0)
            + [("n", 0, "o"), ("n", 0, "w", 0), ("n", 0, "w", 1), ("n", 0, "h")] + pq_steps(0, 0)[:3])

CONST = {}
_at = 0
for _name, _w in [("ident", P), ("cmp_mask", TILES * NCMP), ("causal", 2 * P),
                  ("rope", TILES * 2 * HALF), ("number", NCAND), ("pe", 2 * 16), ("w2k", HD), ("w2v", HD),
                  ("q_gain", 6), ("kv_gain", 2), ("q_up", 8), ("down", HEADS)]:
    CONST[_name] = (_at, _w)
    _at += _w
NCONST = _at


def spread(ap, axis, n):
    ap = ap.unsqueeze(axis)
    shape = list(ap.shape)
    shape[axis] = n
    return ap.broadcast_to(shape)


def trunk_kernel(nc, x, xT, weights, consts, alibi, cmp_table, ln_params, experts0, experts1, out):
    ctx = ExitStack()
    with ctx:
        def sb(name, shape, dt=F32):
            return ctx.enter_context(nc.sbuf_tensor("t_" + name, shape, dt))

        def pb(name, shape):
            return ctx.enter_context(nc.psum_tensor("p_" + name, shape, F32))

        def sem(name):
            return ctx.enter_context(nc.semaphore(name))

        ring = sb("ring", [P, SLOTS, 2 * D])
        wring = sb("wring", [P, WSLOTS, WCOLS])
        h = sb("h", [P, TILES, D])
        hT = sb("hT", [P, KD, SEQ])
        keyscore = sb("keyscore", [P, TILES, 2 * PH, NKEYS])
        lnp = sb("lnp", [P, 2, D])
        cst = sb("cst", [P, NCONST])
        kT_all = sb("kT", [P, HEADS, SEQ])
        kT = kT_all[0:QK, :, :]
        vM = sb("vM", [P, TILES, D])
        S = sb("S", [P, 2, 512])
        shared = sb("shared", [P, 3072])
        ropeT = sb("ropeT", [P, QK])
        small = sb("small", [P, 256])
        gates = sb("gates", [P, TILES, 3, HEADS])
        coef = sb("coef", [P, 3, HEADS])
        diag = sb("diag", [P, BURST, P])
        pqT = sb("pqT", [P, 2, 2, P])
        work = sb("work", [P, 2, NKEYS])
        onehot = sb("onehot", [P, TOPK, NCAND])
        top_val = sb("top_val", [P, 2, TOPK])
        top_pos = sb("top_pos", [P, 2, TOPK], U32)
        top_idx = sb("top_idx", [P, 2, TOPK])
        cand = sb("cand", [P, 2, NCAND])
        cand_idx = sb("cand_idx", [P, NCAND])
        best = sb("best", [P, TOPK])
        best_pos = sb("best_pos", [P, TOPK], U32)
        best_posf = sb("best_posf", [P, TOPK])
        best_idx = sb("best_idx", [P, TOPK])
        expert_id = sb("expert_id", [P, 2, TOPK], U32)
        gate_in = sb("gate_in", [P, 2, TOPK])
        gate_e = sb("gate_e", [P, 2, TOPK])
        gate_sum = sb("gate_sum", [P, 2])
        gate_w = sb("gate_w", [P, 2, TOPK])
        dots = sb("dots", [P, SLOTS])
        gelu = sb("gelu", [P, SLOTS])

        acc = pb("acc", [P, D])
        xdup = pb("xdup", [P, D])
        bank = [pb(f"bank{i}", [P, 512]) for i in range(3)]
        heads_out = pb("heads_out", [P, 512])

        def cuts(ap, what):
            at, parts = 0, []
            for n in what:
                parts.append(ap[:, at:at + n])
                at += n
            assert at <= ap.shape[1]
            return parts

        alibi_sb, qT, vblk, kcT = cuts(kT_all[:].rearrange("p h s -> p (h s)"), [4 * P, 8 * SEQ, GROUPS * 4 * HD, 2 * NCMP])
        alibi_sb = alibi_sb.rearrange("p (o s) -> p o s", o=2)
        qT = qT.rearrange("p (j t) -> p j t", j=8)
        vblk = vblk.rearrange("p (g j d) -> p g j d", g=GROUPS, j=4)
        kcT = kcT.rearrange("p (a n) -> p a n", a=2)
        kswT, vsw = cuts(vM[:].rearrange("p t c -> p (t c)"), [4 * SEQ, TILES * 512])
        kswT = kswT.rearrange("p (b a t) -> p b a t", b=2, a=2)
        vsw = vsw.rearrange("p (t c) -> p t c", t=TILES)
        pc, pcT, sc_raw, sc_exp, cmp_bias = cuts(keyscore[:, 1, :, :].rearrange("p c k -> p (c k)"),
                                                 [HEADS * 32, GROUPS * P, HEADS * NCMP, HEADS * NCMP, TILES * HEADS * NCMP])
        pc = pc.rearrange("p (h n) -> p h n", h=HEADS)
        pcT = pcT.rearrange("p (g t) -> p g t", g=GROUPS)
        sc_raw = sc_raw.rearrange("p (h n) -> p h n", h=HEADS)
        sc_exp = sc_exp.rearrange("p (h n) -> p h n", h=HEADS)
        cmp_bias = cmp_bias.rearrange("p (t h n) -> p t h n", t=TILES, h=HEADS)
        kc2, hk, hv, pe_bias = cuts(ring[:].rearrange("p s c -> p (s c)"), [8 * P, GROUPS * NCMP, GROUPS * 4 * 32, 2])
        kc2 = kc2.rearrange("p (v g u) -> p v g u", v=2, g=GROUPS)
        hk = hk.rearrange("p (g n) -> p g n", g=GROUPS)
        hv = hv.rearrange("p (g j n) -> p g j n", g=GROUPS, j=4)

        def view(name):
            a, w = CONST[name]
            return cst[:, a:a + w]

        ident = view("ident")
        cmp_mask = view("cmp_mask").rearrange("p (t n) -> p t n", t=TILES)
        causal = view("causal")
        rope = view("rope").rearrange("p (t c k) -> p t c k", t=TILES, c=2)
        number = view("number")
        pe_cols = view("pe").rearrange("p (v l) -> p v l", v=2)
        w2k, w2v, q_gain, kv_gain, q_up, down = [view(n) for n in ("w2k", "w2v", "q_gain", "kv_gain", "q_up", "down")]

        ckv = shared[:, 0:KV_LORA + ROPE]
        ckvT = shared[:, 288:288 + 2 * P].rearrange("p (k t) -> p k t", k=2)
        cqT = shared[:, Q_LORA:2 * Q_LORA].rearrange("p (k t) -> p k t", k=6)
        cq = shared[:, 2 * Q_LORA:3 * Q_LORA]
        q_nat = shared[:, 2 * Q_LORA:2 * Q_LORA + HEADS * QK]
        mixed = shared[:, 0:D]
        probs = shared[:, D:2 * D].rearrange("p (s k) -> p s k", s=2)
        probsT = shared[:, 2 * D:3 * D].rearrange("p (s b t) -> p s b t", s=2, b=4)
        mixedT = S[:].rearrange("p a b -> p (a b)").rearrange("p (k t) -> p k t", k=KD)
        rope_tmp = S[:].rearrange("p a b -> p (a b)")

        def mlaqT(t):
            return keyscore[0:QK, t, :, :]

        stat = small[:, 0:12].rearrange("p (a b) -> p a b", a=2)
        moments = small[:, 12:14]
        std = small[:, 14:15]
        rstd = small[:, 15:16]
        row_max = small[:, 224:232]
        neg_max = small[:, 232:240]
        rms_in = small[:, 24:25]
        rms_std = small[:, 25:26]
        rms_r = small[:, 26:27]
        cmp_max = small[:, 32:48]
        row_sum = small[:, 48:96].rearrange("p (b h) -> p b h", b=3)
        inv_sum = small[:, 96:112]
        kr_tmp = small[:, 112:176].rearrange("p (a k) -> p a k", a=4)
        denom = small[:, 176:224].rearrange("p (b h) -> p b h", b=3)

        x_loaded = sem("x_loaded")
        xT_loaded = sem("xT_loaded")
        const_loaded = sem("const_loaded")
        alibi_loaded = sem("alibi_loaded")
        cmp_bias_loaded = sem("cmp_bias_loaded")
        xdup_ready = sem("xdup_ready")
        ln_loaded = sem("ln_loaded")
        w_loaded = [sem(f"w_loaded{i}") for i in range(WSLOTS)]
        zeroed = sem("zeroed")
        bank_filled = [sem(f"bank_filled{i}") for i in range(3)]
        bank_drained = [sem(f"bank_drained{i}") for i in range(3)]
        heads_filled = sem("heads_filled")
        heads_drained = sem("heads_drained")
        scores_ready = sem("scores_ready")
        probs_ready = sem("probs_ready")
        cmp_ready = sem("cmp_ready")
        cmp_exp = sem("cmp_exp")
        cmp_probs = sem("cmp_probs")
        gate_exp = sem("gate_exp")
        pe_done = sem("pe_done")
        mixed_ready = sem("mixed_ready")
        var_ready = sem("var_ready")
        std_ready = sem("std_ready")
        ln_done = sem("ln_done")
        rms_ready = sem("rms_ready")
        rms_std_ready = sem("rms_std_ready")
        latent_ready = sem("latent_ready")
        q_rotated = sem("q_rotated")
        dve_chain = sem("dve_chain")
        act_chain = sem("act_chain")
        gate_in_ready = sem("gate_in_ready")
        gate_e_ready = sem("gate_e_ready")
        ids_ready = sem("ids_ready")
        gathers_issued = sem("gathers_issued")
        gathered = [sem(f"gathered{i}") for i in range(SLOTS)]
        slot_free = sem("slot_free")
        dot_ready = sem("dot_ready")
        gelu_ready = sem("gelu_ready")
        diag_ready = sem("diag_ready")
        acc_read = sem("acc_read")
        out_stored = sem("out_stored")

        ITEMS = 2 * TILES * PH
        LN_LOAD = [0, 0, 1, 2, 3, 4, 5, 5]
        LN_ROW = [0, 2, 1, 2, 1, 3]
        places = chunk_places()
        chunk_order, chunk_end = [], []
        place = {}

        def unit0(kind, t):
            before = list(ATT)[:list(ATT).index((kind, t))]
            return sum(ATT[k] for k in before), sum({"n": 4, "m": 2}[k[0]] for k in before)

        def peer_ln(phase):
            return [3, 5, 7, 8][phase]

        def mla_ln(t):
            return [4, 6][t]

        block = ctx.enter_context(nc.Block())

        @block.tensor
        def _(pe):
            fills = [0]
            chunks = {}

            def chunk(layer, name):
                n = len(chunk_order)
                chunk_order.append((layer, name))
                pe.wait_ge(w_loaded[n % WSLOTS], 16 * (n // WSLOTS + 1))
                return wring[:, n % WSLOTS, :]

            def release(n=1):
                chunk_end.extend([((fills[0] - 1) % 3, (fills[0] - 1) // 3)] * n)

            def fill(step):
                b, use = fills[0] % 3, fills[0] // 3
                fills[0] += 1
                if use:
                    pe.wait_ge(bank_drained[b], use)
                place.setdefault(step, []).append((b, use))
                return b

            def drained(step):
                for b, use in place[step]:
                    pe.wait_ge(bank_drained[b], use + 1)

            def transposed_projection(w, cols, src, b, at, k_tiles, tokens):
                for k in range(k_tiles):
                    last = nc.tensor.matmul(bank[b][:, at:at + tokens.stop - tokens.start], w[:, k, cols],
                                            src[:, k, tokens], start=k == 0, stop=k == k_tiles - 1)
                return last

            def tile_transposes(step, src, n):
                for k in range(n):
                    if k % 4 == 0:
                        b = fill(step)
                    last = nc.tensor.transpose(bank[b][:, (k % 4) * P:(k % 4 + 1) * P], src[:, k * P:(k + 1) * P], ident)
                    if k % 4 == 3 or k == n - 1:
                        last.then_inc(bank_filled[b], 1)

            def natural(step, src, tokens, w, cols, k_tiles, n):
                b = fill(step)
                for k in range(k_tiles):
                    last = nc.tensor.matmul(bank[b][:, 0:n], src[:, k, tokens], w[:, k, cols], start=k == 0, stop=k == k_tiles - 1)
                last.then_inc(bank_filled[b], 1)

            def kxn(w, k_tiles, n):
                return w[:, 0:k_tiles * n].rearrange("p (k n) -> p k n", k=k_tiles)

            def attention(kind, t, i):
                key_blocks = t + 1
                n_heads = 4 // key_blocks
                units = ATT[kind, t]
                first, first_out = unit0(kind, t)
                tok = slice(t * P, (t + 1) * P)
                W = key_blocks * P
                per_branch = HEADS // n_heads

                def operands(u, r):
                    hh = (u % per_branch) * n_heads + r
                    if kind == "m":
                        return mlaqT(t)[:, hh, :], kT[:, hh, 0:W], lambda kb: vM[:, kb, hh * HD:(hh + 1) * HD]
                    g, br = hh // 4, u // per_branch
                    p0 = g % 2 * HD
                    return (qT[p0:p0 + HD, g // 2 * 4 + hh % 4, tok], kswT[p0:p0 + HD, br, g // 2, 0:W],
                            lambda kb: vsw[:, kb, br * 256 + g * HD:br * 256 + (g + 1) * HD])

                if i + 1 < units:
                    b = fill((kind, t, "scores", i + 1))
                    for r in range(n_heads):
                        q, k, _ = operands(i + 1, r)
                        last = nc.tensor.matmul(bank[b][:, r * W:(r + 1) * W], q, k, start=True, stop=True)
                    last.then_inc(bank_filled[b], 1)
                if 0 <= i < units:
                    b = fill((kind, t, "probsT", i))
                    pe.wait_ge(probs_ready, first + i + 1)
                    for c in range(4):
                        last = nc.tensor.transpose(bank[b][:, c * P:(c + 1) * P], probs[:, (first + i) % 2, c * P:(c + 1) * P], ident)
                    last.then_inc(bank_filled[b], 1)
                if i >= 1:
                    u = i - 1
                    per_fill = 8 // n_heads
                    if u % per_fill == 0 and first_out + u // per_fill:
                        pe.wait_ge(heads_drained, first_out + u // per_fill)
                    drained((kind, t, "probsT", u))
                    for r in range(n_heads):
                        at = (u % per_fill * n_heads + r) * HD
                        v = operands(u, r)[2]
                        for kb in range(key_blocks):
                            last = nc.tensor.matmul(heads_out[:, at:at + HD], probsT[:, (first + u) % 2, r * key_blocks + kb, :],
                                                    v(kb), start=kb == 0, stop=kb == key_blocks - 1)
                    if u % per_fill == per_fill - 1:
                        last.then_inc(heads_filled, 1)

            def mixed_transposes(kind, t):
                pe.wait_ge(mixed_ready, t + 1 if kind == "n" else TILES + t + 1)
                tile_transposes((kind, t, "o"), mixed, KD)

            def output(kind, t, half):
                if half == 0:
                    drained((kind, t, "o"))
                w = chunk(0 if kind == "n" else 1, ("wo" if kind == "n" else "mo") + str(half))
                natural((kind, t, "w", half), mixedT, slice(0, P), kxn(w, KD, 512), slice(0, 512), KD, 512)
                release()

            def h_transposes(step, t, count):
                pe.wait_ge(ln_done, count)
                tile_transposes(step, h[:, t, :], KD)

            def peer_scores(layer, t, c):
                tok = slice(t * P, (t + 1) * P)
                if c < PH:
                    if c == 0:
                        drained(("n" if layer == 0 else "m", t, "h"))
                    w = chunk(layer, f"pq{c}")
                    chunks[layer, t, c] = w
                    b = fill((layer, t, "query", c))
                    for i in range(2):
                        last = transposed_projection(kxn(w, KD, 256), slice(i * P, (i + 1) * P), hT, b, i * P, KD, tok)
                    last.then_inc(bank_filled[b], 1)
                if c:
                    w = chunks[layer, t, c - 1]
                    b = fill((layer, t, "keyscore", c - 1))
                    drained((layer, t, "query", c - 1))
                    for i in range(2):
                        last = nc.tensor.matmul(bank[b][:, i * NKEYS:(i + 1) * NKEYS], pqT[:, (c - 1) % 2, i, :],
                                                w[:, KD * 256 + i * NKEYS:KD * 256 + (i + 1) * NKEYS], start=True, stop=True)
                    last.then_inc(bank_filled[b], 1)
                    release()

            def cmp_scores(t):
                for e in range(2):
                    b = fill(("n", t, "cs"))
                    p0 = e * HD
                    for j in range(8):
                        last = nc.tensor.matmul(bank[b][:, j * NCMP:(j + 1) * NCMP], qT[p0:p0 + HD, j, t * P:(t + 1) * P],
                                                kcT[p0:p0 + HD, j // 4, :], start=True, stop=True)
                    last.then_inc(bank_filled[b], 1)

            def cmp_transposes(t):
                b = fill(("n", t, "ct"))
                pe.wait_ge(cmp_probs, t + 1)
                for g in range(GROUPS):
                    last = nc.tensor.transpose(bank[b][:, g * P:(g + 1) * P],
                                               pc[:, 4 * g:4 * g + 4, :].rearrange("p h n -> p (h n)"), ident)
                last.then_inc(bank_filled[b], 1)

            def cmp_values(t):
                drained(("n", t, "ct"))
                for half in range(2):
                    b = fill(("n", t, "cv"))
                    for i in range(2):
                        g = 2 * half + i
                        last = nc.tensor.matmul(bank[b][:, i * 256:(i + 1) * 256], pcT[:, g, :],
                                                vblk[:, g, :, :].rearrange("p j d -> p (j d)"), start=True, stop=True)
                    last.then_inc(bank_filled[b], 1)

            def latent_kv(t):
                drained(("m", t, "h0"))
                n = KV_LORA + ROPE
                natural(("m", t, "dkv"), hT, slice(t * P, (t + 1) * P), kxn(chunk(1, "dkv"), KD, n), slice(0, n), KD, n)
                release()

            def latent_q(t, half):
                natural(("m", t, "dq", half), hT, slice(t * P, (t + 1) * P), kxn(chunk(1, f"dq{half}"), KD, 384),
                        slice(0, 384), KD, 384)
                release()

            def latent_kv_transposes(t):
                b = fill(("m", t, "lt"))
                pe.wait_ge(latent_ready, 2 * t + 1)
                for k in range(2):
                    nc.tensor.transpose(bank[b][:, k * P:(k + 1) * P], ckv[:, k * P:(k + 1) * P], ident)
                nc.tensor.transpose(bank[b][0:QK, 2 * P:3 * P], ropeT[:], ident).then_inc(bank_filled[b], 1)

            def keys(t):
                drained(("m", t, "lt"))
                w = kxn(chunk(1, "uk"), 2, D)
                for n in range(2):
                    b = fill(("m", t, "uk"))
                    for i in range(4):
                        last = transposed_projection(w, slice((4 * n + i) * P, (4 * n + i + 1) * P), ckvT, b, i * P, 2, slice(0, P))
                    last.then_inc(bank_filled[b], 1)
                release()

            def values(t):
                w = kxn(chunk(1, "uv"), 2, D)
                for n in range(2):
                    natural(("m", t, "uv"), ckvT, slice(0, P), w, slice(n * 512, (n + 1) * 512), 2, 512)
                release()

            def latent_q_transposes(t):
                pe.wait_ge(latent_ready, 2 * t + 2)
                tile_transposes(("m", t, "ct"), cq, 6)

            def queries(t, n):
                if n == 0:
                    drained(("m", t, "ct"))
                natural(("m", t, "uq", n), cqT, slice(0, P), kxn(chunk(1, f"uq{n}"), 6, 512), slice(0, 512), 6, 512)
                release()

            def query_transposes(t, half):
                pe.wait_ge(q_rotated, t + 1)
                for n in range(2):
                    b = fill(("m", t, "qt", half))
                    for i in range(4):
                        hh = 8 * half + 4 * n + i
                        last = nc.tensor.transpose(bank[b][0:QK, i * P:(i + 1) * P], q_nat[:, hh * QK:(hh + 1) * QK], ident)
                    last.then_inc(bank_filled[b], 1)

            def run(step):
                a, t, what, *n = step
                if what == "pq":
                    peer_scores(a, t, *n)
                elif what == "att":
                    if a == "m" and n == [-1]:
                        drained((a, t, "qt", 0))
                        drained((a, t, "qt", 1))
                    attention(a, t, *n)
                elif what == "h0":
                    h_transposes(step, t, peer_ln(t))
                elif what == "h":
                    h_transposes(step, t, t + 1 if a == "n" else mla_ln(t))
                elif what == "o":
                    mixed_transposes(a, t)
                elif what == "w":
                    output(a, t, *n)
                elif what != "ln":
                    {"cs": cmp_scores, "ct": cmp_transposes if a == "n" else latent_q_transposes, "cv": cmp_values,
                     "dkv": latent_kv, "dq": latent_q, "lt": latent_kv_transposes, "uk": keys, "uv": values,
                     "uq": queries, "qt": query_transposes}[what](t, *n)

            both = slice(0, SEQ)

            def block_pairs(step, w):
                for n in range(2):
                    b = fill(step)
                    for i in range(2):
                        last = transposed_projection(w, slice((2 * n + i) * P, (2 * n + i + 1) * P), hT, b, i * SEQ, KD, both)
                    last.then_inc(bank_filled[b], 1)
                release()

            pe.wait_ge(xT_loaded, 16)
            pe.wait_ge(const_loaded, 16)
            block_pairs("kvc", kxn(chunk(0, "kvc"), KD, 512))
            for v in range(2):
                w = kxn(chunk(0, ("ck1", "cv1")[v]), 16, P)
                b = fill("hidden")
                for l in range(16):
                    nc.tensor.matmul(bank[b][:, 64:65], w[:, l, :], pe_cols[:, v, l:l + 1], start=l == 0, stop=l == 15)
                if v == 0:
                    drained("kvc")
                rows = kc2[:, v, :, :].rearrange("p g (n l) -> p g n l", l=8)
                for l in range(16):
                    last = nc.tensor.matmul(bank[b][:, 0:GROUPS * (NCMP - 1)], w[:, l, :],
                                            rows[:, :, l // 8:l // 8 + NCMP - 1, l % 8], start=l == 0, stop=l == 15)
                last.then_inc(bank_filled[b], 1)
                release()
            block_pairs("ksw", kxn(chunk(0, "ksw"), KD, 512))
            b = fill("kcT")
            drained("hidden")
            for par in range(2):
                last = nc.tensor.matmul(bank[b][par * HD:(par + 1) * HD, 0:2 * NCMP], w2k,
                                        hk.rearrange("p (a e) n -> p e a n", e=2)[:, par, :, :], start=True, stop=True)
            last.then_inc(bank_filled[b], 1)
            b = fill("vblk")
            for g in range(GROUPS):
                last = nc.tensor.matmul(bank[b][:, g * HD:(g + 1) * HD], hv[:, g, :, :].rearrange("p j n -> p (j n)"), w2v,
                                        start=True, stop=True)
            last.then_inc(bank_filled[b], 1)
            for n in range(2):
                block_pairs(("q", n), kxn(chunk(0, f"q{n}"), KD, 512))
            w = kxn(chunk(0, "vsw"), KD, 512)
            for t in range(TILES):
                natural("vsw", hT, slice(t * P, (t + 1) * P), w, slice(0, 512), KD, 512)
            release()
            w = kxn(chunk(0, "gate"), KD, 48)
            for t in range(TILES):
                natural("gate", hT, slice(t * P, (t + 1) * P), w, slice(0, 48), KD, 48)
            release()
            for done in ("ksw", "kcT", "vblk", ("q", 0), ("q", 1), "vsw"):
                drained(done)
            for step in PROLOGUE:
                run(step)

            def burst(step0, first=False, i=None):
                for k in range(BURST if i is None else SLOTS):
                    pe.wait_ge(diag_ready, step0 + k + 1 if i is None else i * SLOTS + (step0 + k + 1))
                    for half in range(2):
                        last = nc.tensor.matmul(acc[:, half * 512:(half + 1) * 512], diag[:, k % BURST, :],
                                                ring[:, (step0 + k) % SLOTS, D + half * 512:D + (half + 1) * 512],
                                                start=first and k == 0, stop=False, skip_group_check=True)
                    last.then_inc(slot_free, 1)

            pe.sem_inc(slot_free, SLOTS)
            for phase in range(2 * TILES):
                slots = phase_slots(phase)
                if phase:
                    pe.wait_ge(acc_read, phase)
                for head in range(PH):
                    step0 = (phase * PH + head) * TOPK
                    if head and not any(slots[head * BURSTS:(head + 1) * BURSTS]):
                        with pe.Fori(0, TOPK // SLOTS, 1) as i:
                            burst(step0, i=i)
                        continue
                    for k in range(BURSTS):
                        for step in slots[head * BURSTS + k]:
                            run(step)
                        burst(step0 + k * BURST, first=head + k == 0)

        @block.sync
        def _(sp):
            sp.dma_start(hT[:], xT).then_inc(xT_loaded, 16)
            for n, name in enumerate(chunk_order):
                off, width = places[name]
                if n >= WSLOTS:
                    b, use = chunk_end[n - WSLOTS]
                    sp.wait_ge(bank_filled[b], use + 1)
                src = weights[off:off + P * width].rearrange("(p w) -> p w", p=P)
                sp.dma_start(wring[:, n % WSLOTS, 0:width], src).then_inc(w_loaded[n % WSLOTS], 16)
            for t in range(TILES):
                sp.wait_ge(ln_done, peer_ln(2 + t))
                sp.dma_start(out[t * P:(t + 1) * P, :], h[:, t, :]).then_inc(out_stored, 16)
            sp.wait_ge(out_stored, 16 * TILES)

        @block.gpsimd
        def _(pool):
            for ap in (ropeT[:], kcT, vblk, hk, hv):
                nc.gpsimd.memset(ap, 0.0)
            nc.gpsimd.memset(pc, 0.0).then_inc(zeroed, 1)
            for layer, table in enumerate((experts0, experts1)):
                with pool.Fori(0, TILES * PH // 2, 1) as i:
                    for half in range(2):
                        item = 2 * i + (layer * TILES * PH + half)
                        for s in range(TOPK):
                            if s == 0:
                                pool.wait_ge(ids_ready, item + 1)
                            pool.wait_ge(slot_free, item * TOPK + (s + 1))
                            pool.sem_inc(gathers_issued, 1)
                            nc.gpsimd.indirect_dma_start(
                                out=ring[:, s % SLOTS, :], out_offset=None, in_=table,
                                in_offset=bass.IndirectOffsetOnAxis(ap=expert_id[:, half, s:s + 1], axis=0),
                            ).then_inc(gathered[s % SLOTS], 16)

        @block.scalar
        def _(act):
            def full(step, n=0):
                b, use = place[step][n]
                act.wait_ge(bank_filled[b], use + 1)
                return b

            def drain(step, n, dst, width=512):
                b = full(step, n)
                nc.scalar.activation(dst, bank[b][:, 0:width], ACT.Copy).then_inc(bank_drained[b], 1)

            def load_ln(n):
                act.dma_start(lnp[:].rearrange("p a d -> p (a d)"),
                              ln_params[LN_ROW[n], :].partition_broadcast(P)).then_inc(ln_loaded, 16)

            def layer_norm_root(e):
                act.wait_ge(var_ready, e + 1)
                nc.scalar.activation(std, rstd, ACT.Sqrt).then_inc(std_ready, 1)
                if e + 1 < len(LN_LOAD) and LN_LOAD[e + 1] != LN_LOAD[e]:
                    act.wait_ge(ln_done, e + 1)
                    load_ln(LN_LOAD[e + 1])

            def rms_root(n):
                act.wait_ge(rms_ready, n)
                nc.scalar.activation(rms_std, rms_in, ACT.Sqrt).then_inc(rms_std_ready, 1)

            def attention(kind, t, i):
                u = i + 1
                if u >= ATT[kind, t]:
                    return
                W = (t + 1) * P
                n_heads = 4 // (t + 1)
                per_branch = HEADS // n_heads
                n = unit0(kind, t)[0] + u
                act.wait_ge(scores_ready, n + 1)
                for r in range(n_heads):
                    br = 1 + u // per_branch if kind == "n" else 0
                    hh = u % per_branch * n_heads + r
                    last = nc.scalar.activation(probs[:, n % 2, r * W:(r + 1) * W], S[:, n % 2, r * W:(r + 1) * W], ACT.Exp,
                                                bias=neg_max[:, n % 2 * 4 + r:n % 2 * 4 + r + 1],
                                                scale=NSA_SCALE if kind == "n" else MLA_SCALE, accum_out=row_sum[:, br, hh:hh + 1])
                last.then_inc(probs_ready, 1)

            def drain_tiles(step, n, dst):
                b = full(step, n)
                nc.scalar.activation(dst, bank[b][:].rearrange("p (k t) -> p k t", k=4), ACT.Copy).then_inc(bank_drained[b], 1)

            def peer_drains(layer, t, c):
                if c < PH:
                    b = full((layer, t, "query", c))
                    nc.scalar.activation(pqT[:, c % 2, :, :], bank[b][:, 0:2 * P].rearrange("p (i t) -> p i t", i=2),
                                         ACT.Copy).then_inc(bank_drained[b], 1)
                if c:
                    b = full((layer, t, "keyscore", c - 1))
                    nc.scalar.activation(keyscore[:, t, 2 * c - 2:2 * c, :], bank[b][:, 0:2 * NKEYS].rearrange("p (i k) -> p i k", i=2),
                                         ACT.Copy).then_inc(bank_drained[b], 1)

            def latent_kv(t):
                drain(("m", t, "dkv"), 0, ckv, KV_LORA + ROPE)
                rms_root(2 * t + 1)

            def latent_q(t, half):
                drain(("m", t, "dq", half), 0, cq[:, half * 384:(half + 1) * 384], 384)
                if half:
                    rms_root(2 * t + 2)

            def latent_kv_transposes(t):
                b = full(("m", t, "lt"))
                for k in range(2):
                    nc.scalar.activation(ckvT[:, k, :], bank[b][:, k * P:(k + 1) * P], ACT.Copy, scale=kv_gain[:, k:k + 1])
                nc.scalar.activation(kT[HD:QK, :, t * P:(t + 1) * P], spread(bank[b][HD:QK, 2 * P:3 * P], 1, HEADS),
                                     ACT.Copy).then_inc(bank_drained[b], 1)

            def keys(t):
                for n in range(2):
                    b = full(("m", t, "uk"), n)
                    src = bank[b][:].rearrange("p (i s) -> p i s", i=4)
                    dst = kT[0:HD, 8 * n:8 * n + 8, t * P:(t + 1) * P].rearrange("p (i e) s -> p e i s", e=2)
                    for e in range(2):
                        last = nc.scalar.activation(dst[:, e, :, :], src[e * HD:(e + 1) * HD, :, :], ACT.Copy)
                    last.then_inc(bank_drained[b], 1)

            def values(t):
                for n in range(2):
                    drain(("m", t, "uv"), n, vM[:, t, n * 512:(n + 1) * 512])

            def latent_q_transposes(t):
                for n, w in ((0, 4), (1, 2)):
                    b = full(("m", t, "ct"), n)
                    for k in range(w):
                        last = nc.scalar.activation(cqT[:, 4 * n + k, :], bank[b][:, k * P:(k + 1) * P], ACT.Copy,
                                                    scale=q_gain[:, 4 * n + k:4 * n + k + 1])
                    last.then_inc(bank_drained[b], 1)

            def queries(t, n):
                drain(("m", t, "uq", n), 0, q_nat[:, n * 512:(n + 1) * 512])

            def query_transposes(t, half):
                for n in range(2):
                    b = full(("m", t, "qt", half), n)
                    at = 8 * half + 4 * n
                    nc.scalar.activation(mlaqT(t)[:, at:at + 4, :].rearrange("p h t -> p (h t)"), bank[b][0:QK, :],
                                         ACT.Copy).then_inc(bank_drained[b], 1)

            def cmp_exps(t):
                act.wait_ge(cmp_ready, t + 1)
                nc.scalar.activation(sc_exp, sc_raw, ACT.Exp, scale=NSA_SCALE).then_inc(cmp_exp, 1)

            def run(step):
                a, t, what, *n = step
                if what == "pq":
                    peer_drains(a, t, *n)
                elif what == "att":
                    attention(a, t, *n)
                elif what in ("h", "h0"):
                    for i in range(2):
                        drain_tiles(step, i, hT[:, 4 * i:4 * i + 4, t * P:(t + 1) * P])
                elif what == "o":
                    for i in range(2):
                        drain_tiles(step, i, mixedT[:, 4 * i:4 * i + 4, :])
                elif what == "w":
                    if n == [1]:
                        layer_norm_root(t if a == "n" else mla_ln(t) - 1)
                elif what == "ln":
                    layer_norm_root(peer_ln(*n) - 1)
                elif what == "cs":
                    cmp_exps(t)
                elif a == "m":
                    {"ct": latent_q_transposes, "dkv": latent_kv, "dq": latent_q, "lt": latent_kv_transposes, "uk": keys,
                     "uv": values, "uq": queries, "qt": query_transposes}[what](t, *n)

            act.dma_start(cst[:], consts).then_inc(const_loaded, 16)
            act.dma_start(cmp_bias.rearrange("p t h n -> p (t h n)"), cmp_table).then_inc(cmp_bias_loaded, 16)
            act.dma_start(alibi_sb.rearrange("p o s -> p (o s)"), alibi).then_inc(alibi_loaded, 16)
            act.dma_start(h[:], x.rearrange("(t p) d -> p t d", p=P)).then_inc(x_loaded, 16)
            load_ln(0)

            for v in range(2):
                b = full("kvc", v)
                src = bank[b][:].rearrange("p (a u par) -> p a u par", a=2, par=2)
                dst = kc2[:, v, :, :].rearrange("p (a e) u -> p e a u", e=2)
                for e in range(2):
                    for par in range(2):
                        last = nc.scalar.activation(dst[par * HD:(par + 1) * HD, e, :, :],
                                                    src[e * HD:(e + 1) * HD, :, :, par], ACT.Copy)
                last.then_inc(bank_drained[b], 1)
            act.wait_ge(zeroed, 1)
            for v in range(2):
                b = full("hidden", v)
                nc.scalar.activation(pe_bias[:, v:v + 1], bank[b][:, 64:65], ACT.Copy).then_inc(pe_done, 1)
                act.wait_ge(pe_done, v + 1)
                src = bank[b][:, 0:GROUPS * (NCMP - 1)].rearrange("p (g n) -> p g n", g=GROUPS)
                for j in range(1 if v == 0 else 4):
                    dst = hk[:, :, 0:NCMP - 1] if v == 0 else hv[:, :, j, 0:NCMP - 1]
                    last = nc.scalar.activation(dst, src, ACT.Gelu_apprx_tanh, bias=pe_bias[:, v:v + 1])
                last.then_inc(bank_drained[b], 1)
            for br in range(2):
                drain("ksw", br, kswT[:, br, :, :].rearrange("p a t -> p (a t)"))
            drain("kcT", 0, kcT.rearrange("p a n -> p (a n)"), 2 * NCMP)
            b = full("vblk")
            for j in range(4):
                q = slice(32 * j, 32 * j + 32)
                last = nc.scalar.activation(vblk[q, :, j, :], bank[b][q, 0:GROUPS * HD].rearrange("p (g d) -> p g d", g=GROUPS),
                                            ACT.Copy)
            last.then_inc(bank_drained[b], 1)
            for n in range(2):
                for i in range(2):
                    b = full(("q", n), i)
                    for r in range(2):
                        j = 4 * n + 2 * i + r
                        last = nc.scalar.activation(qT[:, j, :], bank[b][:, r * SEQ:(r + 1) * SEQ], ACT.Copy, scale=q_up[:, j:j + 1])
                    last.then_inc(bank_drained[b], 1)
            for t in range(TILES):
                drain("vsw", t, vsw[:, t, :])
            for t in range(TILES):
                b = full("gate", t)
                nc.scalar.activation(gates[:, t, :, :].rearrange("p b h -> p (b h)"), bank[b][:, 0:3 * HEADS], ACT.Exp,
                                     scale=-1.0).then_inc(bank_drained[b], 1)
            for step in PROLOGUE:
                run(step)

            def gate_exps(item):
                act.wait_ge(gate_in_ready, item + 1)
                nc.scalar.activation(gate_e[:, item % 2, :], gate_in[:, item % 2, :], ACT.Exp,
                                     accum_out=gate_sum[:, item % 2:item % 2 + 1]).then_inc(gate_e_ready, 1)

            def burst(step0, i=None):
                for k in range(BURST if i is None else SLOTS):
                    s = (step0 + k) % SLOTS
                    act.wait_ge(dot_ready, step0 + k + 1 if i is None else i * SLOTS + (step0 + k + 1))
                    nc.scalar.activation(gelu[:, s:s + 1], dots[:, s:s + 1], ACT.Gelu_apprx_tanh).then_inc(gelu_ready, 1)

            gate_exps(0)
            for phase in range(2 * TILES):
                slots = phase_slots(phase)
                if phase:
                    act.wait_ge(dot_ready, phase * PH * TOPK)
                act.wait_ge(ln_done, [1, 2, mla_ln(0), mla_ln(1)][phase])
                for half in range(2):
                    last = nc.scalar.activation(xdup[:, half * 512:(half + 1) * 512], h[:, phase % TILES, half * 512:(half + 1) * 512], ACT.Copy)
                last.then_inc(xdup_ready, 1)
                for head in range(PH):
                    item = phase * PH + head
                    step0 = item * TOPK
                    if head and not any(slots[head * BURSTS:(head + 1) * BURSTS]):
                        if item + 1 < ITEMS:
                            gate_exps(item + 1)
                        with act.Fori(0, TOPK // SLOTS, 1) as i:
                            burst(step0, i)
                        continue
                    for k in range(BURSTS):
                        burst(step0 + k * BURST)
                        for step in slots[head * BURSTS + k]:
                            run(step)
                        if k == 0 and item + 1 < ITEMS:
                            gate_exps(item + 1)
            layer_norm_root(peer_ln(2 * TILES - 1) - 1)

        @block.vector
        def _(dve):
            chain = [0]

            def link(ins):
                chain[0] += 1
                ins.then_inc(dve_chain, 1)
                dve.wait_ge(dve_chain, chain[0])

            def full(step, n=0):
                b, use = place[step][n]
                dve.wait_ge(bank_filled[b], use + 1)
                return b

            def drained(step):
                for b, use in place[step]:
                    dve.wait_ge(bank_drained[b], use + 1)

            def attention(kind, t, i):
                units = ATT[kind, t]
                first, first_out = unit0(kind, t)
                key_blocks = t + 1
                W = key_blocks * P
                lo = 2 * P - W
                n_heads = 4 // key_blocks
                per_branch = HEADS // n_heads
                if i + 1 < units:
                    u = i + 1
                    n = first + u
                    b = full((kind, t, "scores", u))
                    slot = slice(n % 2 * 4, n % 2 * 4 + n_heads)
                    for r in range(n_heads):
                        hh = u % per_branch * n_heads + r
                        table = alibi_sb[:, (hh + 1) % 2, :] if kind == "n" else causal
                        last = nc.vector.tensor_tensor_reduce(
                            out=S[:, n % 2, r * W:(r + 1) * W], in0=bank[b][:, r * W:(r + 1) * W], in1=table[:, lo:2 * P],
                            scale=2.0 ** -((hh + 1) // 2) if kind == "n" else 1.0, scalar=LOWEST, op0=ALU.add, op1=ALU.max,
                            accum_out=row_max[:, slot.start + r:slot.start + r + 1])
                    last.then_inc(bank_drained[b], 1)
                    drained((kind, t, "scores", u))
                    nc.vector.tensor_scalar(neg_max[:, slot], row_max[:, slot], -(NSA_SCALE if kind == "n" else MLA_SCALE), None,
                                            ALU.mult).then_inc(scores_ready, 1)
                if 0 <= i < units:
                    b = full((kind, t, "probsT", i))
                    nc.vector.tensor_copy(probsT[:, (first + i) % 2, :, :].rearrange("p b t -> p (b t)"),
                                          bank[b][:]).then_inc(bank_drained[b], 1)
                per_fill = 8 // n_heads
                if i >= 1 and (i - 1) % per_fill == per_fill - 1:
                    u = i - 1
                    n = first_out + u // per_fill + 1
                    h0 = u % per_branch // per_fill * 8
                    hs = slice(h0, h0 + 8)
                    mix = mixed.rearrange("p (h d) -> p h d", h=HEADS)[:, hs, :]
                    out8 = heads_out[:].rearrange("p (h d) -> p h d", h=8)
                    dve.wait_ge(heads_filled, n)
                    if kind == "n":
                        br = 1 + u // per_branch
                        coefficients(t, br, hs)
                        tmp = onehot[:].rearrange("p a b -> p (a b)")[:, 0:512].rearrange("p (h d) -> p h d", h=8)
                        nc.vector.tensor_tensor(tmp, out8, spread(coef[:, br, hs], 2, HD), ALU.mult).then_inc(heads_drained, 1)
                        dve.wait_ge(heads_drained, n)
                        ins = nc.vector.tensor_tensor(mix, mix, tmp, ALU.add)
                        if u == units - 1:
                            ins.then_inc(mixed_ready, 1)
                        else:
                            link(ins)
                    else:
                        link(nc.vector.reciprocal(coef[:, 0, hs], row_sum[:, 0, hs]))
                        nc.vector.tensor_tensor(mix, out8, spread(coef[:, 0, hs], 2, HD), ALU.mult).then_inc(heads_drained, 1)
                        if u == units - 1:
                            dve.wait_ge(heads_drained, n)
                            dve.sem_inc(mixed_ready, 1)

            def coefficients(t, br, hs):
                link(nc.vector.tensor_tensor(denom[:, br, hs], gates[:, t, br, hs], row_sum[:, br, hs], ALU.mult))
                link(nc.vector.reciprocal(coef[:, br, hs], denom[:, br, hs]))

            def residual(t, half, src):
                y = h[:, t, half * 512:(half + 1) * 512]
                return nc.vector.scalar_tensor_tensor(out=y, in0=y, scalar=ALPHA, in1=src, op0=ALU.mult, op1=ALU.add)

            def normalize(e, t):
                y = h[:, t, :]
                for half in range(2):
                    ins = nc.vector.bn_stats(stat[:, half, :], y[:, half * 512:(half + 1) * 512])
                link(ins)
                link(nc.vector.bn_aggr(moments, stat))
                nc.vector.tensor_scalar(rstd, moments[:, 1:2], LN_EPS, None, ALU.add).then_inc(var_ready, 1)
                dve.wait_ge(std_ready, e + 1)
                link(nc.vector.reciprocal(rstd, std))
                link(nc.vector.tensor_scalar(y, y, moments[:, 0:1], rstd, ALU.subtract, ALU.mult))
                dve.wait_ge(ln_loaded, 16 * (LN_LOAD[e] + 1))
                link(nc.vector.tensor_tensor(y, y, lnp[:, 0, :], ALU.mult))
                nc.vector.tensor_tensor(y, y, lnp[:, 1, :], ALU.add).then_inc(ln_done, 1)

            def output(kind, t, half):
                b = full((kind, t, "w", half))
                residual(t, half, bank[b][:]).then_inc(bank_drained[b], 1)
                if half:
                    drained((kind, t, "w", 1))
                    normalize(t if kind == "n" else mla_ln(t) - 1, t)

            def cmp_softmax(t):
                for e in range(2):
                    b = full(("n", t, "cs"), e)
                    src = bank[b][:, 0:8 * NCMP].rearrange("p (a x) -> p a x", a=2)
                    dst = sc_raw.rearrange("p (a e r) n -> p e a (r n)", e=2, r=4)[:, e, :, :]
                    add = cmp_bias[:, t, :, :].rearrange("p (a e r) n -> p e a (r n)", e=2, r=4)[:, e, :, :]
                    nc.vector.tensor_tensor(dst, src, add, ALU.add).then_inc(bank_drained[b], 1)
                drained(("n", t, "cs"))
                link(nc.vector.tensor_tensor(sc_raw, sc_raw, spread(down, 2, NCMP), ALU.mult))
                link(nc.vector.reduce_max(cmp_max, sc_raw, AX.X))
                nc.vector.tensor_tensor(sc_raw, sc_raw, spread(cmp_max, 2, NCMP), ALU.subtract).then_inc(cmp_ready, 1)
                dve.wait_ge(cmp_exp, t + 1)
                nc.vector.reduce_sum(row_sum[:, 0, :], sc_exp, AX.X)
                nc.vector.tensor_tensor(pc[:, :, 0:NCMP], sc_exp, spread(cmp_mask[:, t, :], 1, HEADS), ALU.mult).then_inc(cmp_probs, 1)

            def cmp_drain(t):
                b = full(("n", t, "ct"))
                nc.vector.tensor_copy(pcT.rearrange("p g t -> p (g t)"), bank[b][:]).then_inc(bank_drained[b], 1)

            def cmp_output(t):
                coefficients(t, 0, slice(0, HEADS))
                for half in range(2):
                    b = full(("n", t, "cv"), half)
                    hs = slice(8 * half, 8 * half + 8)
                    nc.vector.tensor_tensor(mixed.rearrange("p (h d) -> p h d", h=HEADS)[:, hs, :],
                                            bank[b][:].rearrange("p (h d) -> p h d", h=8), spread(coef[:, 0, hs], 2, HD),
                                            ALU.mult).then_inc(bank_drained[b], 1)
                drained(("n", t, "cv"))

            def rms(n, data, width):
                link(nc.vector.tensor_tensor_reduce(out=rope_tmp[:, 0:width], in0=data, in1=data, scale=1.0, scalar=0.0,
                                                    op0=ALU.mult, op1=ALU.add, accum_out=rms_r))
                nc.vector.tensor_scalar(rms_in, rms_r, 1.0 / width, RMS_EPS, ALU.mult, ALU.add).then_inc(rms_ready, 1)
                dve.wait_ge(rms_std_ready, n)
                link(nc.vector.reciprocal(rms_r, rms_std))
                link(nc.vector.tensor_scalar(data, data, rms_r, None, ALU.mult))

            def rotate(x1, x2, y1, y2, tmp, cosb, sinb):
                nc.vector.tensor_tensor(tmp[0], x1, cosb, ALU.mult)
                nc.vector.tensor_tensor(tmp[1], x2, sinb, ALU.mult)
                nc.vector.tensor_tensor(tmp[2], x2, cosb, ALU.mult)
                link(nc.vector.tensor_tensor(tmp[3], x1, sinb, ALU.mult))
                nc.vector.tensor_tensor(y1, tmp[0], tmp[1], ALU.subtract)
                return nc.vector.tensor_tensor(y2, tmp[2], tmp[3], ALU.add)

            def latent_kv(t):
                drained(("m", t, "dkv"))
                rms(2 * t + 1, ckv[:, 0:KV_LORA], KV_LORA)
                rotate(ckv[:, KV_LORA:KV_LORA + HALF], ckv[:, KV_LORA + HALF:KV_LORA + ROPE], ropeT[:, HD:HD + HALF],
                       ropeT[:, HD + HALF:QK], [kr_tmp[:, i, :] for i in range(4)], rope[:, t, 0, :], rope[:, t, 1, :]
                       ).then_inc(latent_ready, 1)

            def latent_q(t, half):
                drained(("m", t, "dq", half))
                if half:
                    rms(2 * t + 2, cq, Q_LORA)
                    dve.sem_inc(latent_ready, 1)

            def queries(t, n):
                drained(("m", t, "uq", n))
                if n == 2:
                    q3 = q_nat.rearrange("p (h e) -> p h e", h=HEADS)
                    x1, x2 = q3[:, :, HD:HD + HALF], q3[:, :, HD + HALF:QK]
                    tmp = [rope_tmp[:, i * 256:(i + 1) * 256].rearrange("p (h k) -> p h k", h=HEADS) for i in range(4)]
                    rotate(x1, x2, x1, x2, tmp, spread(rope[:, t, 0, :], 1, HEADS), spread(rope[:, t, 1, :], 1, HEADS)
                           ).then_inc(q_rotated, 1)

            def run(step):
                a, t, what, *n = step
                if what == "att":
                    attention(a, t, *n)
                elif what == "w":
                    output(a, t, *n)
                elif what == "ln":
                    normalize(peer_ln(*n) - 1, t)
                elif a == "n" and what in ("cs", "ct", "cv"):
                    {"cs": cmp_softmax, "ct": cmp_drain, "cv": cmp_output}[what](t)
                elif what in ("dkv", "dq", "uq"):
                    {"dkv": latent_kv, "dq": latent_q, "uq": queries}[what](t, *n)

            dve.wait_ge(const_loaded, 16)
            drained("gate")
            g = gates[:].rearrange("p t b h -> p (t b h)")
            link(nc.vector.tensor_scalar(g, g, 1.0, None, ALU.add))
            dve.wait_ge(alibi_loaded, 16)
            dve.wait_ge(cmp_bias_loaded, 16)
            dve.wait_ge(zeroed, 1)
            dve.wait_ge(x_loaded, 16)
            for step in PROLOGUE:
                run(step)

            def top_k(item):
                phase, head = divmod(item, PH)
                t = phase % TILES
                drained((phase // TILES, t, "keyscore", head))
                for c in range(2):
                    s = keyscore[:, t, 2 * head + c, :]
                    link(nc.vector.max(top_val[:, c, 0:8], s))
                    nc.vector.max_index(top_pos[:, c, 0:8], top_val[:, c, 0:8], s)
                    link(nc.vector.match_replace(work[:, c, :], top_val[:, c, 0:8], s, LOWEST))
                    link(nc.vector.max(top_val[:, c, 8:16], work[:, c, :]))
                    link(nc.vector.max_index(top_pos[:, c, 8:16], top_val[:, c, 8:16], work[:, c, :]))
                link(nc.vector.tensor_copy(top_idx[:], top_pos[:]))
                link(nc.vector.tensor_scalar(top_idx[:, 0, :], top_idx[:, 0, :], float(NKEYS), None, ALU.mult))
                for dst, src in ((cand[:, 0, :], top_val), (cand_idx[:], top_idx)):
                    for i in range(5):
                        nc.vector.tensor_scalar(dst[:, RUN_AT[i]:RUN_AT[i] + RUN[i]], src[:, 1, 0:RUN[i]], src[:, 0, i:i + 1], None, ALU.add)
                    nc.vector.tensor_tensor(dst[:, RUN_AT[5]:RUN_AT[8]].rearrange("p (i j) -> p i j", j=2),
                                            spread(src[:, 1, 0:2], 1, 3), spread(src[:, 0, 5:8], 2, 2), ALU.add)
                    link(nc.vector.tensor_scalar(dst[:, RUN_AT[8]:NCAND], src[:, 0, 8:16], src[:, 1, 0:1], None, ALU.add))
                link(nc.vector.max(best[:, 0:8], cand[:, 0, :]))
                nc.vector.max_index(best_pos[:, 0:8], best[:, 0:8], cand[:, 0, :])
                link(nc.vector.match_replace(cand[:, 1, :], best[:, 0:8], cand[:, 0, :], LOWEST))
                link(nc.vector.max(best[:, 8:16], cand[:, 1, :]))
                nc.vector.tensor_scalar(gate_in[:, item % 2, :], best[:], best[:, 0:1], None, ALU.subtract).then_inc(gate_in_ready, 1)
                link(nc.vector.max_index(best_pos[:, 8:16], best[:, 8:16], cand[:, 1, :]))
                link(nc.vector.tensor_copy(best_posf[:], best_pos[:]))
                link(nc.vector.tensor_tensor(onehot[:], spread(best_posf[:], 2, NCAND), spread(number, 1, TOPK), ALU.is_equal))
                link(nc.vector.tensor_tensor(onehot[:], onehot[:], spread(cand_idx[:], 1, TOPK), ALU.mult))
                link(nc.vector.reduce_sum(best_idx[:], onehot[:], AX.X))
                nc.vector.tensor_copy(expert_id[:, item % 2, :], best_idx[:]).then_inc(ids_ready, 1)

            def gate_weights(item):
                s = item % 2
                dve.wait_ge(gate_e_ready, item + 1)
                link(nc.vector.reciprocal(inv_sum[:, s:s + 1], gate_sum[:, s:s + 1]))
                link(nc.vector.tensor_scalar(gate_w[:, s, :], gate_e[:, s, :], inv_sum[:, s:s + 1], None, ALU.mult))

            def burst(item, at, i=None):
                step0 = item * TOPK + at
                rows = BURST if i is None else SLOTS

                def count(n):
                    return n if i is None else i * SLOTS + n

                for k in range(rows + 1):
                    if k < rows:
                        s = (step0 + k) % SLOTS
                        landed = 16 * ((step0 + k) // SLOTS + 1)
                        dve.wait_ge(gathered[s], landed if i is None else i * 16 + landed)
                        u_row = ring[:, s, 0:D]
                        nc.vector.tensor_tensor_reduce(out=u_row, in0=u_row, in1=xdup[:], scale=1.0, scalar=0.0, op0=ALU.mult,
                                                       op1=ALU.add, accum_out=dots[:, s:s + 1]).then_inc(dot_ready, 1)
                    if k:
                        j = k - 1
                        s = (step0 + j) % SLOTS
                        dve.wait_ge(gelu_ready, count(step0 + j + 1))
                        dve.wait_ge(slot_free, count(step0 + j + 1 + SLOTS - BURST))
                        gate = gate_w[:, item % 2, at + j:at + j + 1] if i is None else gate_w[:, item % 2, bass.ds(i * SLOTS + j, 1)]
                        nc.vector.tensor_scalar(diag[:, j % BURST, :], ident, gelu[:, s:s + 1], gate, ALU.mult,
                                                ALU.mult).then_inc(diag_ready, 1)

            top_k(0)
            for phase in range(2 * TILES):
                slots = phase_slots(phase)
                dve.wait_ge(xdup_ready, phase + 1)
                for head in range(PH):
                    item = phase * PH + head
                    gate_weights(item)
                    if head and not any(slots[head * BURSTS:(head + 1) * BURSTS]):
                        if item + 1 < ITEMS:
                            top_k(item + 1)
                        with dve.Fori(0, TOPK // SLOTS, 1) as i:
                            burst(item, 0, i)
                        continue
                    for k in range(BURSTS):
                        burst(item, k * BURST)
                        for step in slots[head * BURSTS + k]:
                            run(step)
                        if k == 0 and item + 1 < ITEMS:
                            top_k(item + 1)
                dve.wait_ge(slot_free, SLOTS + (phase + 1) * PH * TOPK)
                residual(phase % TILES, 0, acc[:, 0:512])
                residual(phase % TILES, 1, acc[:, 512:D]).then_inc(acc_read, 1)
                dve.wait_ge(acc_read, phase + 1)
            normalize(peer_ln(2 * TILES - 1) - 1, TILES - 1)


def _kxn(w):
    k, n = w.shape
    return w.reshape(k // P, P, n).transpose(1, 0, 2).reshape(P, -1)


def _constants():
    p = np.arange(P)
    out = {"ident": np.eye(P, dtype=np.float32)}
    dist = P + p[:, None] - np.arange(2 * P)[None, :]
    base = np.array([1.0, 2.0 ** -0.5], np.float32)
    shift = (np.arange(HEADS) + 1) // 2
    table = -(base[None, :, None] / np.float32(NSA_SCALE)) * dist[:, None, :].astype(np.float32)
    out["alibi"] = np.where(dist[:, None, :] >= 0, table, np.float32(MASKED)).astype(np.float32)
    out["down"] = np.broadcast_to(2.0 ** -shift, (P, HEADS)).astype(np.float32)
    head = (2 * np.arange(2)[None, :, None] + (p // HD)[:, None, None]) * 4 + np.arange(4)
    out["q_up"] = (2.0 ** shift[head]).astype(np.float32)
    out["causal"] = np.where(dist >= 0, 0.0, MASKED).astype(np.float32)
    t = np.arange(TILES)[None, :] * P + p[:, None]
    end = np.arange(NCMP) * CMP_STRIDE + CMP_LEN - 1
    dist_c = t[:, :, None] - end
    seen = (dist_c >= 0) & (np.arange(NCMP) < NCMP - 1)
    heads_base = base[(np.arange(HEADS) + 1) % 2]
    table = -(heads_base[None, None, :, None] / np.float32(NSA_SCALE)) * dist_c[:, :, None, :].astype(np.float32)
    out["cmp_table"] = np.where(seen[:, :, None, :], table, np.float32(MASKED)).astype(np.float32)
    out["cmp_mask"] = seen.astype(np.float32)
    inv = (1.0 / (np.float32(10000.0) ** (np.arange(0, ROPE, 2, dtype=np.float32) / np.float32(ROPE)))).astype(np.float32)
    ang = t.astype(np.float32)[:, :, None] * inv
    out["rope"] = np.stack([np.cos(ang), np.sin(ang)], 2).astype(np.float32)
    out["number"] = np.broadcast_to(np.arange(NCAND, dtype=np.float32), (P, NCAND))
    return {k: np.ascontiguousarray(v.reshape(P, -1)) for k, v in out.items()}


def _layout(a):
    w = a["nsa_w_in"][0]
    q = w[:, 0:1024].reshape(D, 2, 2, 4, HD)
    q = q.transpose(0, 1, 3, 2, 4).reshape(D, 1024)
    kc, vc, ks, vs, kw, vw = [w[:, 1024 + 256 * i:1280 + 256 * i] for i in range(6)]
    gate = w[:, 2560:2608].reshape(D, HEADS, 3).transpose(0, 2, 1).reshape(D, 48)
    cat = np.concatenate
    wo = a["nsa_w_out"][0]
    ch = {
        (0, "kvc"): _kxn(cat([kc, vc], 1)), (0, "ksw"): _kxn(cat([ks, kw], 1)),
        (0, "ck1"): _kxn(a["nsa_cmp_k_w1"][0]), (0, "cv1"): _kxn(a["nsa_cmp_v_w1"][0]),
        (0, "q0"): _kxn(q[:, 0:512]), (0, "q1"): _kxn(q[:, 512:1024]), (0, "vsw"): _kxn(cat([vs, vw], 1)),
        (0, "gate"): _kxn(gate), (0, "wo0"): _kxn(wo[:, 0:512]), (0, "wo1"): _kxn(wo[:, 512:1024]),
        (1, "dkv"): _kxn(cat([a["mla_w_dkv"], a["mla_w_kr"]], 1)),
        (1, "uk"): _kxn(a["mla_w_uk"].reshape(KV_LORA, 1024)), (1, "uv"): _kxn(a["mla_w_uv"].reshape(KV_LORA, 1024)),
    }
    dq, uq, mo = a["mla_w_dq"][0], a["mla_w_uq"][0].reshape(Q_LORA, HEADS * QK), a["mla_w_out"][0]
    for i in range(2):
        ch[1, f"dq{i}"] = _kxn(dq[:, i * 384:(i + 1) * 384])
        ch[1, f"mo{i}"] = _kxn(mo[:, i * 512:(i + 1) * 512])
    for i in range(3):
        ch[1, f"uq{i}"] = _kxn(uq[:, i * 512:(i + 1) * 512])
    for l in range(2):
        for c in range(PH):
            wq = _kxn(a["peer_w_q"][l][:, c * 256:(c + 1) * 256])
            keys = a["peer_subkeys"][l][c].transpose(2, 0, 1).reshape(P, 2 * NKEYS)
            ch[l, f"pq{c}"] = cat([wq, keys], 1)
    weights = cat([ch[l, n].reshape(-1) for l in range(2) for n, _ in LAYERS[l]])
    c = _constants()
    c["pe"] = cat([a[f"nsa_cmp_{n}_pe"][0].reshape(16, P).T for n in "kv"], 1)
    c["w2k"], c["w2v"] = a["nsa_cmp_k_w2"][0], a["nsa_cmp_v_w2"][0]
    c["q_gain"] = a["mla_q_norm_g"][0].reshape(6, P).T
    c["kv_gain"] = a["mla_kv_norm_g"].reshape(2, P).T
    xs = a["x"][0]
    ln = np.stack([cat([a["nsa_ln_g"][0], a["nsa_ln_b"][0]]), cat([a["mla_ln_g"][0], a["mla_ln_b"][0]]),
                   cat([a["peer_ln_g"][0], a["peer_ln_b"][0]]), cat([a["peer_ln_g"][1], a["peer_ln_b"][1]])])
    return {
        "x": xs, "xT": xs.T.reshape(KD, P, SEQ).transpose(1, 0, 2), "weights": weights,
        "consts": cat([c[n] for n in CONST], 1), "alibi": c["alibi"], "cmp_table": c["cmp_table"], "ln_params": ln,
        "experts0": cat([a["peer_u"][0], a["peer_v"][0]], 1), "experts1": cat([a["peer_u"][1], a["peer_v"][1]], 1),
    }


def kernel(**inputs):
    import concourse.bacc as bacc
    from concourse.bass_utils import run_bass_kernel_spmd

    arrays = {k: np.ascontiguousarray(v) for k, v in _layout({k: np.asarray(v) for k, v in inputs.items()}).items()}
    nc = bacc.Bacc("TRN2", target_bir_lowering=False, num_devices=1)
    args = [nc.dram_tensor(k, v.shape, mybir.dt.from_np(v.dtype), kind="ExternalInput").ap() for k, v in arrays.items()]
    out = nc.dram_tensor("out", (SEQ, D), F32, kind="ExternalOutput").ap()
    trunk_kernel(nc, *args, out)
    r = run_bass_kernel_spmd(nc, [arrays], core_ids=[0])
    return np.asarray(r.results[0]["out"]).reshape(1, SEQ, D)
```

```python
import concourse.bass as bass
import numpy as np
from concourse import mybir
from concourse.alu_op_type import AluOpType as ALU
from contextlib import ExitStack

F32 = mybir.dt.float32
U32 = mybir.dt.uint32
ACT = mybir.ActivationFunctionType
AX = mybir.AxisListType

P = 128
D = 1024
KD = D // P
SEQ = 256
TILES = SEQ // P
HEADS = 16
HD = 64
GROUPS = 4
CMP_STRIDE = 16
CMP_LEN = 32
NCMP = SEQ // CMP_STRIDE
NSA_SCALE = HD ** -0.5
ROPE = 32
HALF = ROPE // 2
QK = HD + ROPE
KV_LORA = 256
Q_LORA = 768
MLA_SCALE = QK ** -0.5
PH = 8
TOPK = 16
NKEYS = 128
ALPHA = 4.0 ** 0.25
LN_EPS = 1e-5
RMS_EPS = 1e-6
MASKED = -1.0e30
LOWEST = -3.0e38

RUN = [TOPK // (i + 1) for i in range(TOPK)]
RUN_AT = [sum(RUN[:i]) for i in range(TOPK)]
NCAND = sum(RUN)

SLOTS = 8
WSLOTS = 4
WCOLS = 3072

NSA_CHUNKS = [("gate", KD * 48), ("ksw", 4096), ("q0", 4096), ("vsw", 4096), ("kvc0", 2048), ("kvc1", 2048),
              ("q1", 4096), ("ck1", 2048), ("cv1", 2048)] + [(f"wo{n}{k}", 2048) for n in range(2) for k in range(2)]
PEER_W = KD * 256 + 2 * NKEYS
PEER_CHUNKS = [(f"pq{c}", PEER_W) for c in range(PH)]
MLA_CHUNKS = [("dkv", KD * (KV_LORA + ROPE)), ("uk", 2048), ("uv", 2048), ("dq0", KD * 384), ("dq1", KD * 384),
              ("uq0", 3072), ("uq1", 3072), ("uq2", 3072)] + [(f"mo{n}{k}", 2048) for n in range(2) for k in range(2)]
LAYERS = [NSA_CHUNKS + PEER_CHUNKS, MLA_CHUNKS + PEER_CHUNKS]




def chunk_places():
    at, off = {}, 0
    for l, chunks in enumerate(LAYERS):
        for name, width in chunks:
            at[l, name] = (off, width)
            off += width * P
    return at


BURST = 2
DIAGS = 4
BURSTS = TOPK // BURST
SLOTS_OF_PHASE = PH * BURSTS
ATT = {("n", 0): 8, ("n", 1): 16, ("m", 0): 4, ("m", 1): 8}


HELD = {"q0": 0, "q1": 2, "ksw": 4, "vsw": 6}


def att_steps(kind, t):
    units = ATT[kind, t]
    steps = [(kind, t, "att", u) for u in range(-1, units + 1)]
    if kind == "n":
        steps.insert(2 + 3 * units // 4, (kind, t, "cv"))
    return steps


def pq_steps(layer, t, heads):
    heads = list(heads)
    steps = []
    for n in range(len(heads) + 1):
        steps.append(([(layer, t, "query", heads[n])] if n < len(heads) else []) + ([(layer, t, "score", heads[n - 1])] if n else []))
    return steps


SHARED_HEAD = 6


def both_tiles(head):
    return head >= SHARED_HEAD


def phase_slots(phase):
    slots = [[] for _ in range(SLOTS_OF_PHASE)]
    others = [n for n in range(SLOTS_OF_PHASE) if n % BURSTS]

    def place_evenly(line, first, last):
        free = [n for n in others if first <= n <= last]
        for n, steps in enumerate(line):
            slots[free[n * len(free) // len(line)]] += steps

    layer, t = (phase + 1) // TILES, (phase + 1) % TILES
    if layer == 0:
        line = [[x] for x in [("n", t, "cs"), ("n", t, "ct")] + att_steps("n", t)]
        kind = "n"
    else:
        line = [[("p", t, "ln", t)], [("m", t, "h0")], [("m", t, "dkv")], [("m", t, "dq", 0)], [("m", t, "dq", 1)], [("m", t, "lt")],
                [("m", t, "uk")], [("m", t, "uv")], [("m", t, "ct")], [("p", 0, "lnp", 2 * t + 2)]]
        line += [[("m", t, "uq", n)] for n in range(3)]
        line += [[("m", t, "qt", n) for n in range(2)]]
        line += [[x] for x in att_steps("m", t)]
        kind = "m"
    line += [[(kind, t, "o")], [(kind, t, "w", 0)], [(kind, t, "w", 1)], [(kind, t, "h")]]
    ln_params = [("p", 0, "lnp", 1 if layer == 0 else 2 * t + 3)]
    first_heads = [[(layer, t, "query", 0)], ln_params, [(layer, t, "score", 0), (layer, t, "query", 1)], [(layer, t, "score", 1)]]
    shared_by = BURSTS * (SHARED_HEAD - 1) - 1
    if layer == 2:
        slots[1].append(("p", 0, "ln", phase - 1))
    elif t == 0:
        place_evenly(line + first_heads, 0, SLOTS_OF_PHASE - BURSTS)
    else:
        place_evenly(line, 0, shared_by - 2)
        for n, steps in zip((shared_by - 1, shared_by, shared_by + 2, shared_by + 4), pq_steps(layer, 0, range(SHARED_HEAD, PH))):
            slots[n] += steps
        place_evenly(first_heads, shared_by + 5, SLOTS_OF_PHASE - BURSTS)
    for c in range(2, SHARED_HEAD):
        slots[BURSTS * (c - 1) - 3].append((phase // TILES, phase % TILES, "query", c))
        slots[BURSTS * (c - 1) - 2].append((phase // TILES, phase % TILES, "score", c))
    return slots


_att = att_steps("n", 0)
PROLOGUE = [("n", 0, "gate"), ("n", 0, "ksw"), ("n", 0, "q", 0), ("n", 0, "vsw"), _att[0], ("n", 0, "kvc"), _att[1],
            ("n", 0, "hidden", 0), _att[2], ("n", 0, "hidden", 1), _att[3], ("n", 0, "q", 1), ("n", 0, "second"), _att[4],
            ("n", 0, "cs"), _att[5], ("n", 0, "ct")] + _att[6:]
PROLOGUE += [("n", 1, "qb", 0), ("n", 0, "o"), ("n", 1, "qb", 1), ("n", 0, "w", 0), ("n", 0, "w", 1), ("n", 1, "qb", 2),
             ("n", 1, "qb", 3), ("n", 1, "qb", 4), ("n", 1, "qb", 5), ("n", 0, "h"), ("n", 1, "qb", 6), (0, 0, "query", 0),
             ("n", 1, "qb", 7), (0, 0, "score", 0), (0, 0, "query", 1), (0, 0, "score", 1), ("p", 0, "free", 4), ("p", 0, "gate exp"),
             ("n", 1, "ksw"), ("p", 1, "free", 2), ("n", 1, "vsw"), ("p", 2, "free", 2)]
NEEDS = {("n", 0, "att", -1): [("n", 0, "ksw"), ("n", 0, "q", 0)], ("n", 0, "att", 1): [("n", 0, "vsw")],
         ("n", 0, "att", 3): [("n", 0, "q", 1)], ("n", 0, "cs"): [("n", 0, "q", 1), ("n", 0, "second")],
         ("n", 0, "hidden", 0): [("n", 0, "kvc")], ("n", 0, "second"): [("n", 0, "hidden", 0), ("n", 0, "hidden", 1)],
         ("n", 1, "cs"): [("n", 1, "qb", _n) for _n in range(8)] + [("n", 1, "ksw"), ("n", 1, "vsw")],
         ("p", 0, "free", 4): [("n", 1, "qb", _n) for _n in range(8)], ("p", 1, "free", 2): [("n", 1, "ksw")],
         ("p", 2, "free", 2): [("n", 1, "vsw")], (0, 0, "score", 0): [("n", 0, "second")]}

CONST = {}
_at = 0
for _name, _w in [("ident", P), ("cmp_mask", TILES * NCMP), ("causal", 2 * P),
                  ("rope", TILES * 2 * HALF), ("number", NCAND), ("pe", 2 * 16), ("w2k", HD), ("w2v", HD),
                  ("q_gain", 6), ("kv_gain", 2), ("q_up", 8), ("down", HEADS), ("ln_rows", P)]:
    CONST[_name] = (_at, _w)
    _at += _w
NCONST = _at


def spread(ap, axis, n):
    ap = ap.unsqueeze(axis)
    shape = list(ap.shape)
    shape[axis] = n
    return ap.broadcast_to(shape)


def trunk_kernel(nc, x, xT, weights, consts, alibi, cmp_table, ln_params, experts0, experts1, out):
    ctx = ExitStack()
    with ctx:
        def sb(name, shape, dt=F32):
            return ctx.enter_context(nc.sbuf_tensor("t_" + name, shape, dt))

        def pb(name, shape):
            return ctx.enter_context(nc.psum_tensor("p_" + name, shape, F32))

        def sem(name):
            return ctx.enter_context(nc.semaphore(name))

        ring = sb("ring", [P, SLOTS, 2 * D])
        wring = sb("wring", [P, WSLOTS, WCOLS])
        h = sb("h", [P, TILES, D])
        hT = sb("hT", [P, KD, SEQ])
        keyscore = sb("keyscore", [P, TILES, 2 * PH, NKEYS])
        lnp = sb("lnp", [P, 2, D])
        cst = sb("cst", [P, NCONST])
        kT_all = sb("kT", [P, HEADS, SEQ])
        kT = kT_all[0:QK, :, :]
        vM = sb("vM", [P, TILES, D])
        S = sb("S", [P, 2, 512])
        shared = sb("shared", [P, 3072])
        ropeT = sb("ropeT", [P, QK])
        small = sb("small", [P, 256])
        gates = sb("gates", [P, TILES, 3, HEADS])
        coef = sb("coef", [P, 3, HEADS])
        diag = sb("diag", [P, DIAGS, P])
        pqT = sb("pqT", [P, 2, 2, P])
        work = sb("work", [P, 2, NKEYS])
        onehot = sb("onehot", [P, TOPK, NCAND])
        top_val = sb("top_val", [P, 2, TOPK])
        top_pos = sb("top_pos", [P, 2, TOPK], U32)
        top_idx = sb("top_idx", [P, 2, TOPK])
        cand = sb("cand", [P, 2, NCAND])
        cand_idx = sb("cand_idx", [P, NCAND])
        best = sb("best", [P, TOPK])
        best_pos = sb("best_pos", [P, TOPK], U32)
        best_posf = sb("best_posf", [P, TOPK])
        best_idx = sb("best_idx", [P, TOPK])
        expert_id = sb("expert_id", [P, 2, TOPK], U32)
        gate_in = sb("gate_in", [P, 2, TOPK])
        gate_e = sb("gate_e", [P, 2, TOPK])
        gate_sum = sb("gate_sum", [P, 2])
        gate_w = sb("gate_w", [P, 2, TOPK])
        dots = sb("dots", [P, SLOTS])
        gelu = sb("gelu", [P, SLOTS])

        acc = pb("acc", [P, D])
        xdup = pb("xdup", [P, D])
        bank = [pb(f"bank{i}", [P, 512]) for i in range(3)]
        heads_out = pb("heads_out", [P, 512])

        def cuts(ap, what):
            at, parts = 0, []
            for n in what:
                parts.append(ap[:, at:at + n])
                at += n
            assert at <= ap.shape[1]
            return parts

        alibi_sb, qT, vblk, kcT = cuts(kT_all[:].rearrange("p h s -> p (h s)"), [4 * P, 8 * SEQ, GROUPS * 4 * HD, 2 * NCMP])
        alibi_sb = alibi_sb.rearrange("p (o s) -> p o s", o=2)
        qT = qT.rearrange("p (j t) -> p j t", j=8)
        vblk = vblk.rearrange("p (g j d) -> p g j d", g=GROUPS, j=4)
        kcT = kcT.rearrange("p (a n) -> p a n", a=2)
        kswT, vsw = cuts(vM[:].rearrange("p t c -> p (t c)"), [4 * SEQ, TILES * 512])
        kswT = kswT.rearrange("p (b a t) -> p b a t", b=2, a=2)
        vsw = vsw.rearrange("p (t c) -> p t c", t=TILES)
        pc, pcT, sc_raw, sc_exp, cmp_bias = cuts(keyscore[:, 1, :, :].rearrange("p c k -> p (c k)"),
                                                 [HEADS * 32, GROUPS * P, HEADS * NCMP, HEADS * NCMP, TILES * HEADS * NCMP])
        pc = pc.rearrange("p (h n) -> p h n", h=HEADS)
        pcT = pcT.rearrange("p (g t) -> p g t", g=GROUPS)
        sc_raw = sc_raw.rearrange("p (h n) -> p h n", h=HEADS)
        sc_exp = sc_exp.rearrange("p (h n) -> p h n", h=HEADS)
        cmp_bias = cmp_bias.rearrange("p (t h n) -> p t h n", t=TILES, h=HEADS)
        kc2, hk, hv, pe_bias = cuts(keyscore[:, 0, :, :].rearrange("p c k -> p (c k)"), [2 * (GROUPS + 1) * P, GROUPS * NCMP, GROUPS * 4 * 32, 2])
        kc2 = kc2.rearrange("p (v g u) -> p v g u", v=2, g=GROUPS + 1)
        hk = hk.rearrange("p (g n) -> p g n", g=GROUPS)
        hv = hv.rearrange("p (g j n) -> p g j n", g=GROUPS, j=4)

        def held(name):
            s = HELD[name]
            return ring[:, s:s + 2, :].rearrange("p s c -> p (s c)")

        def view(name):
            a, w = CONST[name]
            return cst[:, a:a + w]

        ident = view("ident")
        cmp_mask = view("cmp_mask").rearrange("p (t n) -> p t n", t=TILES)
        causal = view("causal")
        ln_rows = view("ln_rows")[0:4 * 2 * KD, :]
        rope = view("rope").rearrange("p (t c k) -> p t c k", t=TILES, c=2)
        number = view("number")
        pe_cols = view("pe").rearrange("p (v l) -> p v l", v=2)
        w2k, w2v, q_gain, kv_gain, q_up, down = [view(n) for n in ("w2k", "w2v", "q_gain", "kv_gain", "q_up", "down")]

        ckv = shared[:, 0:KV_LORA + ROPE]
        ckvT = shared[:, 288:288 + 2 * P].rearrange("p (k t) -> p k t", k=2)
        cqT = shared[:, Q_LORA:2 * Q_LORA].rearrange("p (k t) -> p k t", k=6)
        cq = shared[:, 2 * Q_LORA:3 * Q_LORA]
        q_nat = shared[:, 2 * Q_LORA:2 * Q_LORA + HEADS * QK]
        mixed = shared[:, 0:D]
        probs = shared[:, D:2 * D].rearrange("p (s k) -> p s k", s=2)
        probsT = shared[:, 2 * D:3 * D].rearrange("p (s b t) -> p s b t", s=2, b=4)
        mixedT = S[:].rearrange("p a b -> p (a b)").rearrange("p (k t) -> p k t", k=KD)
        rope_tmp = S[:].rearrange("p a b -> p (a b)")
        pqT_both = S[:].rearrange("p s (i t) -> p s i t", i=2)

        def mlaqT(t):
            return keyscore[0:QK, t, :, :]

        stat = small[:, 0:12].rearrange("p (a b) -> p a b", a=2)
        moments = small[:, 12:14]
        std = small[:, 14:15]
        rstd = small[:, 15:16]
        row_max = small[:, 224:232]
        neg_max = small[:, 232:240]
        rms_in = small[:, 24:25]
        rms_std = small[:, 25:26]
        rms_r = small[:, 26:27]
        cmp_max = small[:, 32:48]
        row_sum = small[:, 48:96].rearrange("p (b h) -> p b h", b=3)
        inv_sum = small[:, 96:112]
        kr_tmp = small[:, 112:176].rearrange("p (a k) -> p a k", a=4)
        denom = small[:, 176:224].rearrange("p (b h) -> p b h", b=3)

        x_loaded = sem("x_loaded")
        xT_loaded = sem("xT_loaded")
        const_loaded = sem("const_loaded")
        alibi_loaded = sem("alibi_loaded")
        cmp_bias_loaded = sem("cmp_bias_loaded")
        xdup_ready = sem("xdup_ready")
        ln_loaded = sem("ln_loaded")
        w_loaded = [sem(f"w_loaded{i}") for i in range(WSLOTS)]
        held_loaded = {name: sem(f"{name}_loaded") for name in HELD}
        zeroed = sem("zeroed")
        bank_filled = [sem(f"bank_filled{i}") for i in range(3)]
        bank_drained = [sem(f"bank_drained{i}") for i in range(3)]
        heads_filled = sem("heads_filled")
        heads_drained = sem("heads_drained")
        scores_ready = sem("scores_ready")
        probs_ready = sem("probs_ready")
        cmp_ready = sem("cmp_ready")
        cmp_exp = sem("cmp_exp")
        cmp_probs = sem("cmp_probs")
        pe_done = sem("pe_done")
        mixed_ready = sem("mixed_ready")
        var_ready = sem("var_ready")
        std_ready = sem("std_ready")
        ln_done = sem("ln_done")
        rms_ready = sem("rms_ready")
        rms_std_ready = sem("rms_std_ready")
        latent_ready = sem("latent_ready")
        q_rotated = sem("q_rotated")
        dve_chain = sem("dve_chain")
        gate_in_ready = sem("gate_in_ready")
        gate_e_ready = sem("gate_e_ready")
        ids_ready = sem("ids_ready")
        gathers_issued = sem("gathers_issued")
        gathered = [sem(f"gathered{i}") for i in range(SLOTS)]
        slot_free = sem("slot_free")
        dot_ready = sem("dot_ready")
        gelu_ready = sem("gelu_ready")
        diag_ready = sem("diag_ready")
        acc_read = sem("acc_read")
        out_stored = sem("out_stored")

        ITEMS = 2 * TILES * PH
        LN_LOAD = [0, 0, 1, 2, 3, 4, 5, 5]
        LN_ROW = [0, 2, 1, 2, 1, 3]
        places = chunk_places()
        chunk_order, chunk_end = [], {}
        place = {}

        def unit0(kind, t):
            before = list(ATT)[:list(ATT).index((kind, t))]
            return sum(ATT[k] for k in before), sum({"n": 4, "m": 2}[k[0]] for k in before)

        def head_of(kind, t, u):
            n_heads = 4 // (t + 1)
            per_fill = 8 // n_heads
            if kind == "m":
                return u * n_heads, 0
            return u // (2 * per_fill) * 8 + u % per_fill * n_heads, u // per_fill % 2

        def peer_ln(phase):
            return [3, 5, 7, 8][phase]

        def mla_ln(t):
            return [4, 6][t]

        block = ctx.enter_context(nc.Block())

        @block.tensor
        def _(pe):
            fills = [0]
            chunks = {}

            def chunk(layer, name):
                n = len(chunk_order)
                chunk_order.append((layer, name))
                pe.wait_ge(w_loaded[n % WSLOTS], 16 * (n // WSLOTS + 1))
                return wring[:, n % WSLOTS, :]

            def held_chunk(name):
                pe.wait_ge(held_loaded[name], 16)
                return held(name)

            def release(n=-1):
                chunk_end[n % len(chunk_order)] = ((fills[0] - 1) % 3, (fills[0] - 1) // 3)

            def fill(step):
                b, use = fills[0] % 3, fills[0] // 3
                fills[0] += 1
                if use:
                    pe.wait_ge(bank_drained[b], use)
                place.setdefault(step, []).append((b, use))
                return b

            def drained(step):
                for b, use in place[step]:
                    pe.wait_ge(bank_drained[b], use + 1)

            def transposed_projection(w, cols, src, b, at, k_tiles, tokens):
                for k in range(k_tiles):
                    last = nc.tensor.matmul(bank[b][:, at:at + tokens.stop - tokens.start], w[:, k, cols],
                                            src[:, k, tokens], start=k == 0, stop=k == k_tiles - 1)
                return last

            def tile_transposes(step, src, n):
                for k in range(n):
                    if k % 4 == 0:
                        b = fill(step)
                    last = nc.tensor.transpose(bank[b][:, (k % 4) * P:(k % 4 + 1) * P], src[:, k * P:(k + 1) * P], ident)
                    if k % 4 == 3 or k == n - 1:
                        last.then_inc(bank_filled[b], 1)

            def natural(step, src, tokens, w, cols, k_tiles, n):
                b = fill(step)
                for k in range(k_tiles):
                    last = nc.tensor.matmul(bank[b][:, 0:n], src[:, k, tokens], w[:, k, cols], start=k == 0, stop=k == k_tiles - 1)
                last.then_inc(bank_filled[b], 1)

            def kxn(w, k_tiles, n):
                return w[:, 0:k_tiles * n].rearrange("p (k n) -> p k n", k=k_tiles)

            def attention(kind, t, i):
                key_blocks = t + 1
                n_heads = 4 // key_blocks
                units = ATT[kind, t]
                first, first_out = unit0(kind, t)
                tok = slice(t * P, (t + 1) * P)
                W = key_blocks * P

                def operands(u, r):
                    hh, br = head_of(kind, t, u)
                    hh += r
                    if kind == "m":
                        return mlaqT(t)[:, hh, :], kT[:, hh, 0:W], lambda kb: vM[:, kb, hh * HD:(hh + 1) * HD]
                    g = hh // 4
                    p0 = g % 2 * HD
                    return (qT[p0:p0 + HD, g // 2 * 4 + hh % 4, tok], kswT[p0:p0 + HD, br, g // 2, 0:W],
                            lambda kb: vsw[:, kb, br * 256 + g * HD:br * 256 + (g + 1) * HD])

                if i + 1 < units:
                    b = fill((kind, t, "scores", i + 1))
                    for r in range(n_heads):
                        q, k, _ = operands(i + 1, r)
                        last = nc.tensor.matmul(bank[b][:, r * W:(r + 1) * W], q, k, start=True, stop=True)
                    last.then_inc(bank_filled[b], 1)
                if 0 <= i < units:
                    b = fill((kind, t, "probsT", i))
                    pe.wait_ge(probs_ready, first + i + 1)
                    for c in range(4):
                        last = nc.tensor.transpose(bank[b][:, c * P:(c + 1) * P], probs[:, (first + i) % 2, c * P:(c + 1) * P], ident)
                    last.then_inc(bank_filled[b], 1)
                if i >= 1:
                    u = i - 1
                    per_fill = 8 // n_heads
                    if u % per_fill == 0 and first_out + u // per_fill:
                        pe.wait_ge(heads_drained, first_out + u // per_fill)
                    drained((kind, t, "probsT", u))
                    for r in range(n_heads):
                        at = (u % per_fill * n_heads + r) * HD
                        v = operands(u, r)[2]
                        for kb in range(key_blocks):
                            last = nc.tensor.matmul(heads_out[:, at:at + HD], probsT[:, (first + u) % 2, r * key_blocks + kb, :],
                                                    v(kb), start=kb == 0, stop=kb == key_blocks - 1)
                    if u % per_fill == per_fill - 1:
                        last.then_inc(heads_filled, 1)

            def mixed_transposes(kind, t):
                pe.wait_ge(mixed_ready, t + 1 if kind == "n" else TILES + t + 1)
                tile_transposes((kind, t, "o"), mixed, KD)

            def output(kind, t, half):
                if half == 0:
                    drained((kind, t, "o"))
                b = fill((kind, t, "w", half))
                for part in range(2):
                    layer, name = (0, "wo") if kind == "n" else (1, "mo")
                    w = kxn(chunk(layer, f"{name}{half}{part}"), 4, 512)
                    for k in range(4):
                        last = nc.tensor.matmul(bank[b][:], mixedT[:, 4 * part + k, :], w[:, k, :], start=part + k == 0, stop=part + k == 4)
                    release()
                last.then_inc(bank_filled[b], 1)

            def h_transposes(step, t, count):
                pe.wait_ge(ln_done, count)
                tile_transposes(step, h[:, t, :], KD)

            def peer_queries(layer, t, c):
                shared_chunk = both_tiles(c)
                if c == 0 or shared_chunk:
                    drained(("m" if layer else "n", 1 if shared_chunk else t, "h"))
                w = chunk(layer, f"pq{c}")
                chunks[layer, t, c] = w, len(chunk_order) - 1
                tok = slice(0, SEQ) if shared_chunk else slice(t * P, (t + 1) * P)
                b = fill((layer, t, "query", c))
                for i in range(2):
                    last = transposed_projection(kxn(w, KD, 256), slice(i * P, (i + 1) * P), hT, b, i * (tok.stop - tok.start), KD, tok)
                last.then_inc(bank_filled[b], 1)

            def peer_scores(layer, t, c):
                w, n_chunk = chunks[layer, t, c]
                b = fill((layer, t, "score", c))
                drained((layer, t, "query", c))
                queries_T = [pqT[:, c % 2, i, :] for i in range(2)]
                if both_tiles(c):
                    place[layer, 1, "score", c] = place[layer, 0, "score", c]
                    queries_T = [pqT_both[:, c % 2, i, j * P:(j + 1) * P] for j in range(TILES) for i in range(2)]
                for n, q in enumerate(queries_T):
                    i = n % 2
                    last = nc.tensor.matmul(bank[b][:, n * NKEYS:(n + 1) * NKEYS], q,
                                            w[:, KD * 256 + i * NKEYS:KD * 256 + (i + 1) * NKEYS], start=True, stop=True)
                last.then_inc(bank_filled[b], 1)
                release(n_chunk)

            def ln_broadcast(n):
                for half in range(4):
                    b = fill(("p", 0, "lnp", n))
                    for i in range(4):
                        row = LN_ROW[n] * 2 * KD + half * 4 + i
                        last = nc.tensor.matmul(bank[b][:, i * P:(i + 1) * P], ident[0:4 * 2 * KD, row:row + 1].broadcast_to([4 * 2 * KD, P]),
                                                ln_rows, start=True, stop=True)
                    last.then_inc(bank_filled[b], 1)

            def rows_to_compress():
                for n in range(2):
                    w = kxn(chunk(0, f"kvc{n}"), KD, 256)
                    b = fill(("n", 0, "kvc"))
                    for i in range(2):
                        last = transposed_projection(w, slice(i * P, (i + 1) * P), hT, b, i * SEQ, KD, slice(0, SEQ))
                    last.then_inc(bank_filled[b], 1)
                    release()

            def held_blocks(step, t, name, blocks):
                w = kxn(held_chunk(name), KD, 512)
                b = fill(step)
                for i, j in enumerate(blocks):
                    last = transposed_projection(w, slice(j % 4 * P, (j % 4 + 1) * P), hT, b, i * P, KD, slice(t * P, (t + 1) * P))
                last.then_inc(bank_filled[b], 1)

            def branch_values(t):
                natural(("n", t, "vsw"), hT, slice(t * P, (t + 1) * P), kxn(held_chunk("vsw"), KD, 512), slice(0, 512), KD, 512)

            def gate_logits():
                w = kxn(chunk(0, "gate"), KD, 48)
                for t in range(TILES):
                    natural(("n", 0, "gate"), hT, slice(t * P, (t + 1) * P), w, slice(0, 48), KD, 48)
                release()

            def compress(v):
                w = kxn(chunk(0, ("ck1", "cv1")[v]), 16, P)
                b = fill(("n", 0, "hidden", v))
                rows = kc2[:, v, :, :].rearrange("p g (n l) -> p g n l", l=8)
                for l in range(16):
                    last = nc.tensor.matmul(bank[b][:, 0:(GROUPS + 1) * (NCMP - 1)], w[:, l, :],
                                            rows[:, :, l // 8:l // 8 + NCMP - 1, l % 8], start=l == 0, stop=l == 15)
                last.then_inc(bank_filled[b], 1)
                release()

            def compress_second():
                b = fill(("n", 0, "second"))
                for par in range(2):
                    last = nc.tensor.matmul(bank[b][par * HD:(par + 1) * HD, 0:2 * NCMP], w2k,
                                            hk.rearrange("p (a e) n -> p e a n", e=2)[:, par, :, :], start=True, stop=True)
                last.then_inc(bank_filled[b], 1)
                b = fill(("n", 0, "second"))
                for g in range(GROUPS):
                    last = nc.tensor.matmul(bank[b][:, g * HD:(g + 1) * HD], hv[:, g, :, :].rearrange("p j n -> p (j n)"), w2v,
                                            start=True, stop=True)
                last.then_inc(bank_filled[b], 1)

            def cmp_scores(t):
                for e in range(2):
                    b = fill(("n", t, "cs"))
                    p0 = e * HD
                    for j in range(8):
                        last = nc.tensor.matmul(bank[b][:, j * NCMP:(j + 1) * NCMP], qT[p0:p0 + HD, j, t * P:(t + 1) * P],
                                                kcT[p0:p0 + HD, j // 4, :], start=True, stop=True)
                    last.then_inc(bank_filled[b], 1)

            def cmp_transposes(t):
                b = fill(("n", t, "ct"))
                pe.wait_ge(cmp_probs, t + 1)
                for g in range(GROUPS):
                    last = nc.tensor.transpose(bank[b][:, g * P:(g + 1) * P],
                                               pc[:, 4 * g:4 * g + 4, :].rearrange("p h n -> p (h n)"), ident)
                last.then_inc(bank_filled[b], 1)

            def cmp_values(t):
                drained(("n", t, "ct"))
                for half in range(2):
                    b = fill(("n", t, "cv"))
                    for i in range(2):
                        g = 2 * half + i
                        last = nc.tensor.matmul(bank[b][:, i * 256:(i + 1) * 256], pcT[:, g, :],
                                                vblk[:, g, :, :].rearrange("p j d -> p (j d)"), start=True, stop=True)
                    last.then_inc(bank_filled[b], 1)

            def latent_kv(t):
                drained(("m", t, "h0"))
                n = KV_LORA + ROPE
                natural(("m", t, "dkv"), hT, slice(t * P, (t + 1) * P), kxn(chunk(1, "dkv"), KD, n), slice(0, n), KD, n)
                release()

            def latent_q(t, half):
                natural(("m", t, "dq", half), hT, slice(t * P, (t + 1) * P), kxn(chunk(1, f"dq{half}"), KD, 384),
                        slice(0, 384), KD, 384)
                release()

            def latent_kv_transposes(t):
                b = fill(("m", t, "lt"))
                pe.wait_ge(latent_ready, 2 * t + 1)
                for k in range(2):
                    nc.tensor.transpose(bank[b][:, k * P:(k + 1) * P], ckv[:, k * P:(k + 1) * P], ident)
                nc.tensor.transpose(bank[b][0:QK, 2 * P:3 * P], ropeT[:], ident).then_inc(bank_filled[b], 1)

            def keys(t):
                drained(("m", t, "lt"))
                w = kxn(chunk(1, "uk"), 2, D)
                for n in range(2):
                    b = fill(("m", t, "uk"))
                    for i in range(4):
                        last = transposed_projection(w, slice((4 * n + i) * P, (4 * n + i + 1) * P), ckvT, b, i * P, 2, slice(0, P))
                    last.then_inc(bank_filled[b], 1)
                release()

            def values(t):
                w = kxn(chunk(1, "uv"), 2, D)
                for n in range(2):
                    natural(("m", t, "uv"), ckvT, slice(0, P), w, slice(n * 512, (n + 1) * 512), 2, 512)
                release()

            def latent_q_transposes(t):
                pe.wait_ge(latent_ready, 2 * t + 2)
                tile_transposes(("m", t, "ct"), cq, 6)

            def queries(t, n):
                if n == 0:
                    drained(("m", t, "ct"))
                natural(("m", t, "uq", n), cqT, slice(0, P), kxn(chunk(1, f"uq{n}"), 6, 512), slice(0, 512), 6, 512)
                release()

            def query_transposes(t, half):
                pe.wait_ge(q_rotated, t + 1)
                for n in range(2):
                    b = fill(("m", t, "qt", half))
                    for i in range(4):
                        hh = 8 * half + 4 * n + i
                        last = nc.tensor.transpose(bank[b][0:QK, i * P:(i + 1) * P], q_nat[:, hh * QK:(hh + 1) * QK], ident)
                    last.then_inc(bank_filled[b], 1)

            def run(step):
                a, t, what, *n = step
                for other in NEEDS.get(step, []):
                    drained(other)
                if what == "query":
                    peer_queries(a, t, *n)
                elif what == "score":
                    peer_scores(a, t, *n)
                elif what == "lnp":
                    ln_broadcast(*n)
                elif what == "free":
                    pe.sem_inc(slot_free, *n)
                elif what == "kvc":
                    rows_to_compress()
                elif what == "ksw":
                    held_blocks(step, t, "ksw", range(4))
                elif what == "q":
                    held_blocks(step, t, f"q{n[0]}", range(4))
                elif what == "qb":
                    held_blocks(step, t, f"q{n[0] // 4}", n)
                elif what == "gate":
                    gate_logits()
                elif what == "hidden":
                    compress(*n)
                elif what == "second":
                    compress_second()
                elif what == "att":
                    if a == "m" and n == [-1]:
                        drained((a, t, "qt", 0))
                        drained((a, t, "qt", 1))
                    attention(a, t, *n)
                elif what == "h0":
                    h_transposes(step, t, peer_ln(t))
                elif what == "h":
                    h_transposes(step, t, t + 1 if a == "n" else mla_ln(t))
                elif what == "o":
                    mixed_transposes(a, t)
                elif what == "w":
                    output(a, t, *n)
                elif what not in ("ln", "gate exp"):
                    {"cs": cmp_scores, "ct": cmp_transposes if a == "n" else latent_q_transposes, "cv": cmp_values, "vsw": branch_values,
                     "dkv": latent_kv, "dq": latent_q, "lt": latent_kv_transposes, "uk": keys, "uv": values,
                     "uq": queries, "qt": query_transposes}[what](t, *n)

            pe.wait_ge(xT_loaded, 16)
            pe.wait_ge(const_loaded, 16)
            for step in PROLOGUE:
                run(step)

            def burst(step0, first=False, i=None):
                for k in range(BURST if i is None else SLOTS):
                    pe.wait_ge(diag_ready, step0 + k + 1 if i is None else i * SLOTS + (step0 + k + 1))
                    for half in range(2):
                        last = nc.tensor.matmul(acc[:, half * 512:(half + 1) * 512], diag[:, (step0 + k) % DIAGS, :],
                                                ring[:, (step0 + k) % SLOTS, D + half * 512:D + (half + 1) * 512],
                                                start=first and k == 0, stop=False, skip_group_check=True)
                    last.then_inc(slot_free, 1)

            for phase in range(2 * TILES):
                slots = phase_slots(phase)
                if phase:
                    pe.wait_ge(acc_read, phase)
                for head in range(PH):
                    step0 = (phase * PH + head) * TOPK
                    if head and not any(slots[head * BURSTS:(head + 1) * BURSTS]):
                        with pe.Fori(0, TOPK // SLOTS, 1) as i:
                            burst(step0, i=i)
                        continue
                    for k in range(BURSTS):
                        for step in slots[head * BURSTS + k]:
                            run(step)
                        burst(step0 + k * BURST, first=head + k == 0)

        @block.sync
        def _(sp):
            sp.dma_start(hT[:], xT).then_inc(xT_loaded, 16)
            follows = {"gate": ["ksw", "q0", "vsw"], "kvc0": ["q1"]}
            for n, name in enumerate(chunk_order):
                off, width = places[name]
                if n >= WSLOTS:
                    b, use = chunk_end[n - WSLOTS]
                    sp.wait_ge(bank_filled[b], use + 1)
                src = weights[off:off + P * width].rearrange("(p w) -> p w", p=P)
                sp.dma_start(wring[:, n % WSLOTS, 0:width], src).then_inc(w_loaded[n % WSLOTS], 16)
                for other in follows.get(name[1], []):
                    off, width = places[0, other]
                    src = weights[off:off + P * width].rearrange("(p w) -> p w", p=P)
                    sp.dma_start(held(other), src).then_inc(held_loaded[other], 16)
            for t in range(TILES):
                sp.wait_ge(ln_done, peer_ln(2 + t))
                sp.dma_start(out[t * P:(t + 1) * P, :], h[:, t, :]).then_inc(out_stored, 16)
            sp.wait_ge(out_stored, 16 * TILES)

        @block.gpsimd
        def _(pool):
            for ap in (kc2[:, :, GROUPS, :], ropeT[:], kcT, vblk, hk, hv):
                nc.gpsimd.memset(ap, 0.0)
            nc.gpsimd.memset(pc, 0.0).then_inc(zeroed, 1)
            for layer, table in enumerate((experts0, experts1)):
                with pool.Fori(0, TILES * PH // 2, 1) as i:
                    for half in range(2):
                        item = 2 * i + (layer * TILES * PH + half)
                        for s in range(TOPK):
                            if s == 0:
                                pool.wait_ge(ids_ready, item + 1)
                            pool.wait_ge(slot_free, item * TOPK + (s + 1))
                            pool.sem_inc(gathers_issued, 1)
                            nc.gpsimd.indirect_dma_start(
                                out=ring[:, s % SLOTS, :], out_offset=None, in_=table,
                                in_offset=bass.IndirectOffsetOnAxis(ap=expert_id[:, half, s:s + 1], axis=0),
                            ).then_inc(gathered[s % SLOTS], 16)

        @block.scalar
        def _(act):
            def full(step, n=0):
                b, use = place[step][n]
                act.wait_ge(bank_filled[b], use + 1)
                return b

            def drain(step, n, dst, width=512):
                b = full(step, n)
                nc.scalar.activation(dst, bank[b][:, 0:width], ACT.Copy).then_inc(bank_drained[b], 1)

            def layer_norm_root(e):
                act.wait_ge(var_ready, e + 1)
                nc.scalar.activation(std, rstd, ACT.Sqrt).then_inc(std_ready, 1)

            def rms_root(n):
                act.wait_ge(rms_ready, n)
                nc.scalar.activation(rms_std, rms_in, ACT.Sqrt).then_inc(rms_std_ready, 1)

            def attention(kind, t, i):
                u = i + 1
                if u < ATT[kind, t]:
                    exponentials(kind, t, u)
                if 0 <= i < ATT[kind, t]:
                    drain((kind, t, "probsT", i), 0, probsT[:, (unit0(kind, t)[0] + i) % 2, :, :].rearrange("p b t -> p (b t)"))

            def exponentials(kind, t, u):
                W = (t + 1) * P
                n_heads = 4 // (t + 1)
                n = unit0(kind, t)[0] + u
                h0, br = head_of(kind, t, u)
                br += kind == "n"
                act.wait_ge(scores_ready, n + 1)
                for r in range(n_heads):
                    hh = h0 + r
                    last = nc.scalar.activation(probs[:, n % 2, r * W:(r + 1) * W], S[:, n % 2, r * W:(r + 1) * W], ACT.Exp,
                                                bias=neg_max[:, n % 2 * 4 + r:n % 2 * 4 + r + 1],
                                                scale=NSA_SCALE if kind == "n" else MLA_SCALE, accum_out=row_sum[:, br, hh:hh + 1])
                last.then_inc(probs_ready, 1)

            def drain_tiles(step, n, dst):
                b = full(step, n)
                nc.scalar.activation(dst, bank[b][:].rearrange("p (k t) -> p k t", k=4), ACT.Copy).then_inc(bank_drained[b], 1)

            def peer_queries(step, layer, t, c):
                b = full(step)
                both = both_tiles(c)
                src = bank[b][:, 0:(4 if both else 2) * P].rearrange("p (i t) -> p i t", i=2)
                nc.scalar.activation((pqT_both if both else pqT)[:, c % 2, :, :], src, ACT.Copy).then_inc(bank_drained[b], 1)

            def peer_scores(step, layer, t, c):
                b = full(step)
                n = 2 if both_tiles(c) else 1
                nc.scalar.activation(keyscore[:, t:t + n, 2 * c:2 * c + 2, :],
                                     bank[b][:, 0:n * 2 * NKEYS].rearrange("p (t i k) -> p t i k", t=n, i=2),
                                     ACT.Copy).then_inc(bank_drained[b], 1)

            def ln_broadcast(step, n):
                act.wait_ge(ln_done, LN_LOAD.index(n))
                for half in range(4):
                    drain(step, half, lnp[:].rearrange("p a d -> p (a d)")[:, half * 512:(half + 1) * 512])

            def latent_kv(t):
                drain(("m", t, "dkv"), 0, ckv, KV_LORA + ROPE)
                rms_root(2 * t + 1)

            def latent_q(t, half):
                drain(("m", t, "dq", half), 0, cq[:, half * 384:(half + 1) * 384], 384)
                if half:
                    rms_root(2 * t + 2)

            def latent_kv_transposes(t):
                b = full(("m", t, "lt"))
                for k in range(2):
                    nc.scalar.activation(ckvT[:, k, :], bank[b][:, k * P:(k + 1) * P], ACT.Copy, scale=kv_gain[:, k:k + 1])
                nc.scalar.activation(kT[HD:QK, :, t * P:(t + 1) * P], spread(bank[b][HD:QK, 2 * P:3 * P], 1, HEADS),
                                     ACT.Copy).then_inc(bank_drained[b], 1)

            def keys(t):
                for n in range(2):
                    b = full(("m", t, "uk"), n)
                    src = bank[b][:].rearrange("p (i s) -> p i s", i=4)
                    dst = kT[0:HD, 8 * n:8 * n + 8, t * P:(t + 1) * P].rearrange("p (i e) s -> p e i s", e=2)
                    for e in range(2):
                        last = nc.scalar.activation(dst[:, e, :, :], src[e * HD:(e + 1) * HD, :, :], ACT.Copy)
                    last.then_inc(bank_drained[b], 1)

            def values(t):
                for n in range(2):
                    drain(("m", t, "uv"), n, vM[:, t, n * 512:(n + 1) * 512])

            def latent_q_transposes(t):
                for n, w in ((0, 4), (1, 2)):
                    b = full(("m", t, "ct"), n)
                    for k in range(w):
                        last = nc.scalar.activation(cqT[:, 4 * n + k, :], bank[b][:, k * P:(k + 1) * P], ACT.Copy,
                                                    scale=q_gain[:, 4 * n + k:4 * n + k + 1])
                    last.then_inc(bank_drained[b], 1)

            def queries(t, n):
                drain(("m", t, "uq", n), 0, q_nat[:, n * 512:(n + 1) * 512])

            def query_transposes(t, half):
                for n in range(2):
                    b = full(("m", t, "qt", half), n)
                    at = 8 * half + 4 * n
                    nc.scalar.activation(mlaqT(t)[:, at:at + 4, :].rearrange("p h t -> p (h t)"), bank[b][0:QK, :],
                                         ACT.Copy).then_inc(bank_drained[b], 1)

            def gate_exps(item):
                act.wait_ge(gate_in_ready, item + 1)
                nc.scalar.activation(gate_e[:, item % 2, :], gate_in[:, item % 2, :], ACT.Exp,
                                     accum_out=gate_sum[:, item % 2:item % 2 + 1]).then_inc(gate_e_ready, 1)

            def gates_exp():
                for t in range(TILES):
                    b = full(("n", 0, "gate"), t)
                    nc.scalar.activation(gates[:, t, :, :].rearrange("p b h -> p (b h)"), bank[b][:, 0:3 * HEADS], ACT.Exp,
                                         scale=-1.0).then_inc(bank_drained[b], 1)

            def rows_to_compress():
                act.wait_ge(zeroed, 1)
                act.wait_ge(const_loaded, 16)
                for v in range(2):
                    nc.scalar.activation(kc2[:, v, GROUPS, 0:16], pe_cols[:, v, :], ACT.Copy)
                    b = full(("n", 0, "kvc"), v)
                    src = bank[b][:].rearrange("p (a u par) -> p a u par", a=2, par=2)
                    dst = kc2[:, v, 0:GROUPS, :].rearrange("p (a e) u -> p e a u", e=2)
                    for e in range(2):
                        for par in range(2):
                            last = nc.scalar.activation(dst[par * HD:(par + 1) * HD, e, :, :],
                                                        src[e * HD:(e + 1) * HD, :, :, par], ACT.Copy)
                    last.then_inc(bank_drained[b], 1)

            def hidden(v):
                b = full(("n", 0, "hidden", v))
                nc.scalar.activation(pe_bias[:, v:v + 1], bank[b][:, GROUPS * (NCMP - 1):GROUPS * (NCMP - 1) + 1], ACT.Copy).then_inc(pe_done, 1)
                act.wait_ge(pe_done, v + 1)
                src = bank[b][:, 0:GROUPS * (NCMP - 1)].rearrange("p (g n) -> p g n", g=GROUPS)
                for j in range(1 if v == 0 else 4):
                    dst = hk[:, :, 0:NCMP - 1] if v == 0 else hv[:, :, j, 0:NCMP - 1]
                    last = nc.scalar.activation(dst, src, ACT.Gelu_apprx_tanh, bias=pe_bias[:, v:v + 1])
                last.then_inc(bank_drained[b], 1)

            def compressed():
                step = ("n", 0, "second")
                drain(step, 0, kcT.rearrange("p a n -> p (a n)"), 2 * NCMP)
                b = full(step, 1)
                for j in range(4):
                    q = slice(32 * j, 32 * j + 32)
                    last = nc.scalar.activation(vblk[q, :, j, :], bank[b][q, 0:GROUPS * HD].rearrange("p (g d) -> p g d", g=GROUPS),
                                                ACT.Copy)
                last.then_inc(bank_drained[b], 1)

            def nsa_queries(step, t, blocks):
                b = full(step)
                for i, j in enumerate(blocks):
                    last = nc.scalar.activation(qT[:, j, t * P:(t + 1) * P], bank[b][:, i * P:(i + 1) * P], ACT.Copy,
                                                scale=q_up[:, j:j + 1])
                last.then_inc(bank_drained[b], 1)

            def cmp_exps(t):
                act.wait_ge(cmp_ready, t + 1)
                nc.scalar.activation(sc_exp, sc_raw, ACT.Exp, scale=NSA_SCALE).then_inc(cmp_exp, 1)

            def run(step):
                a, t, what, *n = step
                if what == "query":
                    peer_queries(step, a, t, *n)
                elif what == "score":
                    peer_scores(step, a, t, *n)
                elif what == "lnp":
                    ln_broadcast(step, *n)
                elif what == "att":
                    attention(a, t, *n)
                elif what in ("h", "h0"):
                    for i in range(2):
                        drain_tiles(step, i, hT[:, 4 * i:4 * i + 4, t * P:(t + 1) * P])
                elif what == "o":
                    for i in range(2):
                        drain_tiles(step, i, mixedT[:, 4 * i:4 * i + 4, :])
                elif what == "w":
                    if n == [1]:
                        layer_norm_root(t if a == "n" else mla_ln(t) - 1)
                elif what == "ln":
                    layer_norm_root(peer_ln(*n) - 1)
                elif what == "cs":
                    cmp_exps(t)
                elif what == "gate":
                    gates_exp()
                elif what == "gate exp":
                    gate_exps(0)
                elif what == "ksw":
                    b = full(step)
                    nc.scalar.activation(kswT[:, :, :, t * P:(t + 1) * P].rearrange("p b a t -> p (b a) t"),
                                         bank[b][:].rearrange("p (i t) -> p i t", i=4), ACT.Copy).then_inc(bank_drained[b], 1)
                elif what == "kvc":
                    rows_to_compress()
                elif what == "hidden":
                    hidden(*n)
                elif what == "second":
                    compressed()
                elif what == "q":
                    nsa_queries(step, t, range(4 * n[0], 4 * n[0] + 4))
                elif what == "qb":
                    nsa_queries(step, t, n)
                elif what == "vsw":
                    drain(step, 0, vsw[:, t, :])
                elif a == "m":
                    {"ct": latent_q_transposes, "dkv": latent_kv, "dq": latent_q, "lt": latent_kv_transposes, "uk": keys,
                     "uv": values, "uq": queries, "qt": query_transposes}[what](t, *n)

            act.dma_start(cst[:], consts).then_inc(const_loaded, 16)
            act.dma_start(alibi_sb.rearrange("p o s -> p (o s)"), alibi).then_inc(alibi_loaded, 16)
            act.dma_start(cmp_bias.rearrange("p t h n -> p (t h n)"), cmp_table).then_inc(cmp_bias_loaded, 16)
            for step in PROLOGUE:
                run(step)
                if step[2] == "vsw" and step[1] == 0:
                    act.dma_start(h[:], x.rearrange("(t p) d -> p t d", p=P)).then_inc(x_loaded, 16)
                    act.dma_start(lnp[:].rearrange("p a d -> p (a d)"),
                                  ln_params[LN_ROW[0], :].partition_broadcast(P)).then_inc(ln_loaded, 16)

            def burst(step0, i=None):
                for k in range(BURST if i is None else SLOTS):
                    s = (step0 + k) % SLOTS
                    act.wait_ge(dot_ready, step0 + k + 1 if i is None else i * SLOTS + (step0 + k + 1))
                    nc.scalar.activation(gelu[:, s:s + 1], dots[:, s:s + 1], ACT.Gelu_apprx_tanh).then_inc(gelu_ready, 1)

            for phase in range(2 * TILES):
                slots = phase_slots(phase)
                if phase:
                    act.wait_ge(dot_ready, phase * PH * TOPK)
                act.wait_ge(ln_done, [1, 2, mla_ln(0), mla_ln(1)][phase])
                for half in range(2):
                    last = nc.scalar.activation(xdup[:, half * 512:(half + 1) * 512], h[:, phase % TILES, half * 512:(half + 1) * 512], ACT.Copy)
                last.then_inc(xdup_ready, 1)
                for head in range(PH):
                    item = phase * PH + head
                    step0 = item * TOPK
                    if head and not any(slots[head * BURSTS:(head + 1) * BURSTS]):
                        if item + 1 < ITEMS:
                            gate_exps(item + 1)
                        with act.Fori(0, TOPK // SLOTS, 1) as i:
                            burst(step0, i)
                        continue
                    for k in range(BURSTS):
                        burst(step0 + k * BURST)
                        for step in slots[head * BURSTS + k]:
                            run(step)
                        if k == 0 and item + 1 < ITEMS:
                            gate_exps(item + 1)
            layer_norm_root(peer_ln(2 * TILES - 1) - 1)

        @block.vector
        def _(dve):
            chain = [0]

            def link(ins):
                chain[0] += 1
                ins.then_inc(dve_chain, 1)
                dve.wait_ge(dve_chain, chain[0])

            def full(step, n=0):
                b, use = place[step][n]
                dve.wait_ge(bank_filled[b], use + 1)
                return b

            def drained(step):
                for b, use in place[step]:
                    dve.wait_ge(bank_drained[b], use + 1)

            def attention(kind, t, i):
                units = ATT[kind, t]
                first, first_out = unit0(kind, t)
                key_blocks = t + 1
                W = key_blocks * P
                lo = 2 * P - W
                n_heads = 4 // key_blocks
                if i + 1 < units:
                    u = i + 1
                    n = first + u
                    b = full((kind, t, "scores", u))
                    slot = slice(n % 2 * 4, n % 2 * 4 + n_heads)
                    for r in range(n_heads):
                        hh = head_of(kind, t, u)[0] + r
                        table = alibi_sb[:, (hh + 1) % 2, :] if kind == "n" else causal
                        last = nc.vector.tensor_tensor_reduce(
                            out=S[:, n % 2, r * W:(r + 1) * W], in0=bank[b][:, r * W:(r + 1) * W], in1=table[:, lo:2 * P],
                            scale=2.0 ** -((hh + 1) // 2) if kind == "n" else 1.0, scalar=LOWEST, op0=ALU.add, op1=ALU.max,
                            accum_out=row_max[:, slot.start + r:slot.start + r + 1])
                    last.then_inc(bank_drained[b], 1)
                    drained((kind, t, "scores", u))
                    nc.vector.tensor_scalar(neg_max[:, slot], row_max[:, slot], -(NSA_SCALE if kind == "n" else MLA_SCALE), None,
                                            ALU.mult).then_inc(scores_ready, 1)
                per_fill = 8 // n_heads
                if i >= 1 and (i - 1) % per_fill == per_fill - 1:
                    u = i - 1
                    n = first_out + u // per_fill + 1
                    h0, br = head_of(kind, t, u - per_fill + 1)
                    hs = slice(h0, h0 + 8)
                    mix = mixed.rearrange("p (h d) -> p h d", h=HEADS)[:, hs, :]
                    out8 = heads_out[:].rearrange("p (h d) -> p h d", h=8)
                    dve.wait_ge(heads_filled, n)
                    if kind == "n":
                        coefficients(t, 1 + br, hs)
                        dst = mix_tmp if br else mix
                        nc.vector.tensor_tensor(dst, out8, spread(coef[:, 1 + br, hs], 2, HD), ALU.mult).then_inc(heads_drained, 1)
                        dve.wait_ge(heads_drained, n)
                        if u == units - 1:
                            nc.vector.tensor_tensor(mix, mix, mix_tmp, ALU.add).then_inc(mixed_ready, 1)
                        elif br:
                            link(nc.vector.tensor_tensor(mix, mix, mix_tmp, ALU.add))
                    else:
                        link(nc.vector.reciprocal(coef[:, 0, hs], row_sum[:, 0, hs]))
                        nc.vector.tensor_tensor(mix, out8, spread(coef[:, 0, hs], 2, HD), ALU.mult).then_inc(heads_drained, 1)
                        if u == units - 1:
                            dve.wait_ge(heads_drained, n)
                            dve.sem_inc(mixed_ready, 1)

            mix_tmp = onehot[:].rearrange("p a b -> p (a b)")[:, 0:512].rearrange("p (h d) -> p h d", h=8)

            def coefficients(t, br, hs):
                link(nc.vector.tensor_tensor(denom[:, br, hs], gates[:, t, br, hs], row_sum[:, br, hs], ALU.mult))
                link(nc.vector.reciprocal(coef[:, br, hs], denom[:, br, hs]))

            def residual(t, half, src):
                y = h[:, t, half * 512:(half + 1) * 512]
                return nc.vector.scalar_tensor_tensor(out=y, in0=y, scalar=ALPHA, in1=src, op0=ALU.mult, op1=ALU.add)

            def normalize(e, t):
                y = h[:, t, :]
                for half in range(2):
                    ins = nc.vector.bn_stats(stat[:, half, :], y[:, half * 512:(half + 1) * 512])
                link(ins)
                link(nc.vector.bn_aggr(moments, stat))
                nc.vector.tensor_scalar(rstd, moments[:, 1:2], LN_EPS, None, ALU.add).then_inc(var_ready, 1)
                if LN_LOAD[e]:
                    drained(("p", 0, "lnp", LN_LOAD[e]))
                else:
                    dve.wait_ge(ln_loaded, 16)
                link(nc.vector.scalar_tensor_tensor(out=y, in0=y, scalar=moments[:, 0:1], in1=lnp[:, 0, :], op0=ALU.subtract,
                                                    op1=ALU.mult))
                dve.wait_ge(std_ready, e + 1)
                link(nc.vector.reciprocal(rstd, std))
                nc.vector.scalar_tensor_tensor(out=y, in0=y, scalar=rstd, in1=lnp[:, 1, :], op0=ALU.mult, op1=ALU.add).then_inc(ln_done, 1)

            def output(kind, t, half):
                b = full((kind, t, "w", half))
                residual(t, half, bank[b][:]).then_inc(bank_drained[b], 1)
                if half:
                    drained((kind, t, "w", 1))
                    normalize(t if kind == "n" else mla_ln(t) - 1, t)

            def cmp_softmax(t):
                for e in range(2):
                    b = full(("n", t, "cs"), e)
                    src = bank[b][:, 0:8 * NCMP].rearrange("p (a x) -> p a x", a=2)
                    dst = sc_raw.rearrange("p (a e r) n -> p e a (r n)", e=2, r=4)[:, e, :, :]
                    add = cmp_bias[:, t, :, :].rearrange("p (a e r) n -> p e a (r n)", e=2, r=4)[:, e, :, :]
                    nc.vector.tensor_tensor(dst, src, add, ALU.add).then_inc(bank_drained[b], 1)
                drained(("n", t, "cs"))
                link(nc.vector.tensor_tensor(sc_raw, sc_raw, spread(down, 2, NCMP), ALU.mult))
                link(nc.vector.reduce_max(cmp_max, sc_raw, AX.X))
                nc.vector.tensor_tensor(sc_raw, sc_raw, spread(cmp_max, 2, NCMP), ALU.subtract).then_inc(cmp_ready, 1)
                dve.wait_ge(cmp_exp, t + 1)
                nc.vector.reduce_sum(row_sum[:, 0, :], sc_exp, AX.X)
                nc.vector.tensor_tensor(pc[:, :, 0:NCMP], sc_exp, spread(cmp_mask[:, t, :], 1, HEADS), ALU.mult).then_inc(cmp_probs, 1)

            def cmp_drain(t):
                b = full(("n", t, "ct"))
                nc.vector.tensor_copy(pcT.rearrange("p g t -> p (g t)"), bank[b][:]).then_inc(bank_drained[b], 1)

            def cmp_output(t):
                coefficients(t, 0, slice(0, HEADS))
                for half in range(2):
                    b = full(("n", t, "cv"), half)
                    hs = slice(8 * half, 8 * half + 8)
                    mix = mixed.rearrange("p (h d) -> p h d", h=HEADS)[:, hs, :]
                    nc.vector.tensor_tensor(mix_tmp, bank[b][:].rearrange("p (h d) -> p h d", h=8), spread(coef[:, 0, hs], 2, HD),
                                            ALU.mult).then_inc(bank_drained[b], 1)
                    use = place["n", t, "cv"][half][1]
                    dve.wait_ge(bank_drained[b], use + 1)
                    link(nc.vector.tensor_tensor(mix, mix, mix_tmp, ALU.add))

            def rms(n, data, width):
                link(nc.vector.tensor_tensor_reduce(out=rope_tmp[:, 0:width], in0=data, in1=data, scale=1.0, scalar=0.0,
                                                    op0=ALU.mult, op1=ALU.add, accum_out=rms_r))
                nc.vector.tensor_scalar(rms_in, rms_r, 1.0 / width, RMS_EPS, ALU.mult, ALU.add).then_inc(rms_ready, 1)
                dve.wait_ge(rms_std_ready, n)
                link(nc.vector.reciprocal(rms_r, rms_std))
                link(nc.vector.tensor_scalar(data, data, rms_r, None, ALU.mult))

            def rotate(x1, x2, y1, y2, tmp, cosb, sinb):
                nc.vector.tensor_tensor(tmp[0], x1, cosb, ALU.mult)
                nc.vector.tensor_tensor(tmp[1], x2, sinb, ALU.mult)
                nc.vector.tensor_tensor(tmp[2], x2, cosb, ALU.mult)
                link(nc.vector.tensor_tensor(tmp[3], x1, sinb, ALU.mult))
                nc.vector.tensor_tensor(y1, tmp[0], tmp[1], ALU.subtract)
                return nc.vector.tensor_tensor(y2, tmp[2], tmp[3], ALU.add)

            def latent_kv(t):
                drained(("m", t, "dkv"))
                rms(2 * t + 1, ckv[:, 0:KV_LORA], KV_LORA)
                rotate(ckv[:, KV_LORA:KV_LORA + HALF], ckv[:, KV_LORA + HALF:KV_LORA + ROPE], ropeT[:, HD:HD + HALF],
                       ropeT[:, HD + HALF:QK], [kr_tmp[:, i, :] for i in range(4)], rope[:, t, 0, :], rope[:, t, 1, :]
                       ).then_inc(latent_ready, 1)

            def latent_q(t, half):
                drained(("m", t, "dq", half))
                if half:
                    rms(2 * t + 2, cq, Q_LORA)
                    dve.sem_inc(latent_ready, 1)

            def queries(t, n):
                drained(("m", t, "uq", n))
                if n == 2:
                    q3 = q_nat.rearrange("p (h e) -> p h e", h=HEADS)
                    x1, x2 = q3[:, :, HD:HD + HALF], q3[:, :, HD + HALF:QK]
                    tmp = [rope_tmp[:, i * 256:(i + 1) * 256].rearrange("p (h k) -> p h k", h=HEADS) for i in range(4)]
                    rotate(x1, x2, x1, x2, tmp, spread(rope[:, t, 0, :], 1, HEADS), spread(rope[:, t, 1, :], 1, HEADS)
                           ).then_inc(q_rotated, 1)

            def run(step):
                a, t, what, *n = step
                if what == "att":
                    attention(a, t, *n)
                elif what == "w":
                    output(a, t, *n)
                elif what == "ln":
                    normalize(peer_ln(*n) - 1, t)
                elif a == "n" and what in ("cs", "ct", "cv"):
                    {"cs": cmp_softmax, "ct": cmp_drain, "cv": cmp_output}[what](t)
                elif what in ("dkv", "dq", "uq"):
                    {"dkv": latent_kv, "dq": latent_q, "uq": queries}[what](t, *n)

            def run_prologue():
                dve.wait_ge(const_loaded, 16)
                drained(("n", 0, "gate"))
                g = gates[:].rearrange("p t b h -> p (t b h)")
                link(nc.vector.tensor_scalar(g, g, 1.0, None, ALU.add))
                for step in PROLOGUE:
                    if step == ("n", 0, "att", -1):
                        dve.wait_ge(alibi_loaded, 16)
                    elif step == ("n", 0, "cs"):
                        dve.wait_ge(cmp_bias_loaded, 16)
                        dve.wait_ge(zeroed, 1)
                    elif step == ("n", 0, "w", 0):
                        dve.wait_ge(x_loaded, 16)
                    run(step)

            def top_k(item):
                phase, head = divmod(item, PH)
                t = phase % TILES
                drained((phase // TILES, t, "score", head))
                for c in range(2):
                    s = keyscore[:, t, 2 * head + c, :]
                    link(nc.vector.max(top_val[:, c, 0:8], s))
                    nc.vector.max_index(top_pos[:, c, 0:8], top_val[:, c, 0:8], s)
                    link(nc.vector.match_replace(work[:, c, :], top_val[:, c, 0:8], s, LOWEST))
                    link(nc.vector.max(top_val[:, c, 8:16], work[:, c, :]))
                    link(nc.vector.max_index(top_pos[:, c, 8:16], top_val[:, c, 8:16], work[:, c, :]))
                link(nc.vector.tensor_copy(top_idx[:], top_pos[:]))
                link(nc.vector.tensor_scalar(top_idx[:, 0, :], top_idx[:, 0, :], float(NKEYS), None, ALU.mult))
                for dst, src in ((cand[:, 0, :], top_val), (cand_idx[:], top_idx)):
                    for i in range(5):
                        nc.vector.tensor_scalar(dst[:, RUN_AT[i]:RUN_AT[i] + RUN[i]], src[:, 1, 0:RUN[i]], src[:, 0, i:i + 1], None, ALU.add)
                    nc.vector.tensor_tensor(dst[:, RUN_AT[5]:RUN_AT[8]].rearrange("p (i j) -> p i j", j=2),
                                            spread(src[:, 1, 0:2], 1, 3), spread(src[:, 0, 5:8], 2, 2), ALU.add)
                    link(nc.vector.tensor_scalar(dst[:, RUN_AT[8]:NCAND], src[:, 0, 8:16], src[:, 1, 0:1], None, ALU.add))
                link(nc.vector.max(best[:, 0:8], cand[:, 0, :]))
                nc.vector.max_index(best_pos[:, 0:8], best[:, 0:8], cand[:, 0, :])
                link(nc.vector.match_replace(cand[:, 1, :], best[:, 0:8], cand[:, 0, :], LOWEST))
                link(nc.vector.max(best[:, 8:16], cand[:, 1, :]))
                nc.vector.tensor_scalar(gate_in[:, item % 2, :], best[:], best[:, 0:1], None, ALU.subtract).then_inc(gate_in_ready, 1)
                link(nc.vector.max_index(best_pos[:, 8:16], best[:, 8:16], cand[:, 1, :]))
                link(nc.vector.tensor_copy(best_posf[:], best_pos[:]))
                link(nc.vector.tensor_tensor(onehot[:], spread(best_posf[:], 2, NCAND), spread(number, 1, TOPK), ALU.is_equal))
                link(nc.vector.tensor_tensor(onehot[:], onehot[:], spread(cand_idx[:], 1, TOPK), ALU.mult))
                link(nc.vector.reduce_sum(best_idx[:], onehot[:], AX.X))
                nc.vector.tensor_copy(expert_id[:, item % 2, :], best_idx[:]).then_inc(ids_ready, 1)

            def gate_weights(item):
                s = item % 2
                dve.wait_ge(gate_e_ready, item + 1)
                link(nc.vector.reciprocal(inv_sum[:, s:s + 1], gate_sum[:, s:s + 1]))
                link(nc.vector.tensor_scalar(gate_w[:, s, :], gate_e[:, s, :], inv_sum[:, s:s + 1], None, ALU.mult))

            def burst(item, at, i=None):
                step0 = item * TOPK + at
                rows = BURST if i is None else SLOTS

                def count(n):
                    return n if i is None else i * SLOTS + n

                for k in range(rows + 1):
                    if k < rows:
                        s = (step0 + k) % SLOTS
                        landed = 16 * ((step0 + k) // SLOTS + 1)
                        dve.wait_ge(gathered[s], landed if i is None else i * 16 + landed)
                        u_row = ring[:, s, 0:D]
                        nc.vector.tensor_tensor_reduce(out=u_row, in0=u_row, in1=xdup[:], scale=1.0, scalar=0.0, op0=ALU.mult,
                                                       op1=ALU.add, accum_out=dots[:, s:s + 1]).then_inc(dot_ready, 1)
                    if k:
                        j = k - 1
                        s = (step0 + j) % SLOTS
                        dve.wait_ge(gelu_ready, count(step0 + j + 1))
                        dve.wait_ge(slot_free, count(step0 + j + 1 + SLOTS - DIAGS))
                        gate = gate_w[:, item % 2, at + j:at + j + 1] if i is None else gate_w[:, item % 2, bass.ds(i * SLOTS + j, 1)]
                        nc.vector.tensor_scalar(diag[:, (step0 + j) % DIAGS, :], ident, gelu[:, s:s + 1], gate, ALU.mult,
                                                ALU.mult).then_inc(diag_ready, 1)

            run_prologue()
            top_k(0)
            for phase in range(2 * TILES):
                slots = phase_slots(phase)
                dve.wait_ge(xdup_ready, phase + 1)
                for head in range(PH):
                    item = phase * PH + head
                    gate_weights(item)
                    if head and not any(slots[head * BURSTS:(head + 1) * BURSTS]):
                        if item + 1 < ITEMS:
                            top_k(item + 1)
                        with dve.Fori(0, TOPK // SLOTS, 1) as i:
                            burst(item, 0, i)
                        continue
                    for k in range(BURSTS):
                        burst(item, k * BURST)
                        for step in slots[head * BURSTS + k]:
                            run(step)
                        if k == 0 and item + 1 < ITEMS:
                            top_k(item + 1)
                dve.wait_ge(slot_free, SLOTS + (phase + 1) * PH * TOPK)
                residual(phase % TILES, 0, acc[:, 0:512])
                residual(phase % TILES, 1, acc[:, 512:D]).then_inc(acc_read, 1)
                dve.wait_ge(acc_read, phase + 1)
            normalize(peer_ln(2 * TILES - 1) - 1, TILES - 1)


def _kxn(w):
    k, n = w.shape
    return w.reshape(k // P, P, n).transpose(1, 0, 2).reshape(P, -1)


def _constants():
    p = np.arange(P)
    out = {"ident": np.eye(P, dtype=np.float32)}
    dist = P + p[:, None] - np.arange(2 * P)[None, :]
    base = np.array([1.0, 2.0 ** -0.5], np.float32)
    shift = (np.arange(HEADS) + 1) // 2
    table = -(base[None, :, None] / np.float32(NSA_SCALE)) * dist[:, None, :].astype(np.float32)
    out["alibi"] = np.where(dist[:, None, :] >= 0, table, np.float32(MASKED)).astype(np.float32)
    out["down"] = np.broadcast_to(2.0 ** -shift, (P, HEADS)).astype(np.float32)
    head = (2 * np.arange(2)[None, :, None] + (p // HD)[:, None, None]) * 4 + np.arange(4)
    out["q_up"] = (2.0 ** shift[head]).astype(np.float32)
    out["causal"] = np.where(dist >= 0, 0.0, MASKED).astype(np.float32)
    t = np.arange(TILES)[None, :] * P + p[:, None]
    end = np.arange(NCMP) * CMP_STRIDE + CMP_LEN - 1
    dist_c = t[:, :, None] - end
    seen = (dist_c >= 0) & (np.arange(NCMP) < NCMP - 1)
    heads_base = base[(np.arange(HEADS) + 1) % 2]
    table = -(heads_base[None, None, :, None] / np.float32(NSA_SCALE)) * dist_c[:, :, None, :].astype(np.float32)
    out["cmp_table"] = np.where(seen[:, :, None, :], table, np.float32(MASKED)).astype(np.float32)
    out["cmp_mask"] = seen.astype(np.float32)
    inv = (1.0 / (np.float32(10000.0) ** (np.arange(0, ROPE, 2, dtype=np.float32) / np.float32(ROPE)))).astype(np.float32)
    ang = t.astype(np.float32)[:, :, None] * inv
    out["rope"] = np.stack([np.cos(ang), np.sin(ang)], 2).astype(np.float32)
    out["number"] = np.broadcast_to(np.arange(NCAND, dtype=np.float32), (P, NCAND))
    return {k: np.ascontiguousarray(v.reshape(P, -1)) for k, v in out.items()}


def _layout(a):
    w = a["nsa_w_in"][0]
    q = w[:, 0:1024].reshape(D, 2, 2, 4, HD)
    q = q.transpose(0, 1, 3, 2, 4).reshape(D, 1024)
    kc, vc, ks, vs, kw, vw = [w[:, 1024 + 256 * i:1280 + 256 * i] for i in range(6)]
    gate = w[:, 2560:2608].reshape(D, HEADS, 3).transpose(0, 2, 1).reshape(D, 48)
    cat = np.concatenate
    wo = a["nsa_w_out"][0]
    ch = {
        (0, "kvc0"): _kxn(kc), (0, "kvc1"): _kxn(vc), (0, "ksw"): _kxn(cat([ks, kw], 1)),
        (0, "ck1"): _kxn(a["nsa_cmp_k_w1"][0]), (0, "cv1"): _kxn(a["nsa_cmp_v_w1"][0]),
        (0, "q0"): _kxn(q[:, 0:512]), (0, "q1"): _kxn(q[:, 512:1024]), (0, "vsw"): _kxn(cat([vs, vw], 1)),
        (0, "gate"): _kxn(gate),
        (1, "dkv"): _kxn(cat([a["mla_w_dkv"], a["mla_w_kr"]], 1)),
        (1, "uk"): _kxn(a["mla_w_uk"].reshape(KV_LORA, 1024)), (1, "uv"): _kxn(a["mla_w_uv"].reshape(KV_LORA, 1024)),
    }
    dq, uq, mo = a["mla_w_dq"][0], a["mla_w_uq"][0].reshape(Q_LORA, HEADS * QK), a["mla_w_out"][0]
    for i in range(2):
        ch[1, f"dq{i}"] = _kxn(dq[:, i * 384:(i + 1) * 384])
        for k in range(2):
            ch[0, f"wo{i}{k}"] = _kxn(wo[k * 512:(k + 1) * 512, i * 512:(i + 1) * 512])
            ch[1, f"mo{i}{k}"] = _kxn(mo[k * 512:(k + 1) * 512, i * 512:(i + 1) * 512])
    for i in range(3):
        ch[1, f"uq{i}"] = _kxn(uq[:, i * 512:(i + 1) * 512])
    for l in range(2):
        for c in range(PH):
            wq = _kxn(a["peer_w_q"][l][:, c * 256:(c + 1) * 256])
            keys = a["peer_subkeys"][l][c].transpose(2, 0, 1).reshape(P, 2 * NKEYS)
            ch[l, f"pq{c}"] = cat([wq, keys], 1)
    weights = cat([ch[l, n].reshape(-1) for l in range(2) for n, _ in LAYERS[l]])
    c = _constants()
    c["pe"] = cat([a[f"nsa_cmp_{n}_pe"][0].reshape(16, P).T for n in "kv"], 1)
    c["w2k"], c["w2v"] = a["nsa_cmp_k_w2"][0], a["nsa_cmp_v_w2"][0]
    c["q_gain"] = a["mla_q_norm_g"][0].reshape(6, P).T
    c["kv_gain"] = a["mla_kv_norm_g"].reshape(2, P).T
    ln = np.stack([cat([a["nsa_ln_g"][0], a["nsa_ln_b"][0]]), cat([a["mla_ln_g"][0], a["mla_ln_b"][0]]),
                   cat([a["peer_ln_g"][0], a["peer_ln_b"][0]]), cat([a["peer_ln_g"][1], a["peer_ln_b"][1]])])
    c["ln_rows"] = cat([ln.reshape(-1, P), np.zeros((P - 4 * 2 * KD, P), np.float32)])
    xs = a["x"][0]
    return {
        "x": xs, "xT": xs.T.reshape(KD, P, SEQ).transpose(1, 0, 2), "weights": weights,
        "consts": cat([c[n] for n in CONST], 1), "alibi": c["alibi"], "cmp_table": c["cmp_table"], "ln_params": ln,
        "experts0": cat([a["peer_u"][0], a["peer_v"][0]], 1), "experts1": cat([a["peer_u"][1], a["peer_v"][1]], 1),
    }


def kernel(**inputs):
    import concourse.bacc as bacc
    from concourse.bass_utils import run_bass_kernel_spmd

    arrays = {k: np.ascontiguousarray(v) for k, v in _layout({k: np.asarray(v) for k, v in inputs.items()}).items()}
    nc = bacc.Bacc("TRN2", target_bir_lowering=False, num_devices=1)
    args = [nc.dram_tensor(k, v.shape, mybir.dt.from_np(v.dtype), kind="ExternalInput").ap() for k, v in arrays.items()]
    out = nc.dram_tensor("out", (SEQ, D), F32, kind="ExternalOutput").ap()
    trunk_kernel(nc, *args, out)
    r = run_bass_kernel_spmd(nc, [arrays], core_ids=[0])
    return np.asarray(r.results[0]["out"]).reshape(1, SEQ, D)
```
